# Optimizing a Trainium2 kernel written in Bass

```python
import jax, jax.numpy as jnp
from jax import lax
import numpy as np

D_MODEL = 1024
BATCH = 1
SEQ = 1024
DEPTH = 2

GRID_W = 64
CTX_LEN = 256
W_CONV = D_MODEL
W_LRU = D_MODEL
W_EVEN = W_CONV + W_LRU
N_LRU_HEADS = 8
LRU_HEAD_DIM = W_LRU // N_LRU_HEADS
CONV_WIDTH = 31
CONV_PAD = (15, 15)
SHORT_CONV_WIDTH = 4
SHORT_CONV_PAD = (2, 1)
LRU_C = 8.0
W_POOL = 2 * D_MODEL
POOL_WINDOWS = (2, 4, 8, 16)
N_POOL_GROUPS = len(POOL_WINDOWS)
POOL_GROUP_DIM = W_POOL // N_POOL_GROUPS
N_EVEN = (DEPTH + 1) // 2
N_ODD = DEPTH // 2
RMS_EPS = 1e-6
LN_EPS = 1e-5


def rmsnorm(x, g):
    xf = x.astype(jnp.float32)
    y = xf * lax.rsqrt(jnp.mean(xf * xf, axis=-1, keepdims=True) + RMS_EPS)
    return (y * g.astype(jnp.float32)).astype(x.dtype)

def layernorm(x, g, b):
    xf = x.astype(jnp.float32)
    mu = jnp.mean(xf, axis=-1, keepdims=True)
    var = jnp.mean(jnp.square(xf - mu), axis=-1, keepdims=True)
    y = (xf - mu) * lax.rsqrt(var + LN_EPS) * g.astype(jnp.float32) + b.astype(jnp.float32)
    return y.astype(x.dtype)

def modulate(h, shift, scale):
    return h * (1 + scale) + shift

def depthwise_conv(u, w, b, pad):
    y = lax.conv_general_dilated(
        u, w[:, None, :].astype(u.dtype), window_strides=(1,), padding=(pad,),
        dimension_numbers=("NWC", "WIO", "NWC"), feature_group_count=u.shape[-1])
    return y + b.astype(u.dtype)

def conformer_conv(va, vg, p):
    u = va * jax.nn.sigmoid(vg)
    u = depthwise_conv(u, p["conv_w"], p["conv_b"], CONV_PAD)
    return jax.nn.silu(layernorm(u, p["ln_g"], p["ln_b"]))

def lru_coeffs(u2, p):
    bn, n = u2.shape[0], u2.shape[1]
    uf = u2.astype(jnp.float32)
    uh = uf.reshape(bn, n, 2, N_LRU_HEADS, LRU_HEAD_DIM)
    gr = jnp.einsum("bnkhi,khij->bnkhj", uh, p["w_r"].astype(jnp.float32)).reshape(bn, n, 2, W_LRU)
    gi = jnp.einsum("bnkhi,khij->bnkhj", uh, p["w_i"].astype(jnp.float32)).reshape(bn, n, 2, W_LRU)
    r = jax.nn.sigmoid(gr + p["b_r"].astype(jnp.float32))
    i = jax.nn.sigmoid(gi + p["b_i"].astype(jnp.float32))
    log_a = -LRU_C * r * jax.nn.softplus(-p["lam"].astype(jnp.float32))
    a = jnp.exp(log_a)
    bx = jnp.sqrt(-jnp.expm1(2.0 * log_a)) * (i * uf)
    return a, bx

def lru_scan(a, bx, h0, with_outputs):
    def step(h, ab):
        at, bt = ab
        h = at * h + bt
        return h, (h if with_outputs else None)
    hT, hs = lax.scan(step, h0, (jnp.swapaxes(a, 0, 1), jnp.swapaxes(bx, 0, 1)))
    return hT, hs

def rglru_branch(xb, p, h0, with_outputs):
    u = depthwise_conv(xb, p["sconv_w"], p["sconv_b"], SHORT_CONV_PAD)
    u2 = jnp.stack([u, u[:, ::-1]], axis=2)
    a, bx = lru_coeffs(u2, p)
    hT, hs = lru_scan(a, bx, h0, with_outputs)
    if not with_outputs:
        return None, hT
    y = hs[:, :, 0] + hs[::-1, :, 1]
    return jnp.swapaxes(y, 0, 1).astype(xb.dtype), hT

def even_mixer(h, h0, p):
    z = h @ p["w_in"]
    va, vg, ga, xb, gb = jnp.split(
        z, [W_CONV, 2 * W_CONV, 3 * W_CONV, 3 * W_CONV + W_LRU], axis=-1)
    y_a = conformer_conv(va, vg, p) * jax.nn.silu(ga)
    y_b, hT = rglru_branch(xb, p, h0, True)
    y_b = y_b * jax.nn.silu(gb)
    return jnp.concatenate([y_a, y_b], axis=-1) @ p["w_out"], hT

def multiscale_pool(u):
    n = u.shape[1]
    uf = u.astype(jnp.float32)
    s = jnp.pad(jnp.cumsum(uf, axis=1), ((0, 0), (1, 0), (0, 0)))
    t = jnp.arange(n)
    parts = []
    for g, w in enumerate(POOL_WINDOWS):
        lo = jnp.clip(t - w // 2, 0, n)
        hi = jnp.clip(t + w // 2, 0, n)
        sg = s[:, :, g * POOL_GROUP_DIM:(g + 1) * POOL_GROUP_DIM]
        cnt = (hi - lo).astype(jnp.float32)[None, :, None]
        parts.append((sg[:, hi] - sg[:, lo]) / cnt)
    return (jnp.concatenate(parts, axis=-1) - uf).astype(u.dtype)

def odd_mixer(h, p, on_grid):
    bn, n = h.shape[0], h.shape[1]
    z = h @ p["w_in"]
    u, g = jnp.split(z, [W_POOL], axis=-1)
    if on_grid:
        rows = n // GRID_W
        d = multiscale_pool(u.reshape(bn * rows, GRID_W, W_POOL)).reshape(bn, n, W_POOL)
    else:
        d = multiscale_pool(u)
    d = d.reshape(bn, n, N_POOL_GROUPS, POOL_GROUP_DIM)
    y = jnp.einsum("bngi,gij->bngj", d, p["w_grp"]).reshape(bn, n, W_POOL) * p["scale"]
    return (y * jax.nn.silu(g)) @ p["w_out"]

def first_inputs(seed: int = 0) -> dict:
    key = jax.random.key(seed)
    ks = jax.random.split(key, 32)
    f32 = jnp.float32

    def nrm(k, shape, s):
        return s * jax.random.normal(k, shape, f32)

    ua = jax.random.uniform(ks[20], (N_EVEN, 2, W_LRU), f32, 0.9, 0.999)
    pa = ua ** (1.0 / LRU_C)
    lam = jnp.log(pa) - jnp.log1p(-pa)
    return {
        "x": nrm(ks[0], (BATCH, SEQ, D_MODEL), 1.0),
        "c": nrm(ks[1], (BATCH, D_MODEL), 1.0),
        "ctx": nrm(ks[2], (BATCH, CTX_LEN, D_MODEL), 1.0),
        "c_ctx": nrm(ks[3], (D_MODEL,), 1.0),
        "norm_g": 1.0 + nrm(ks[4], (DEPTH, D_MODEL), 0.1),
        "mod_w": nrm(ks[5], (DEPTH, D_MODEL, 3 * D_MODEL), 0.5 * D_MODEL ** -0.5),
        "mod_b": nrm(ks[6], (DEPTH, 3 * D_MODEL), 0.02),
        "ev_w_in": nrm(ks[7], (N_EVEN, D_MODEL, 3 * W_CONV + 2 * W_LRU), D_MODEL ** -0.5),
        "ev_conv_w": nrm(ks[8], (N_EVEN, CONV_WIDTH, W_CONV), CONV_WIDTH ** -0.5),
        "ev_conv_b": nrm(ks[9], (N_EVEN, W_CONV), 0.02),
        "ev_ln_g": 1.0 + nrm(ks[10], (N_EVEN, W_CONV), 0.1),
        "ev_ln_b": nrm(ks[11], (N_EVEN, W_CONV), 0.02),
        "ev_sconv_w": nrm(ks[12], (N_EVEN, SHORT_CONV_WIDTH, W_LRU), SHORT_CONV_WIDTH ** -0.5),
        "ev_sconv_b": nrm(ks[13], (N_EVEN, W_LRU), 0.02),
        "ev_w_r": nrm(ks[14], (N_EVEN, 2, N_LRU_HEADS, LRU_HEAD_DIM, LRU_HEAD_DIM), LRU_HEAD_DIM ** -0.5),
        "ev_b_r": nrm(ks[15], (N_EVEN, 2, W_LRU), 0.02),
        "ev_w_i": nrm(ks[16], (N_EVEN, 2, N_LRU_HEADS, LRU_HEAD_DIM, LRU_HEAD_DIM), LRU_HEAD_DIM ** -0.5),
        "ev_b_i": nrm(ks[17], (N_EVEN, 2, W_LRU), 0.02),
        "ev_lam": lam,
        "ev_w_out": nrm(ks[18], (N_EVEN, W_EVEN, D_MODEL), W_EVEN ** -0.5),
        "od_w_in": nrm(ks[21], (N_ODD, D_MODEL, 2 * W_POOL), D_MODEL ** -0.5),
        "od_w_grp": nrm(ks[22], (N_ODD, N_POOL_GROUPS, POOL_GROUP_DIM, POOL_GROUP_DIM), POOL_GROUP_DIM ** -0.5),
        "od_scale": 1.0 + nrm(ks[23], (N_ODD, W_POOL), 0.1),
        "od_w_out": nrm(ks[24], (N_ODD, W_POOL, D_MODEL), W_POOL ** -0.5),
        "final_g": 1.0 + nrm(ks[25], (D_MODEL,), 0.1),
    }

def first_block(x, c, ctx, c_ctx, norm_g, mod_w, mod_b,
              ev_w_in, ev_conv_w, ev_conv_b, ev_ln_g, ev_ln_b, ev_sconv_w, ev_sconv_b,
              ev_w_r, ev_b_r, ev_w_i, ev_b_i, ev_lam, ev_w_out,
              od_w_in, od_w_grp, od_scale, od_w_out, final_g):
    bn = x.shape[0]
    sc = jax.nn.silu(c)
    scc = jax.nn.silu(c_ctx)
    for l in range(DEPTH):
        ctx_out_needed = any(j % 2 == 0 for j in range(l + 1, DEPTH))
        shift, scale, gate = jnp.split(sc @ mod_w[l] + mod_b[l], 3, axis=-1)
        hx = modulate(rmsnorm(x, norm_g[l]), shift[:, None], scale[:, None])
        if ctx_out_needed or l % 2 == 0:
            shift_c, scale_c, gate_c = jnp.split(scc @ mod_w[l] + mod_b[l], 3, axis=-1)
            hc = modulate(rmsnorm(ctx, norm_g[l]), shift_c, scale_c)
        j = l // 2
        if l % 2 == 0:
            pe = {"w_in": ev_w_in[j], "conv_w": ev_conv_w[j], "conv_b": ev_conv_b[j],
                  "ln_g": ev_ln_g[j], "ln_b": ev_ln_b[j], "sconv_w": ev_sconv_w[j],
                  "sconv_b": ev_sconv_b[j], "w_r": ev_w_r[j], "b_r": ev_b_r[j],
                  "w_i": ev_w_i[j], "b_i": ev_b_i[j], "lam": ev_lam[j], "w_out": ev_w_out[j]}
            h0 = jnp.zeros((bn, 2, W_LRU), jnp.float32)
            if ctx_out_needed:
                out_c, h_ctx = even_mixer(hc, h0, pe)
            else:
                xb_c = hc @ pe["w_in"][:, 3 * W_CONV:3 * W_CONV + W_LRU]
                _, h_ctx = rglru_branch(xb_c, pe, h0, False)
            out_x, _ = even_mixer(hx, h_ctx, pe)
        else:
            po = {"w_in": od_w_in[j], "w_grp": od_w_grp[j], "scale": od_scale[j], "w_out": od_w_out[j]}
            if ctx_out_needed:
                out_c = odd_mixer(hc, po, False)
            out_x = odd_mixer(hx, po, True)
        x = x + gate[:, None] * out_x
        if ctx_out_needed:
            ctx = ctx + gate_c * out_c
    return rmsnorm(x, final_g)


PLE_DIM = 256
N_MIXERS = 2
EPS = 1e-6

GLA_HEADS = 4
GLA_KEY_DIM = D_MODEL // 2
GLA_VAL_DIM = D_MODEL
GLA_DK = GLA_KEY_DIM // GLA_HEADS
GLA_DV = GLA_VAL_DIM // GLA_HEADS
GLA_GATE_RANK = 16
GLA_GATE_NORMALIZER = 16.0
GLA_CHUNK = 64
GLA_IN = 2 * GLA_KEY_DIM + 2 * GLA_VAL_DIM + GLA_GATE_RANK

FOX_HEADS = 16
FOX_WIDTH = D_MODEL
FOX_HD = FOX_WIDTH // FOX_HEADS
FOX_BLOCK = 128
FOX_IN = 4 * FOX_WIDTH + FOX_HEADS

N_GLA = (DEPTH + 1) // 2
N_FOX = DEPTH // 2


def rms_norm(x, g):
    xf = x.astype(jnp.float32)
    y = xf * lax.rsqrt(jnp.mean(xf * xf, axis=-1, keepdims=True) + EPS)
    return (y * g.astype(jnp.float32)).astype(x.dtype)

def to_heads(t, n_heads):
    b, s, w = t.shape
    return t.reshape(b, s, n_heads, w // n_heads).transpose(0, 2, 1, 3)

def gla_chunked(q, k, v, log_a):
    b_, h_, s_, dk = q.shape
    dv = v.shape[-1]
    n = s_ // GLA_CHUNK
    q = q.reshape(b_, h_, n, GLA_CHUNK, dk)
    k = k.reshape(b_, h_, n, GLA_CHUNK, dk)
    v = v.reshape(b_, h_, n, GLA_CHUNK, dv)
    cum = jnp.cumsum(log_a.reshape(b_, h_, n, GLA_CHUNK, dk), axis=3)
    q_in = q * jnp.exp(cum)
    k_in = k * jnp.exp(-cum)
    causal = jnp.tril(jnp.ones((GLA_CHUNK, GLA_CHUNK), dtype=bool))
    attn = jnp.where(causal, jnp.einsum('bhncd,bhnjd->bhncj', q_in, k_in), 0.0)
    o_intra = jnp.einsum('bhncj,bhnjv->bhncv', attn, v)
    cum_last = cum[:, :, :, -1:, :]
    k_dec = k * jnp.exp(cum_last - cum)
    decay_chunk = jnp.exp(cum_last[:, :, :, 0, :])

    def step(state, inp):
        k_n, v_n, d_n = inp
        new_state = state * d_n[..., None] + jnp.einsum('bhcd,bhcv->bhdv', k_n, v_n)
        return new_state, state

    xs = (jnp.moveaxis(k_dec, 2, 0), jnp.moveaxis(v, 2, 0), jnp.moveaxis(decay_chunk, 2, 0))
    init = jnp.zeros((b_, h_, dk, dv), jnp.float32)
    _, states = lax.scan(step, init, xs)
    o_inter = jnp.einsum('bhncd,nbhdv->bhncv', q_in, states)
    return (o_intra + o_inter).reshape(b_, h_, s_, dv)

def gla_mixer(h, w_in, w_a2, b_a, o_gain, w_out):
    b_, s_, _ = h.shape
    proj = h @ w_in
    q, k, v, g, a_lr = jnp.split(
        proj, [GLA_KEY_DIM, 2 * GLA_KEY_DIM, 2 * GLA_KEY_DIM + GLA_VAL_DIM, 2 * GLA_KEY_DIM + 2 * GLA_VAL_DIM], axis=-1)
    log_a = jax.nn.log_sigmoid((a_lr @ w_a2).astype(jnp.float32) + b_a.astype(jnp.float32)) / GLA_GATE_NORMALIZER
    qh = to_heads(q, GLA_HEADS).astype(jnp.float32) * (GLA_DK ** -0.5)
    kh = to_heads(k, GLA_HEADS).astype(jnp.float32)
    vh = to_heads(v, GLA_HEADS).astype(jnp.float32)
    ah = to_heads(log_a, GLA_HEADS)
    o = gla_chunked(qh, kh, vh, ah).astype(h.dtype)
    o = rms_norm(o.transpose(0, 2, 1, 3), o_gain).reshape(b_, s_, GLA_VAL_DIM)
    return (o * jax.nn.silu(g)) @ w_out

def fox_attention(q, k, v, log_f):
    b_, h_, s_, d = q.shape
    nq = s_ // FOX_BLOCK
    c = jnp.cumsum(log_f, axis=-1)
    q_blocks = jnp.moveaxis(q.reshape(b_, h_, nq, FOX_BLOCK, d), 2, 0)
    c_blocks = jnp.moveaxis(c.reshape(b_, h_, nq, FOX_BLOCK), 2, 0)
    starts = jnp.arange(nq, dtype=jnp.int32) * FOX_BLOCK
    key_pos = jnp.arange(s_, dtype=jnp.int32)
    scale = FOX_HD ** -0.5

    def block(args):
        qb, cb, start = args
        q_pos = start + jnp.arange(FOX_BLOCK, dtype=jnp.int32)
        logits = (jnp.einsum('bhqd,bhkd->bhqk', qb, k).astype(jnp.float32) * scale
                  + cb[..., :, None] - c[..., None, :])
        mask = key_pos[None, :] <= q_pos[:, None]
        probs = jax.nn.softmax(jnp.where(mask, logits, -jnp.inf), axis=-1)
        return jnp.einsum('bhqk,bhkd->bhqd', probs.astype(v.dtype), v)

    out = lax.map(block, (q_blocks, c_blocks, starts))
    return jnp.moveaxis(out, 0, 2).reshape(b_, h_, s_, d)

def fox_mixer(h, w_in, b_f, q_gain, k_gain, w_out):
    b_, s_, _ = h.shape
    proj = h @ w_in
    q, k, v, g, f_logit = jnp.split(proj, [FOX_WIDTH, 2 * FOX_WIDTH, 3 * FOX_WIDTH, 4 * FOX_WIDTH], axis=-1)
    log_f = jax.nn.log_sigmoid(f_logit.astype(jnp.float32) + b_f.astype(jnp.float32))
    qh = rms_norm(to_heads(q, FOX_HEADS), q_gain)
    kh = rms_norm(to_heads(k, FOX_HEADS), k_gain)
    vh = to_heads(v, FOX_HEADS)
    o = fox_attention(qh, kh, vh, log_f.transpose(0, 2, 1))
    o = o.transpose(0, 2, 1, 3).reshape(b_, s_, FOX_WIDTH)
    return (o * jax.nn.silu(g)) @ w_out

def second_inputs(seed: int = 0) -> dict:
    key = jax.random.key(seed)
    ks = jax.random.split(key, 20)
    f32 = jnp.float32
    nrm = lambda k, shape, fan_in: jax.random.normal(k, shape, f32) * (fan_in ** -0.5)
    gain = lambda k, shape: 1.0 + 0.02 * jax.random.normal(k, shape, f32)
    return {
        "x": jax.random.normal(ks[0], (BATCH, SEQ, D_MODEL), f32),
        "p": jax.random.normal(ks[1], (DEPTH, BATCH, SEQ, PLE_DIM), f32),
        "norm_mixer": gain(ks[2], (DEPTH, D_MODEL)),
        "gla_w_in": nrm(ks[3], (N_GLA, D_MODEL, GLA_IN), D_MODEL),
        "gla_w_a2": nrm(ks[4], (N_GLA, GLA_GATE_RANK, GLA_KEY_DIM), GLA_GATE_RANK),
        "gla_b_a": 0.1 * jax.random.normal(ks[5], (N_GLA, GLA_KEY_DIM), f32),
        "gla_o_norm": gain(ks[6], (N_GLA, GLA_DV)),
        "gla_w_out": nrm(ks[7], (N_GLA, GLA_VAL_DIM, D_MODEL), GLA_VAL_DIM),
        "fox_w_in": nrm(ks[8], (N_FOX, D_MODEL, FOX_IN), D_MODEL),
        "fox_b_f": 2.0 + 0.5 * jax.random.normal(ks[9], (N_FOX, FOX_HEADS), f32),
        "fox_q_norm": gain(ks[10], (N_FOX, FOX_HD)),
        "fox_k_norm": gain(ks[11], (N_FOX, FOX_HD)),
        "fox_w_out": nrm(ks[12], (N_FOX, FOX_WIDTH, D_MODEL), FOX_WIDTH),
        "ple_proj": nrm(ks[13], (DEPTH, PLE_DIM, D_MODEL), PLE_DIM),
        "ple_gate": nrm(ks[14], (DEPTH, D_MODEL, D_MODEL), D_MODEL),
        "ple_norm": gain(ks[15], (DEPTH, D_MODEL)),
        "final_norm": gain(ks[16], (D_MODEL,)),
    }

def second_block(x, p, norm_mixer, gla_w_in, gla_w_a2, gla_b_a, gla_o_norm, gla_w_out,
              fox_w_in, fox_b_f, fox_q_norm, fox_k_norm, fox_w_out,
              ple_proj, ple_gate, ple_norm, final_norm):
    h = x
    for i in range(DEPTH):
        hn = rms_norm(h, norm_mixer[i])
        j = i // N_MIXERS
        if i % N_MIXERS == 0:
            h = h + gla_mixer(hn, gla_w_in[j], gla_w_a2[j], gla_b_a[j], gla_o_norm[j], gla_w_out[j])
        else:
            h = h + fox_mixer(hn, fox_w_in[j], fox_b_f[j], fox_q_norm[j], fox_k_norm[j], fox_w_out[j])
        h = h + (p[i] @ ple_proj[i]) * jax.nn.sigmoid(rms_norm(h, ple_norm[i]) @ ple_gate[i])
    return rms_norm(h, final_norm)


def setup_inputs(seed=0):
    out = dict(first_inputs(seed))
    for name, value in second_inputs(seed + 1).items():
        if name != "x":
            out[name + "_2"] = value
    return out


def reference(
    x, c, ctx, c_ctx, norm_g, mod_w, mod_b, ev_w_in, ev_conv_w, ev_conv_b, ev_ln_g, ev_ln_b,
    ev_sconv_w, ev_sconv_b, ev_w_r, ev_b_r, ev_w_i, ev_b_i, ev_lam, ev_w_out, od_w_in, od_w_grp,
    od_scale, od_w_out, final_g, p_2, norm_mixer_2, gla_w_in_2, gla_w_a2_2, gla_b_a_2,
    gla_o_norm_2, gla_w_out_2, fox_w_in_2, fox_b_f_2, fox_q_norm_2, fox_k_norm_2, fox_w_out_2,
    ple_proj_2, ple_gate_2, ple_norm_2, final_norm_2,
):
    x = first_block(
        x, c, ctx, c_ctx, norm_g, mod_w, mod_b, ev_w_in, ev_conv_w, ev_conv_b, ev_ln_g, ev_ln_b,
        ev_sconv_w, ev_sconv_b, ev_w_r, ev_b_r, ev_w_i, ev_b_i, ev_lam, ev_w_out, od_w_in,
        od_w_grp, od_scale, od_w_out, final_g,
    )
    return second_block(
        x, p_2, norm_mixer_2, gla_w_in_2, gla_w_a2_2, gla_b_a_2, gla_o_norm_2, gla_w_out_2,
        fox_w_in_2, fox_b_f_2, fox_q_norm_2, fox_k_norm_2, fox_w_out_2, ple_proj_2, ple_gate_2,
        ple_norm_2, final_norm_2,
    )


_drawn_inputs = setup_inputs


def setup_inputs(seed=0):
    import zlib

    import numpy as np

    out = dict(_drawn_inputs(seed))
    spreads = {}
    factors = {'ev_conv_b': 8.0,
     'ev_ln_g': 5.155,
     'ev_ln_b': 8.0,
     'ev_b_r': 8.0,
     'ev_b_i': 8.0,
     'od_scale': 2.907,
     'norm_mixer_2': 2.912,
     'gla_o_norm_2': 5.949,
     'fox_q_norm_2': 8.0,
     'fox_k_norm_2': 8.0,
     'ple_norm_2': 8.0,
     'final_norm_2': 2.715}
    for name, (base, spread) in spreads.items():
        noise = np.random.default_rng([zlib.crc32(name.encode()), seed]).standard_normal(out[name].shape)
        drawn = base * np.exp(spread * noise) if base else spread * noise
        out[name] = __import__('jax').numpy.asarray(drawn.astype(out[name].dtype))
    for name, factor in factors.items():
        out[name] = (out[name] * factor).astype(out[name].dtype)
    return out
```

```python
import numpy as np
import concourse.bass as bass
from concourse import mybir

F32, F32R, BF16 = mybir.dt.float32, mybir.dt.float32r, mybir.dt.bfloat16
ALU, ACT, AX = mybir.AluOpType, mybir.ActivationFunctionType, mybir.AxisListType

P = 128
D = 1024
T = 1024
C = 256
KT = D // P
TC = T + C
HALF = 512
TAPS, PAD = 31, 15
ROW = 64
CH = 64
DK, DV = 128, 256
FH = 64
LRU_C = 8.0
KB = 1024

STREAMS = [
    ("w_even_in", 4, [1024, 1024, 1024, 512, 1024, 1024] * 2),
    ("w_even_out", 4, [1024] * 4),
    ("w_odd_in_a", 2, [1024] * 4 + [1024, 512] * 4),
    ("w_odd_out_a", 4, [1024] * 2),
    ("w_odd_in_b", 2, [1024] * 4 + [1024, 512] * 4),
    ("w_odd_out_b", 4, [1024] * 2),
    ("w_gla_rank", 1, [512] * 2),
    ("w_gla_in", 4, [1024] * 6),
    ("w_gla_out", 4, [1024] * 2),
    ("w_ple_0", 8, [256, 1024]),
    ("w_fox_gate", 1, [512] * 2),
    ("w_fox_in", 8, [1024] * 4),
    ("w_fox_out", 4, [1024] * 2),
    ("w_ple_1", 8, [256, 1024]),
]

VEC = {}
_at = 0
for _name, _n in [("c", 16), ("mod_b", 48), ("norm_g", 16), ("conv_w", 8 * TAPS), ("conv_b", 8),
                  ("ln_g", 8), ("ln_b", 8), ("sconv_w", 32), ("sconv_b", 8), ("b_r", 16), ("b_i", 16),
                  ("lam", 16), ("od_scale", 16), ("final_g", 8), ("norm_mixer", 16), ("b_a", 4),
                  ("o_norm", 2), ("q_norm", 1), ("k_norm", 1), ("b_f", 1), ("ple_norm", 16),
                  ("final_norm", 8), ("rcount", 4 * ROW), ("ident", P), ("ones", P), ("heads", P)]:
    VEC[_name] = (_at, _n)
    _at += _n
NVEC = _at


class Line:

    def __init__(self, eng, sem):
        self.eng, self.sem, self.base, self.k = eng, sem, 0, 0

    def __call__(self, ins):
        ins.then_inc(self.sem, 1)
        self.k += 1
        self.eng.wait_ge(self.sem, self.base + self.k)

    def go(self, ins):
        ins.then_inc(self.sem, 1)
        self.k += 1

    def sync(self, back=0):
        self.eng.wait_ge(self.sem, self.base + (self.k - back))

    def repeat(self, times, steps, body):
        start = self.base + self.k
        with self.eng.Fori(0, times) as i:
            self.base, self.k = start + i * steps, 0
            body(i)
            assert self.k == steps, (self.k, steps)
        self.base, self.k = start + times * steps, 0


def build(nc, dram, out):
    base = (nc.sbuf_base + 31) // 32 * 32
    R0, R1, MISC = base + 32 * KB - 160, base + 96 * KB - 160, base + 160 * KB - 160
    assert MISC + 48 * KB <= nc.sbuf_usable_end, (MISC, nc.sbuf_usable_end)

    def sb(name, cols, at, dt=F32):
        return nc.alloc_sbuf_tensor_at("t_" + name, [P, cols], dt, offset=at)

    sems = {}

    def S(name):
        if name not in sems:
            sems[name] = nc.alloc_semaphore(name)
        return sems[name]

    wst = [sb(f"wst{i}", 1024, base + i * 4 * KB) for i in range(2)]
    wh = [sb(f"wh{i}", 1024, base + (2 + i) * 4 * KB, F32R) for i in range(2)]
    wl = [sb(f"wl{i}", 1024, base + (4 + i) * 4 * KB, F32R) for i in range(2)]
    cst = base + 24 * KB
    vec = sb("vec", NVEC, cst)
    vend = cst + (4 * NVEC + 31) // 32 * 32
    a2s = sb("a2s", P, vend)
    cx_rs = sb("cx_rs", C, vend + 512)
    sm = vend + 512 + 1024
    modv = sb("modv", 96, sm)
    gsc = sb("gsc", 32, sm + 384)
    silc = sb("silc", 16, sm + 512)
    sp8 = sb("sp8", 16, sm + 576)
    nsp8 = sb("nsp8", 16, sm + 640)
    lt = [sb(f"lt{i}", 16, sm + 704 + 64 * i) for i in range(3)]
    dec = sb("dec", 16, sm + 896)
    mx = [sb(f"mx{i}", 1, sm + 960 + 32 * i) for i in range(2)]
    nmx = [sb(f"nmx{i}", 1, sm + 1024 + 32 * i) for i in range(2)]
    psm = [sb(f"psm{i}", 1, sm + 1088 + 32 * i) for i in range(2)]
    rps = [sb(f"rps{i}", 1, sm + 1152 + 32 * i) for i in range(2)]
    gq = sb("gq", 1, sm + 1216)
    eps6 = sb("eps6", 1, sm + 1248)
    eps5 = sb("eps5", 1, sm + 1280)
    one1 = sb("one1", 1, sm + 1312)
    tri = sb("tri", P, sm + 1344, BF16)
    idb = sb("idb", P, sm + 1600, BF16)
    assert sm + 1856 <= R0, (sm + 1856, R0)

    h_hi, h_lo = sb("h_hi", 8192, R0, F32R), sb("h_lo", 8192, R0 + 32 * KB, F32R)
    y_hi, y_lo = sb("y_hi", 8192, R1, F32R), sb("y_lo", 8192, R1 + 32 * KB, F32R)
    xr = sb("xr", 8192, MISC)
    xs_ = sb("rs", 1024, MISC + 32 * KB)
    tmp = [sb(f"tmp{i}", 1024, MISC + (36 + 4 * i) * KB) for i in range(3)]

    def V(name, j=0, n=1):
        return vec[:, bass.ds(VEC[name][0] + j, n)]

    ident, ones, heads = V("ident", 0, P), V("ones", 0, P), V("heads", 0, P)

    ps = nc.alloc_psum_tensor("ps", [P, 8, HALF], F32)

    def slot(s, cols=1024):
        return ps[:, 2 * s:2 * s + 2, :].rearrange("p a b -> p (a b)")[:, 0:cols]

    def kv_at(n):
        c = (n % 2) * 2 + n % 4 // 2
        return slot(2 + n // 4 % 2)[:, c * DV:(c + 1) * DV]

    def bank(b, lo=0, hi=HALF):
        return ps[:, b, lo:hi]

    def scratch(name, n, cols=1024):
        return nc.dram_tensor(name, [n * P, cols], F32, kind="Internal").ap()
    yb_hi_d, yb_lo_d, ga_d = scratch("yb_hi_d", 9), scratch("yb_lo_d", 9), scratch("ga_d", 8)
    x_d = scratch("x_d", 8)
    negc_d = nc.dram_tensor("negc_d", [16, 1024], F32, kind="Internal").ap()

    def tile(ap, m):
        return ap[bass.ds(m * P, P), :]

    def col(t, m, n=1024):
        return t[:, bass.ds(m * n, n)]

    first, n = {}, 0
    for name, times, widths in STREAMS:
        first[name] = n
        n += times * len(widths)
        assert len(widths) % 2 == 0
    TILES = n
    PHASES = ["start", "even_in", "even_out", "odd_a", "oout_a", "odd_b", "oout_b", "final1",
              "gla", "gout", "ple0", "fox", "fout", "ple1", "end"]

    def begin(eng, phase):
        k = PHASES.index(phase)
        if k:
            eng.wait_ge(S("phase_ended"), 3 * k)

    def end(eng):
        eng.sem_inc(S("phase_ended"), 1)

    hc_hi, hc_lo = sb("hc_hi", 2048, R1, F32R), sb("hc_lo", 2048, R1 + 8 * KB, F32R)
    L0 = R1 + 16 * KB
    u = sb("u", TC, L0)
    u_hi, u_lo = sb("u_hi", TC, L0 + 5120, F32R), sb("u_lo", TC, L0 + 2 * 5120, F32R)
    yb_hi, yb_lo = sb("yb_hi", T, L0 + 5120, F32R), sb("yb_lo", T, L0 + 2 * 5120, F32R)
    a2 = sb("a2", TC, L0 + 5120)
    gb = sb("gb", T, L0 + 5120)
    ra = [sb(f"ra{d}", TC, L0 + (3 + 2 * d) * 5120) for d in range(2)]
    ii = [sb(f"ii{d}", TC, L0 + (4 + 2 * d) * 5120) for d in range(2)]
    tt = [sb("tt0", TC, L0 + 7 * 5120), sb("tt1", TC, MISC + 32 * KB)]
    sg = sb("sg", T, L0 + 8 * 5120)
    acc1 = sb("acc1", T, L0 + 8 * 5120 + 4096)
    uc = sb("uc", 8192, MISC)
    XB0, XBC = 2, 2 + T + 1 + 2
    xbp = sb("xbp", XBC + C + 1, MISC + 32 * KB + 5120)
    upad = sb("upad", T + 2 * PAD, MISC + 32 * KB + 5120 + 5152)
    assert 4 * (XBC + C + 1) <= 5152 and 5120 + 5152 + 4 * (T + 2 * PAD) <= 16 * KB
    d_hi, d_lo = sb("d_hi", 4096, MISC, F32R), sb("d_lo", 4096, MISC + 16 * KB, F32R)
    gs = [sb(f"gs{i}", T, MISC + (32 + 4 * i) * KB) for i in range(2)]
    up = sb("up", 8 * 80, MISC + 40 * KB)
    pa, pb = sb("pa", 8 * 80, MISC + 40 * KB + 2560), sb("pb", 8 * 80, MISC + 40 * KB + 5120)
    qin, kin, kdec, cum, te = (sb(nm, T, MISC + 4 * i * KB) for i, nm in enumerate(["qin", "kin", "kdec", "cum", "te"]))
    vt = sb("vt", 2048, MISC + 20 * KB)
    kdt = sb("kdt", T, MISC + 28 * KB)
    att = sb("att", T, MISC + 32 * KB)
    st = sb("st", 2048, MISC + 36 * KB)
    cmask = sb("cmask", T, MISC + 44 * KB)
    alr = sb("alr", T, R1 + 60 * KB)
    osq = sb("osq", 2048, MISC)
    qh, ql, kh, kl = (sb(nm, T, MISC + 4 * i * KB, F32R) for i, nm in enumerate(["qh", "ql", "kh", "kl"]))
    vh, vl = sb("vh", T, MISC + 16 * KB, F32R), sb("vl", T, MISC + 20 * KB, F32R)
    negc = sb("negc", T, MISC + 24 * KB)
    lg = [sb(f"lg{i}", T, MISC + (28 + 4 * i) * KB) for i in range(2)]
    pth, ptl = sb("pth", T, MISC + 36 * KB, F32R), sb("ptl", T, MISC + 40 * KB, F32R)
    fsq, frs = sb("fsq", T, MISC + 36 * KB), sb("frs", T, MISC + 40 * KB)
    gf = sb("gf", T, MISC + 44 * KB)
    fz = [sb(f"fz{i}", T, MISC + 4 * i * KB) for i in range(4)]
    pf = sb("pf", 2048, R1 + 16 * KB)
    p_hi, p_lo = sb("p_hi", 2048, R1, F32R), sb("p_lo", 2048, R1 + 8 * KB, F32R)

    block_cm = nc.Block()
    block = block_cm.__enter__()

    modw = sb("modw", 16384, R1)
    ctxr = sb("ctxr", 2048, MISC + 32 * KB)
    squares = sb("squares", 10 * T, R0)
    sq0 = sb("sq0", T, MISC + 40 * KB)
    n_tmp = sb("n_tmp", T, MISC + 44 * KB)
    NCHUNK = 12

    @block.sync
    def _(sp):
        sp.dma_start(vec[:, :], dram["vec"]).then_inc(S("vec_loaded"), 16)
        sp.dma_start(xr[:, :].rearrange("p (k t) -> p k t", k=KT),
                     dram["xT"].rearrange("(k p) t -> p k t", p=P)).then_inc(S("x_loaded"), 16)
        sp.dma_start(ctxr[:, :].rearrange("p (k t) -> p k t", k=KT),
                     dram["ctxT"].rearrange("(k p) t -> p k t", p=P)).then_inc(S("ctx_loaded"), 16)
        for c in range(NCHUNK):
            if c >= 4:
                sp.wait_ge(S("mod_used"), c - 3)
            sp.dma_start(modw[:, (c % 4) * 4096:(c % 4 + 1) * 4096],
                         dram["w_mod"][c * P:(c + 1) * P, :]).then_inc(S(f"mod_loaded{c % 4}"), 16)
        for s, (name, times, widths) in enumerate(STREAMS):
            total = sum(widths)
            with sp.Fori(0, times) as i:
                at = 0
                for j, w in enumerate(widths):
                    n = first[name] + j + i * len(widths)
                    sp.wait_ge(S("w_split"), n + 1)
                    sp.dma_start(wst[j % 2][:, 0:w],
                                 dram[name][bass.ds(i * P, P), at:at + w]).then_inc(S(f"w_loaded{j % 2}"), 16)
                    at += w
        sp.wait_ge(S("out_stored"), 16 * KT)

    @block.gpsimd
    def _(pool):
        pool.sem_inc(S("w_split"), 2)
        pool.memset(tri[:, :], 0.0).then_inc(S("tri"), 1)
        pool.memset(idb[:, :], 0.0).then_inc(S("tri"), 1)
        pool.wait_ge(S("tri"), 2)
        pool.affine_select(out=tri[:, :], in_=tri[:, :], compare_op=ALU.is_ge, fill=-1e30, base=0,
                           pattern=[[-1, P]], channel_multiplier=1).then_inc(S("tri"), 1)
        pool.affine_select(out=idb[:, :], in_=idb[:, :], compare_op=ALU.not_equal, fill=1.0, base=0,
                           pattern=[[-1, P]], channel_multiplier=1).then_inc(S("tri"), 1)
        for name, times, widths in STREAMS:
            gla = name == "w_gla_in"
            with pool.Fori(0, times) as i:
                for j, w in enumerate(widths):
                    n = first[name] + j + i * len(widths)
                    if gla and j == 4:
                        pool.wait_ge(S("g_att"), i + 1)
                        for q in range(2):
                            pool.sem_inc(S("pool_begun"), 1)
                            a = att[64 * q:64 * q + 64, :].rearrange("p (b c) -> p b c", b=8)[:, :, 64 * q:64 * q + 64]
                            pool.affine_select(out=a, in_=a, compare_op=ALU.is_ge, fill=0.0, base=0,
                                               pattern=[[0, 8], [1, 64]], channel_multiplier=-1)\
                                .then_inc(S("g_causal"), 1)
                            pool.wait_ge(S("g_causal"), 2 * i + q + 1)
                    pool.wait_ge(S(f"w_loaded{j % 2}"), (first[name] // 2 + j // 2 + 1) * 16 + i * (len(widths) * 8))
                    pool.wait_ge(S("w_used"), n + 1)
                    pool.sem_inc(S("pool_begun"), 1)
                    pool.tensor_copy(wh[j % 2][:, 0:w], wst[j % 2][:, 0:w]).then_inc(S("w_high"), 1)
                    pool.wait_ge(S("w_high"), n + 1)
                    pool.tensor_tensor(wl[j % 2][:, 0:w], wst[j % 2][:, 0:w], wh[j % 2][:, 0:w].bitcast(F32),
                                       ALU.subtract).then_inc(S("w_split"), 1)

    @block.tensor
    def _(pe):
        def three(out_, pairs, cols):
            n = len(pairs)
            for k, (ah, al, bh, bl) in enumerate(pairs):
                pe.matmul(out_, ah, bh[:, cols] if cols else bh, start=(k == 0), stop=False)
                pe.matmul(out_, ah, bl[:, cols] if cols else bl, start=False, stop=False)
                last = pe.matmul(out_, al, bh[:, cols] if cols else bh, start=False, stop=(k == n - 1))
            return last

        def wtile(s, kts=8, off=0):
            return [(wh[s][:, off + 128 * k:off + 128 * k + 128], wl[s][:, off + 128 * k:off + 128 * k + 128])
                    for k in range(kts)]

        def project(s, dst, hi, lo, kts=8, off=0, kt0=0, ready=None, chunks=None, start=True, stop=True):
            for k in range(kts):
                w1, w2 = wtile(s, kts, off)[k]
                if ready:
                    ready(k)
                for c0, cn, o in chunks or [(0, HALF, dst[:, 0:HALF]), (HALF, HALF, dst[:, HALF:2 * HALF])]:
                    src = o[1:] if isinstance(o, tuple) else (hi, lo)
                    o = o[0] if isinstance(o, tuple) else o
                    stride = T if len(o.shape) and src[0] is not hc_hi else C
                    x1 = src[0][:, (kt0 + k) * stride + c0:(kt0 + k) * stride + c0 + cn]
                    x2 = src[1][:, (kt0 + k) * stride + c0:(kt0 + k) * stride + c0 + cn]
                    pe.matmul(o, w1, x1, start=start and k == 0, stop=False)
                    pe.matmul(o, w1, x2, start=False, stop=False)
                    last = pe.matmul(o, w2, x1, start=False, stop=stop and k == kts - 1)
            return last

        def take(name, i, j):
            per = len(next(w for nm, _, w in STREAMS if nm == name))
            pe.wait_ge(S("w_split"), first[name] + j + 3 + i * per)

        pe.wait_ge(S("vec_loaded"), 16)

        def stats(r, sums=xs_):
            pe.wait_ge(S("sq_ready"), r + 1)
            for b in range(2):
                last = pe.matmul(bank(6 + b), ones, sums[:, b * HALF:(b + 1) * HALF], start=True, stop=True)
            last.then_inc(S("stats"), 1)

        def hready(r):
            return lambda k: pe.wait_ge(S("h_ready"), 8 * r + k + 1)

        pe.sem_inc(S("w_used"), 2)
        stats(0, sq0)
        pe.wait_ge(S("cx_sq"), 1)
        pe.matmul(bank(5, 0, C), ones, cx_rs[:, :], start=True, stop=True).then_inc(S("cx_stats"), 1)
        pe.wait_ge(S("silc"), 1)
        for c in range(NCHUNK):
            pe.wait_ge(S(f"mod_loaded{c % 4}"), 16 * (c // 4 + 1))
            for q in range(4):
                m = 4 * c + q
                layer, m = divmod(m, 24)
                for k in range(KT):
                    at = (c % 4) * 4096 + q * 1024 + k * P
                    last = pe.matmul(bank(layer, 2 * m, 2 * m + 2), modw[:, at:at + P],
                                     silc[:, 2 * k:2 * k + 2], start=(k == 0), stop=(k == KT - 1))
            last.then_inc(S("mod_used"), 1)
        pe.wait_ge(S("mod_used"), NCHUNK)
        end(pe)

        def even_head(i, q):
            h = 2 * i + q
            j = 6 * q
            nm = "w_even_in"
            evac = lambda n: pe.wait_ge(S("e_evac"), 8 * h + n)
            used = lambda ins: ins.then_inc(S("w_used"), 1)
            full = lambda dst, c: [(0, HALF, dst[:, 0:HALF]), (HALF, HALF, dst[:, HALF:2 * HALF])] + \
                ([(0, C, (c, hc_hi, hc_lo))] if c is not None else [])
            evac(6)
            take(nm, i, j)
            used(project(j % 2, slot(0), h_hi, h_lo, chunks=full(slot(0), bank(6, 0, C)),
                         ready=lambda k: pe.wait_ge(S("h_ready"), k + 1)))
            evac(7)
            take(nm, i, j + 1)
            used(project((j + 1) % 2, slot(1), h_hi, h_lo))
            evac(8)
            take(nm, i, j + 2)
            used(project(j % 2, slot(2), h_hi, h_lo))
            take(nm, i, j + 3)
            pe.wait_ge(S("e_ul"), h + 1)
            for g, (sl, b, wait) in enumerate([(0, 7, lambda: evac(9)), (1, 6, lambda: pe.wait_ge(S("e_va"), h + 1)),
                                               (2, 7, lambda: evac(11)), (0, 6, lambda: evac(12))]):
                wait()
                w1 = wh[(j + 3) % 2][:, g * P:(g + 1) * P]
                w2 = wl[(j + 3) % 2][:, g * P:(g + 1) * P]
                for o, c0, cn in ((slot(sl)[:, 0:HALF], 0, HALF), (slot(sl)[:, HALF:T], HALF, HALF), (bank(b, 0, C), T, C)):
                    pe.matmul(o, w1, u_hi[:, c0:c0 + cn], start=True, stop=False)
                    pe.matmul(o, w1, u_lo[:, c0:c0 + cn], start=False, stop=False)
                    last = pe.matmul(o, w2, u_hi[:, c0:c0 + cn], start=False, stop=True)
                if g < 3:
                    last.then_inc(S("e_gate"), 1)
            used(last)
            take(nm, i, j + 4)
            evac(12)
            used(project(j % 2, slot(1), h_hi, h_lo))
            take(nm, i, j + 5)
            evac(13)
            used(project((j + 1) % 2, slot(2), h_hi, h_lo))

        begin(pe, "even_in")
        with pe.Fori(0, 4) as i:
            even_head(i, 0)
            even_head(i, 1)
        pe.wait_ge(S("w_used"), first["w_even_out"] + 2)
        end(pe)

        begin(pe, "even_out")
        for k in range(KT):
            for b in range(2):
                last = pe.matmul(bank(6 + b), ones, uc[:, k * T + b * HALF:k * T + (b + 1) * HALF],
                                 start=(k == 0), stop=(k == KT - 1))
        last.then_inc(S("ln_sum"), 1)

        def out_pair(nm, i, parts, ring, tiles):
            for q in range(2):
                pe.wait_ge(S(ring), 8 * out_pair.call[nm] + 2 * i + q + 1)
            j = 0
            for p_, (hi, lo, ready) in enumerate(parts):
                for q in range(2):
                    take(nm, i, j)
                    project(j % 2, slot(q), hi, lo, ready=ready if q == 0 else None, start=(p_ == 0),
                            stop=(p_ == len(parts) - 1)).then_inc(S("w_used"), 1)
                    j += 1

        out_pair.call = {"w_even_out": 0, "w_odd_out_a": 1, "w_odd_out_b": 2, "w_gla_out": 3, "w_fox_out": 4}
        for k in range(KT):
            pe.wait_ge(S("ln_sq"), k + 1)
            for b in range(2):
                last = pe.matmul(bank(6 + b), ones, tmp[k % 2][:, b * HALF:(b + 1) * HALF],
                                 start=(k == 0), stop=(k == KT - 1))
            last.then_inc(S("ln_var"), 1)
        with pe.Fori(0, 4) as i:
            out_pair("w_even_out", i, [(h_hi, h_lo, lambda k: pe.wait_ge(S("yb_loaded"), 32)),
                                       (y_hi, y_lo, lambda k: pe.wait_ge(S("ya_ready"), k + 1))], "x_added", 4)
        pe.wait_ge(S("w_used"), first["w_odd_in_a"] + 2)
        stats(1)
        end(pe)

        def odd_groups(part):
            nm = "w_odd_in_" + "ab"[part]

            def group(i):
                g = 2 * part + i
                act = lambda n: pe.wait_ge(S("o_act"), 8 * g + n)
                yev = lambda n: pe.wait_ge(S("o_y"), 4 * g + n)
                for j in range(4):
                    (act, yev)[j % 2](7 + j // 2 if j % 2 == 0 else 3 + j // 2)
                    take(nm, i, j)
                    project(j % 2, slot(j), h_hi, h_lo, ready=hready(1) if j == 0 and part == 0 else None)\
                        .then_inc(S("w_used"), 1)
                for j in range(4):
                    a, b = 2 * j % 4, (2 * j + 1) % 4
                    act((9, 11, 13, 14)[j])
                    take(nm, i, 4 + 2 * j)
                    project(0, slot(a), h_hi, h_lo).then_inc(S("w_used"), 1)
                    act(10) if j == 0 else act(12) if j == 1 else yev(3 + j)
                    take(nm, i, 5 + 2 * j)
                    if j == 0:
                        pe.wait_ge(S("o_d"), 4 * g + 4)
                    project(1, slot(b), d_hi, d_lo, kts=4).then_inc(S("w_used"), 1)
            with pe.Fori(0, 2) as i:
                group(i)
            pe.wait_ge(S("w_used"), first["w_odd_out_" + "ab"[part]] + 2)
            end(pe)

        def out_phase(nm, ready, stat, after):
            with pe.Fori(0, 4) as i:
                out_pair(nm, i, [(y_hi, y_lo, ready)], "x_added", 2)
            pe.wait_ge(S("w_used"), first[after] + 2)
            if stat is not None:
                stats(stat)
            end(pe)

        begin(pe, "odd_a")
        odd_groups(0)
        begin(pe, "oout_a")
        out_phase("w_odd_out_a", None, None, "w_odd_in_b")
        begin(pe, "odd_b")
        odd_groups(1)
        begin(pe, "oout_b")
        out_phase("w_odd_out_b", None, 2, "w_gla_rank")
        begin(pe, "final1")
        stats(3)
        end(pe)

        begin(pe, "gla")
        for j in range(2):
            take("w_gla_rank", 0, j)
            project(j, slot(0), h_hi, h_lo, kts=4, kt0=4 * j, ready=lambda k, j=j: hready(2)(4 * j + k),
                    start=(j == 0), stop=(j == 1)).then_inc(S("w_used"), 1)

        def transposed(s, dst):
            for blk in range(8):
                for k in range(KT):
                    w1, w2 = wtile(s)[k]
                    x1 = h_hi[:, k * T + blk * P:k * T + (blk + 1) * P]
                    x2 = h_lo[:, k * T + blk * P:k * T + (blk + 1) * P]
                    o = dst[:, blk * P:(blk + 1) * P]
                    pe.matmul(o, x1, w1, start=(k == 0), stop=False)
                    pe.matmul(o, x1, w2, start=False, stop=False)
                    last = pe.matmul(o, x2, w1, start=False, stop=(k == KT - 1))
            return last

        def gla_head(i):
            nm = "w_gla_in"
            pe.wait_ge(S("g_alr"), 1)
            pe.wait_ge(S("g_go"), i + 1)
            pe.wait_ge(S("a2_loaded"), 16 * i + 16)
            for b in range(2):
                last = pe.matmul(bank(6 + b), a2s[0:16, :],
                                 alr[0:16, b * HALF:(b + 1) * HALF], start=True, stop=True)
            last.then_inc(S("g_lg"), 1)
            for j in range(2):
                take(nm, i, j)
                project(j, slot(j), h_hi, h_lo).then_inc(S("w_used"), 1)
            take(nm, i, 2)
            transposed(0, slot(2)).then_inc(S("w_used"), 1)
            take(nm, i, 3)
            pe.wait_ge(S("g_ab"), i + 1)
            transposed(1, slot(3)).then_inc(S("w_used"), 1)
            pe.wait_ge(S("g_kdec"), i + 1)
            for b in range(8):
                last = pe.matmul(slot(0)[:, b * P:(b + 1) * P], kin[:, b * P:(b + 1) * P],
                                 qin[:, b * P:(b + 1) * P], start=True, stop=True)
            last.then_inc(S("g_pe"), 1)
            for b in range(8):
                last = pe.transpose(slot(1)[:, b * P:(b + 1) * P], kdec[:, b * P:(b + 1) * P], ident)
            last.then_inc(S("g_pe"), 1)
            pe.wait_ge(S("g_kdt"), i + 1)
            for r in range(4):
                if r >= 2:
                    pe.wait_ge(S("g_st"), 16 * i + 4 * (r - 1) + 1)
                for c in range(4):
                    n = 4 * r + c
                    lo = 64 * (n % 2)
                    last = pe.matmul(kv_at(n), kdt[lo:lo + 64, (n // 2) * P:(n // 2 + 1) * P],
                                     vt[lo:lo + 64, (n // 2) * DV:(n // 2 + 1) * DV], start=True, stop=True)
                last.then_inc(S("g_kv"), 1)
                if r == 0:
                    pe.wait_ge(S("g_causal"), 2 * i + 2)
                    pe.wait_ge(S("g_kdt"), i + 1)
                if r in (1, 3):
                    for b in range(4 * (r // 2), 4 * (r // 2) + 4):
                        pe.wait_ge(S("g_st"), 16 * i + 2 * b + 2)
                        for v in range(2):
                            o = slot(v)[:, b * P:(b + 1) * P]
                            pe.matmul(o, vt[:, b * DV + v * P:b * DV + (v + 1) * P], att[:, b * P:(b + 1) * P],
                                      start=True, stop=False)
                            for c in range(2):
                                n = 2 * b + c
                                if n == 0:
                                    continue
                                last = pe.matmul(slot(v)[:, b * P + c * 64:b * P + c * 64 + 64],
                                                 st[:, (n % 8) * DV + v * P:(n % 8) * DV + (v + 1) * P],
                                                 qin[:, b * P + c * 64:b * P + c * 64 + 64], start=False, stop=(c == 1))
                        last.then_inc(S("g_o"), 1)
            pe.wait_ge(S("g_st"), 16 * i + 16)
            take(nm, i, 4)
            project(0, slot(2), h_hi, h_lo).then_inc(S("w_used"), 1)
            pe.wait_ge(S("g_sq"), i + 1)
            for b in range(2):
                for v in range(2):
                    last = pe.matmul(bank(6 + b), ones, osq[:, v * T + b * HALF:v * T + (b + 1) * HALF],
                                     start=(v == 0), stop=(v == 1))
            last.then_inc(S("g_ss"), 1)
            take(nm, i, 5)
            pe.wait_ge(S("g_g0"), i + 1)
            project(1, slot(2), h_hi, h_lo).then_inc(S("w_used"), 1)

        with pe.Fori(0, 4) as i:
            gla_head(i)
        pe.wait_ge(S("w_used"), first["w_gla_out"] + 2)
        end(pe)
        begin(pe, "gout")
        out_phase("w_gla_out", None, 4, "w_ple_0")

        def ple(r):
            nm = f"w_ple_{r}"

            def two(i):
                for q in range(2):
                    m = 2 * i + q
                    pe.wait_ge(S("p_added"), 8 * r + m + 1)
                    pe.wait_ge(S("p_split"), r + 1)
                    with_round(nm, m, 0)
                    project(0, slot(2 * q), p_hi, p_lo, kts=2).then_inc(S("w_used"), 1)
                    with_round(nm, m, 1)
                    project(1, slot(2 * q + 1), h_hi, h_lo, ready=hready(3 + 2 * r)).then_inc(S("w_used"), 1)

            def with_round(nm, m, j):
                pe.wait_ge(S("w_split"), first[nm] + j + 3 + m * 2)
            with pe.Fori(0, 4) as i:
                two(i)
            pe.wait_ge(S("w_used"), (first["w_fox_gate"] if r == 0 else TILES) + 2)
            stats(5 + 2 * r)
            end(pe)

        begin(pe, "ple0")
        ple(0)

        begin(pe, "fox")
        pe.wait_ge(S("tri"), 4)
        for j in range(2):
            take("w_fox_gate", 0, j)
            project(j, slot(0), h_hi, h_lo, kts=4, kt0=4 * j, ready=lambda k, j=j: hready(4)(4 * j + k),
                    start=(j == 0), stop=(j == 1)).then_inc(S("w_used"), 1)
        pe.wait_ge(S("f_negc"), 1)

        def fox_pair(i):
            nm = "w_fox_in"
            pe.wait_ge(S("f_go"), i + 1)
            for j in range(2):
                take(nm, i, j)
                project(j, slot(j), h_hi, h_lo).then_inc(S("w_used"), 1)
            for j in range(2):
                pe.wait_ge(S("f_sq"), 2 * i + j + 1)
                for b in range(2):
                    last = pe.matmul(slot(2 + j)[:, b * HALF:(b + 1) * HALF], heads, fsq[:, b * HALF:(b + 1) * HALF],
                                     start=True, stop=True)
                last.then_inc(S("f_ss"), 1)
            take(nm, i, 2)
            transposed(0, slot(0)).then_inc(S("w_used"), 1)
            take(nm, i, 3)
            project(1, slot(1), h_hi, h_lo).then_inc(S("w_used"), 1)
            pe.wait_ge(S("f_ready"), i + 1)

            def scores(s):
                hh, t = divmod(s, 8)
                rows = slice(64 * hh, 64 * hh + 64)
                n = (t + 1) * P
                if s >= 2:
                    pe.wait_ge(S("f_max"), 16 * i + s - 1)
                for c0 in range(0, n, HALF):
                    cn = min(HALF, n - c0)
                    o = slot(2 + s % 2)[:, c0:c0 + cn]
                    diag = c0 + cn == n
                    a = slice(t * P, (t + 1) * P)
                    b = slice(c0, c0 + cn)
                    pe.matmul(o, qh[rows, a], kh[rows, b], start=True, stop=False)
                    pe.matmul(o, qh[rows, a], kl[rows, b], start=False, stop=False)
                    last = pe.matmul(o, ql[rows, a], kh[rows, b], start=False, stop=not diag)
                    if diag:
                        last = pe.matmul(slot(2 + s % 2)[:, n - P:n], idb[:, :], tri[:, :], start=False, stop=True)
                last.then_inc(S("f_qk"), 1)

            def turn(s):
                t = s % 8
                pe.wait_ge(S("f_prob"), 16 * i + s + 1)
                if s >= 1:
                    pe.wait_ge(S("f_pt"), 16 * i + s)
                for b in range(t + 1):
                    last = pe.transpose(slot(0)[:, b * P:(b + 1) * P], lg[s % 2][:, b * P:(b + 1) * P], ident)
                last.then_inc(S("f_t"), 1)

            def values(s):
                hh, t = divmod(s, 8)
                if s == 8:
                    pe.wait_ge(S("f_y"), 2 * i + 1)
                pe.wait_ge(S("f_pt"), 16 * i + s + 1)
                o = slot(1)[:, t * P:(t + 1) * P]
                for b in range(t + 1):
                    c = slice(b * P, (b + 1) * P)
                    pe.matmul(o, vh[:, c], pth[:, c], start=(b == 0), stop=False)
                    pe.matmul(o, vl[:, c], pth[:, c], start=False, stop=False)
                    last = pe.matmul(o, vh[:, c], ptl[:, c], start=False, stop=(b == t))
                last.then_inc(S("f_pv"), 1)

            scores(0)
            for s in range(16):
                if s < 15:
                    scores(s + 1)
                turn(s)
                values(s)

        with pe.Fori(0, 8) as i:
            fox_pair(i)
        pe.wait_ge(S("f_pv"), 128)
        end(pe)
        begin(pe, "fout")
        out_phase("w_fox_out", None, 6, "w_ple_1")
        begin(pe, "ple1")
        ple(1)
        begin(pe, "end")

    @block.scalar
    def _(act):
        line = Line(act, S("act_line"))
        A = act.activation

        def rsqrt(dst, src, n, eps):
            line(A(dst, src, ACT.Ln, bias=eps[:, 0:1], scale=1.0 / n))
            return A(dst, dst, ACT.Exp, scale=-0.5)

        def high(r):
            act.wait_ge(S("stats"), r["stat"] + 1)
            rsqrt(xs_[:, :], slot(3), D, eps6).then_inc(S("rs"), 1)
            if r.get("op") is None:
                return
            for k in range(KT):
                t = tmp[k % r["bufs"]]
                act.wait_ge(S("n_scaled"), 8 * r["op"] + k + 1)
                A(col(h_hi, k), t[:, :], ACT.Copy).then_inc(S("n_high"), 1)

        act.wait_ge(S("vec_loaded"), 16)
        act.wait_ge(S("consts"), 1)
        A(silc[:, :], V("c", 0, 16), ACT.Silu).then_inc(S("silc"), 1)
        for k in range(KT):
            act.wait_ge(S("x_loaded"), 16)
            if k >= 2:
                act.wait_ge(S("x_sq_used"), k - 1)
            A(squares[:, (k % 2) * T:(k % 2 + 1) * T], col(xr, k), ACT.Square).then_inc(S("x_sq"), 1)
        act.wait_ge(S("ctx_loaded"), 16)
        for k in range(KT):
            A(squares[:, (2 + k) * T:(2 + k) * T + C], ctxr[:, k * C:(k + 1) * C], ACT.Square).then_inc(S("c_sq"), 1)
        line(A(lt[0][:, :], V("lam", 0, 16), ACT.Abs))
        A(lt[0][:, :], lt[0][:, :], ACT.Exp, scale=-1.0).then_inc(S("lam_exp"), 1)
        act.wait_ge(S("stats"), 1)
        rsqrt(sq0[:, :], slot(3), D, eps6).then_inc(S("rs"), 1)
        act.wait_ge(S("cx_stats"), 1)
        rsqrt(cx_rs[:, :], bank(5, 0, C), D, eps6).then_inc(S("cx_rs"), 1)
        for k in range(KT):
            act.wait_ge(S("n_scaled"), k + 1)
            A(col(h_hi, k), n_tmp[:, :], ACT.Copy).then_inc(S("n_high"), 1)
        act.wait_ge(S("c_scaled"), 1)
        A(hc_hi[:, :], ctxr[:, :], ACT.Copy).then_inc(S("c_high"), 1)
        act.wait_ge(S("c_high"), 1)
        end(act)

        begin(act, "even_in")
        act.sem_inc(S("e_evac"), 8)
        act.sem_inc(S("ga_stored"), 16)

        def even_head(h):
            w0 = first["w_even_in"] + 2
            wu = lambda n: act.wait_ge(S("w_used"), w0 + n + 6 * h)
            ev = lambda ins: ins.then_inc(S("e_evac"), 1)
            wu(1)
            act.wait_ge(S("e_u"), h + 1)
            A(xbp[:, XB0:XB0 + T], slot(0), ACT.Copy)
            ev(A(xbp[:, XBC:XBC + C], bank(6, 0, C), ACT.Copy))
            wu(3)
            act.wait_ge(S("ga_stored"), 16 * h + 16)
            ev(A(sg[:, :], slot(2), ACT.Sigmoid))
            store_yb(h)
            act.wait_ge(S("e_u"), h + 2)
            act.wait_ge(S("yb_stored"), 32 * h + 32)
            A(u_hi[:, :], u[:, :], ACT.Copy).then_inc(S("e_uh"), 1)
            act.wait_ge(S("e_lru"), h + 1)
            for g in range(4):
                d = g // 2
                if g < 3:
                    act.wait_ge(S("e_gate"), 3 * h + g + 1)
                else:
                    wu(4)
                buf, bias = (ra, ii)[g % 2][d], V(("b_r", "b_i")[g % 2], 8 * d + h)
                sl, b = ((0, 7), (1, 6), (2, 7), (0, 6))[g]
                A(buf[:, 0:T], slot(sl), ACT.Sigmoid, bias=bias)
                ev(A(buf[:, T:TC], bank(b, 0, C), ACT.Sigmoid, bias=bias))
            act.wait_ge(S("e_evac"), 8 * h + 14)
            for d in range(2):
                line.go(A(tt[d][:, :], ra[d][:, :], ACT.Tanh, scale=sp8[:, bass.ds(8 * d + h, 1)]))
            line.sync()
            for d in range(2):
                line(A(ra[d][:, :], ra[d][:, :], ACT.Exp, scale=nsp8[:, bass.ds(8 * d + h, 1)]))
                if d == 1:
                    act.wait_ge(S("e_q"), 2 * h + 1)
                A(a2[:, :], ra[d][:, :], ACT.Square).then_inc(S("e_a2"), 1)
            for d in range(2):
                act.wait_ge(S("e_q"), 2 * h + d + 1)
                A(tt[d][:, :], tt[d][:, :], ACT.Sqrt).then_inc(S("e_sqrt"), 1)
            wu(5)
            ev(A(gb[:, :], slot(1), ACT.Silu))
            wu(6)
            act.wait_ge(S("e_va"), h + 1)
            ev(A(sg[:, :], slot(2), ACT.Silu))
            act.wait_ge(S("e_evac"), 8 * h + 16)
            act.dma_start(tile(ga_d, h), sg[:, :]).then_inc(S("ga_stored"), 16)

        def store_yb(h):
            act.wait_ge(S("e_lru"), h + 1)
            act.dma_start(tile(yb_hi_d, h), yb_hi[:, :].bitcast(F32)).then_inc(S("yb_stored"), 16)
            act.dma_start(tile(yb_lo_d, h), yb_lo[:, :].bitcast(F32)).then_inc(S("yb_stored"), 16)

        line.repeat(8, 4, even_head)
        store_yb(8)
        act.wait_ge(S("yb_stored"), 32 * 9)
        act.wait_ge(S("ga_stored"), 16 * 9)
        end(act)

        begin(act, "even_out")
        act.dma_start(h_hi[:, :].bitcast(F32).rearrange("p (k t) -> p k t", k=KT),
                      yb_hi_d[P:9 * P, :].rearrange("(k p) t -> p k t", p=P)).then_inc(S("yb_loaded"), 16)
        act.dma_start(h_lo[:, :].bitcast(F32).rearrange("p (k t) -> p k t", k=KT),
                      yb_lo_d[P:9 * P, :].rearrange("(k p) t -> p k t", p=P)).then_inc(S("yb_loaded"), 16)
        for k in range(KT):
            act.wait_ge(S("ln_centered"), k + 1)
            if k >= 2:
                act.wait_ge(S("ln_var"), k - 1)
            A(tmp[k % 2][:, :], col(uc, k), ACT.Square).then_inc(S("ln_sq"), 1)
        act.wait_ge(S("ln_var"), 8)
        for k in range(2):
            act.dma_start(tmp[k][:, :], tile(ga_d, k)).then_inc(S(f"ga_loaded{k}"), 16)
        rsqrt(xs_[:, :], slot(3), D, eps5).then_inc(S("ln_rs"), 1)
        for k in range(KT):
            act.wait_ge(S("ln_scaled"), k + 1)
            A(col(uc, k), col(uc, k), ACT.Silu, bias=V("ln_b", k), scale=V("ln_g", k)).then_inc(S("ln_silu"), 1)
            act.wait_ge(S("ya_gated"), k + 1)
            A(col(y_hi, k), col(uc, k), ACT.Copy).then_inc(S("ya_high"), 1)
            if k + 2 < KT:
                act.dma_start(tmp[k % 2][:, :], tile(ga_d, k + 2)).then_inc(S(f"ga_loaded{k % 2}"), 16)
            act.wait_ge(S("ya_ready"), k + 1)
            act.dma_start(col(xr, k), tile(dram["xT"], k)).then_inc(S("x_in"), 16)
        def stored(m):
            act.wait_ge(S("x_new"), m + 1)
            act.dma_start(tile(x_d, m), col(xr, m)).then_inc(S("x_stored"), 16)
        with act.Fori(0, KT) as m:
            stored(m)
        high({"stat": 1, "op": 1, "bufs": 3})
        act.wait_ge(S("n_high"), 16)
        act.wait_ge(S("x_stored"), 16 * 8)
        end(act)

        def odd_groups(part):
            nm = "w_odd_in_" + "ab"[part]

            def group(i):
                g = 2 * part + i
                w0 = first[nm] + 2
                ev = lambda ins: ins.then_inc(S("o_act"), 1)
                for j in range(4):
                    act.wait_ge(S("w_used"), w0 + j + 1 + i * 12)
                    for b in range(2):
                        act.wait_ge(S("o_up"), 8 * g + 2 * j + b + 1)
                        ins = A(up[:, :].rearrange("p (r c) -> p r c", c=80)[:, :, 8:72],
                                bank(2 * j + b).rearrange("p (r c) -> p r c", c=64), ACT.Copy)
                        ins.then_inc(S("o_u"), 1)
                    act.wait_ge(S("o_u"), 8 * g + 2 * j + 2)
                    act.sem_inc(S("o_act"), 1)
                for j in range(4):
                    act.wait_ge(S("w_used"), w0 + 5 + 2 * j + i * 12)
                    act.wait_ge(S("o_gs"), 4 * g + j + 1)
                    ev(A(gs[j % 2][:, :], slot(2 * j % 4), ACT.Silu))
            with act.Fori(0, 2) as i:
                group(i)
            act.wait_ge(S("o_act"), 16 * part + 24)
            end(act)

        def out_load(src):
            for k in range(KT):
                act.dma_start(col(xr, k), tile(src, k)).then_inc(S("x_in"), 16)

        begin(act, "odd_a")
        act.sem_inc(S("o_act"), 8)
        odd_groups(0)

        def out_phase(r, name, spec=None, store=True):
            begin(act, name)
            out_load(x_d)
            if store:
                n0 = 8 * out_phase.stores

                def stored(m):
                    act.wait_ge(S("x_new"), 8 * r + m + 1)
                    act.dma_start(tile(x_d, m), col(xr, m)).then_inc(S("x_stored"), 16)
                with act.Fori(0, KT) as m:
                    stored(m)
                out_phase.stores += 1
                act.wait_ge(S("x_stored"), 16 * 8 * out_phase.stores)
            if spec:
                high(spec)
            end(act)
        out_phase.stores = 1

        out_phase(1, "oout_a")
        begin(act, "odd_b")
        odd_groups(1)
        out_phase(2, "oout_b", {"stat": 2}, store=False)
        begin(act, "final1")
        with act.Fori(0, KT) as m:
            act.wait_ge(S("f1_new"), m + 1)
            act.dma_start(tile(x_d, m), col(xr, m)).then_inc(S("x_stored"), 16)
        out_phase.stores += 1
        high({"stat": 3, "op": 2, "bufs": 3})
        act.wait_ge(S("n_high"), 24)
        act.wait_ge(S("x_stored"), 16 * 8 * out_phase.stores)
        end(act)

        begin(act, "gla")
        act.wait_ge(S("w_used"), first["w_gla_in"] + 2)
        A(alr[0:16, :], slot(0)[0:16, :], ACT.Copy).then_inc(S("g_alr"), 1)

        def gla_head(i):
            wu = lambda n: act.wait_ge(S("w_used"), first["w_gla_in"] + 2 + n + 6 * i)
            act.dma_start(a2s[0:16, :], dram["a2"][bass.ds(i * 16, 16), :]).then_inc(S("a2_loaded"), 16)
            act.wait_ge(S("g_min"), i + 1)
            line(A(te[:, :], slot(3), ACT.Abs, bias=V("b_a", i)))
            act.sem_inc(S("g_ab"), 1)
            line(A(te[:, :], te[:, :], ACT.Exp, scale=-1.0))
            A(te[:, :], te[:, :], ACT.Ln, bias=one1[:, 0:1]).then_inc(S("g_te"), 1)
            act.wait_ge(S("g_cum"), i + 1)
            A(te[:, :], cum[:, :], ACT.Exp, scale=1.0 / 16).then_inc(S("g_exp"), 1)
            A(kdec[:, :], cum[:, :], ACT.Exp, scale=-1.0 / 16).then_inc(S("g_exp"), 1)
            A(dec[:, :], cum[:, CH - 1::CH],
              ACT.Exp, scale=1.0 / 16).then_inc(S("g_exp"), 1)
            act.wait_ge(S("g_cl"), i + 1)
            A(kdec[:, :], kdec[:, :], ACT.Exp, scale=1.0 / 16).then_inc(S("g_exp"), 1)
            for v in range(2):
                wu(3 + v)
                A(vt[:, :].rearrange("p (b d) -> p b d", d=DV)[:, :, v * P:(v + 1) * P],
                  slot(2 + v).rearrange("p (b d) -> p b d", d=P), ACT.Copy).then_inc(S("g_v"), 1)
            act.wait_ge(S("g_pe"), 2 * i + 1)
            for q in range(2):
                r = slice(64 * q, 64 * q + 64)
                line.go(A(att[r, :].rearrange("p (b c) -> p b c", b=8)[:, :, 64 * q:64 * q + 64],
                          slot(0)[r, :].rearrange("p (b c) -> p b c", b=8)[:, :, 64 * q:64 * q + 64], ACT.Copy))
            line.sync()
            act.sem_inc(S("g_att"), 1)
            act.wait_ge(S("g_pe"), 2 * i + 2)
            act.wait_ge(S("g_v"), 2 * i + 2)
            A(kdt[:, :], slot(1), ACT.Copy).then_inc(S("g_kdt"), 1)
            act.wait_ge(S("g_o"), 8 * i + 8)
            line(A(osq[:, 0:T], slot(0), ACT.Square))
            A(osq[:, T:2 * T], slot(1), ACT.Square).then_inc(S("g_sq"), 1)
            wu(5)
            act.wait_ge(S("g_kdt"), i + 1)
            A(att[:, :], slot(2), ACT.Silu).then_inc(S("g_g0"), 1)
            act.wait_ge(S("g_ss"), i + 1)
            rsqrt(cum[:, :], slot(3), DV, eps6).then_inc(S("g_rs"), 1)
            wu(6)
            A(kdt[:, :], slot(2), ACT.Silu).then_inc(S("g_g1"), 1)

        line.repeat(4, 6, gla_head)
        act.wait_ge(S("g_g1"), 4)
        end(act)

        def p_load(r, layer):
            act.dma_start(pf[:, :].rearrange("p (k t) -> p k t", k=2),
                          dram["pT"][layer * 2 * P:(layer + 1) * 2 * P, :].rearrange("(k p) t -> p k t", p=P))\
                .then_inc(S("p_loaded"), 16)

        out_phase(3, "gout", {"stat": 4, "op": 3, "bufs": 3}, store=False)

        def ple(r, name):
            begin(act, name)
            p_load(r, r)
            nm = f"w_ple_{r}"

            def two(i):
                for q in range(2):
                    m = 2 * i + q
                    act.wait_ge(S("w_used"), first[nm] + 4 + 2 * m)
                    act.wait_ge(S("p_added"), 8 * r + m + 1)
                    A(tmp[q][:, :], slot(2 * q + 1), ACT.Sigmoid).then_inc(S("p_sig"), 1)
            with act.Fori(0, 4) as i:
                two(i)
            if r == 0:
                with act.Fori(0, KT) as m:
                    act.wait_ge(S("p_new"), m + 1)
                    act.dma_start(tile(x_d, m), col(xr, m)).then_inc(S("x_stored"), 16)
                out_phase.stores += 1
                high({"stat": 5, "op": 4, "bufs": 3})
                act.wait_ge(S("n_high"), 40)
                act.wait_ge(S("x_stored"), 16 * 8 * out_phase.stores)
            else:
                high({"stat": 7})
            end(act)
        ple(0, "ple0")

        begin(act, "fox")
        act.wait_ge(S("f_min"), 1)
        r16 = slice(0, 16)
        line(A(fz[1][r16, :], slot(0)[r16, :], ACT.Abs, bias=vec[0:16, VEC["b_f"][0]:VEC["b_f"][0] + 1]))
        line(A(fz[1][r16, :], fz[1][r16, :], ACT.Exp, scale=-1.0))
        A(fz[1][r16, :], fz[1][r16, :], ACT.Ln, bias=one1[0:16, 0:1]).then_inc(S("f_te"), 1)
        act.wait_ge(S("f_c"), 1)
        act.dma_start(negc_d, fz[2][r16, :]).then_inc(S("f_negc_out"), 16)
        act.wait_ge(S("f_negc_out"), 16)
        act.sem_inc(S("f_negc"), 1)

        def fox_pair(i):
            wu = lambda n: act.wait_ge(S("w_used"), first["w_fox_in"] + 2 + n + 4 * i)
            act.wait_ge(S("f_go"), i + 1)
            for j in range(2):
                wu(1 + j)
                line(A(lg[j][:, :], slot(j), ACT.Copy))
                if j == 1:
                    act.wait_ge(S("f_ss"), 2 * i + 1)
                A(fsq[:, :], lg[j][:, :], ACT.Square).then_inc(S("f_sq"), 1)
            for j in range(2):
                act.wait_ge(S("f_ss"), 2 * i + j + 1)
                if j == 1:
                    act.wait_ge(S("f_nrm"), 2 * i + 1)
                rsqrt(frs[:, :], slot(2 + j), FH, eps6).then_inc(S("f_rs"), 1)
            act.wait_ge(S("f_nrm"), 2 * i + 1)
            A(qh[:, :], lg[0][:, :], ACT.Copy).then_inc(S("f_high"), 1)
            act.wait_ge(S("f_nrm"), 2 * i + 2)
            A(kh[:, :], lg[1][:, :], ACT.Copy).then_inc(S("f_high"), 1)
            wu(3)
            A(vh[:, :], slot(0), ACT.Copy).then_inc(S("f_high"), 1)
            wu(4)
            A(gf[:, :], slot(1), ACT.Silu).then_inc(S("f_g"), 1)

            def load_c(hh):
                act.dma_start(negc[:, :], negc_d[bass.ds(2 * i + hh, 1), :].to_broadcast((P, T)))\
                    .then_inc(S("f_cin"), 16)
            load_c(0)

            def expo(s):
                t = s % 8
                n = (t + 1) * P
                act.wait_ge(S("f_nmx"), 16 * i + s + 1)
                A(lg[s % 2][:, 0:n], lg[s % 2][:, 0:n], ACT.Exp, bias=nmx[s % 2][:, 0:1],
                  accum_out=psm[s % 2][:, 0:1]).then_inc(S("f_exp"), 1)

            def pt_high(s):
                n = (s % 8 + 1) * P
                act.wait_ge(S("f_t"), 16 * i + s + 1)
                if s >= 1:
                    act.wait_ge(S("f_pv"), 16 * i + s)
                A(pth[:, 0:n], slot(0)[:, 0:n], ACT.Copy).then_inc(S("f_ph"), 1)

            expo(0)
            for s in range(16):
                if s == 7:
                    act.wait_ge(S("f_max"), 16 * i + 8)
                    load_c(1)
                if s < 15:
                    expo(s + 1)
                pt_high(s)

        line.repeat(8, 4, fox_pair)
        act.wait_ge(S("f_ph"), 128)
        end(act)
        out_phase(4, "fout", {"stat": 6, "op": 5, "bufs": 3}, store=False)
        ple(1, "ple1")
        begin(act, "end")
        for k in range(KT):
            act.wait_ge(S("out_ready"), k + 1)
            act.dma_start(tile(out, k), col(xr, k)).then_inc(S("out_stored"), 16)
        act.wait_ge(S("out_stored"), 16 * KT)

    @block.vector
    def _(dve):
        line = Line(dve, S("dve_line"))
        TT_, TS, STT = dve.tensor_tensor, dve.tensor_scalar, dve.scalar_tensor_tensor
        for t, v in ((eps6, 1e-6), (eps5, 1e-5), (one1, 1.0)):
            line.go(dve.memset(t[:, :], v))
        line.sync()
        dve.sem_inc(S("consts"), 1)
        dve.wait_ge(S("vec_loaded"), 16)
        line(TS(gq[:, :], V("q_norm"), FH ** -0.5, None, ALU.mult))

        for k in range(KT):
            dve.wait_ge(S("x_sq"), k + 1)
            s = squares[:, (k % 2) * T:(k % 2 + 1) * T]
            if k == 0:
                line.go(dve.tensor_copy(sq0[:, :], s))
            else:
                line.go(TT_(sq0[:, :], sq0[:, :], s, ALU.add))
            line.sync()
            dve.sem_inc(S("x_sq_used"), 1)
        dve.sem_inc(S("sq_ready"), 1)
        dve.wait_ge(S("c_sq"), 8)
        line(TT_(cx_rs[:, :], squares[:, 2 * T:2 * T + C], squares[:, 3 * T:3 * T + C], ALU.add))
        for k in range(2, KT):
            line(TT_(cx_rs[:, :], cx_rs[:, :], squares[:, (2 + k) * T:(2 + k) * T + C], ALU.add))
        dve.sem_inc(S("cx_sq"), 1)
        dve.wait_ge(S("lam_exp"), 1)
        line(TS(lt[1][:, :], lt[0][:, :], 2.0, None, ALU.add))
        line(dve.reciprocal(lt[1][:, :], lt[1][:, :]))
        line(TT_(lt[0][:, :], lt[0][:, :], lt[1][:, :], ALU.mult))
        line(TT_(lt[1][:, :], lt[0][:, :], lt[0][:, :], ALU.mult))
        line(TS(lt[2][:, :], lt[1][:, :], 1 / 17, 1 / 15, ALU.mult, ALU.add))
        for n in (13, 11, 9, 7, 5, 3, 1):
            line(TT_(lt[2][:, :], lt[2][:, :], lt[1][:, :], ALU.mult))
            line(TS(lt[2][:, :], lt[2][:, :], 1 / n, None, ALU.add))
        line(TT_(lt[2][:, :], lt[2][:, :], lt[0][:, :], ALU.mult))
        line(TS(lt[1][:, :], V("lam", 0, 16), -1.0, 0.0, ALU.mult, ALU.max))
        line(STT(out=lt[2][:, :], in0=lt[2][:, :], scalar=2.0, in1=lt[1][:, :], op0=ALU.mult, op1=ALU.add))
        line(TS(sp8[:, :], lt[2][:, :], LRU_C, None, ALU.mult))
        line(TS(nsp8[:, :], lt[2][:, :], -LRU_C, None, ALU.mult))
        mv = modv[:, :].rearrange("p (l m v) -> p l v m", l=2, v=2)

        def mod_layer(layer):
            dve.wait_ge(S("mod_used"), 6 * (layer + 1))
            for v in range(2):
                line(TT_(mv[:, layer, v, :], bank(layer, 0, 48).rearrange("p (m v) -> p v m", v=2)[:, v, :],
                         V("mod_b", 24 * layer, 24), ALU.add))
                line(STT(out=gsc[:, (2 * layer + v) * 8:(2 * layer + v + 1) * 8], in0=mv[:, layer, v, 8:16],
                         scalar=1.0, in1=V("norm_g", 8 * layer, 8), op0=ALU.add, op1=ALU.mult))
        mod_layer(0)

        def mod(layer, v, part, k):
            return modv[:, bass.ds(48 * layer + 2 * (8 * part + k) + v, 1)]

        dve.wait_ge(S("rs"), 1)
        for k in range(KT):
            if k >= 1:
                dve.wait_ge(S("n_high"), k)
                line(TT_(col(h_lo, k - 1), n_tmp[:, :], col(h_hi, k - 1).bitcast(F32), ALU.subtract))
            line(TT_(n_tmp[:, :], col(xr, k), sq0[:, :], ALU.mult))
            TS(n_tmp[:, :], n_tmp[:, :], gsc[:, k:k + 1], mod(0, 0, 0, k), ALU.mult, ALU.add)\
                .then_inc(S("n_scaled"), 1)
        dve.wait_ge(S("n_high"), 8)
        line(TT_(col(h_lo, 7), n_tmp[:, :], col(h_hi, 7).bitcast(F32), ALU.subtract))
        dve.sem_inc(S("h_ready"), 8)
        dve.wait_ge(S("cx_rs"), 1)
        for k in range(KT):
            c = ctxr[:, k * C:(k + 1) * C]
            line(TT_(c, c, cx_rs[:, :], ALU.mult))
            line(TS(c, c, gsc[:, 8 + k:9 + k], mod(0, 1, 0, k), ALU.mult, ALU.add))
        mod_layer(1)
        dve.sem_inc(S("c_scaled"), 1)
        dve.wait_ge(S("c_high"), 1)
        line(TT_(hc_lo[:, :], ctxr[:, :], hc_hi[:, :].bitcast(F32), ALU.subtract))
        end(dve)

        begin(dve, "even_in")
        line.go(dve.memset(xbp[:, :], 0.0))
        line.go(dve.memset(upad[:, :], 0.0))
        line.go(dve.memset(yb_hi[:, :].bitcast(F32), 0.0))
        line.go(dve.memset(yb_lo[:, :].bitcast(F32), 0.0))
        line.sync()
        dve.sem_inc(S("e_u"), 1)
        dve.sem_inc(S("e_lru"), 1)

        def even_head(h):
            dve.wait_ge(S("e_evac"), 8 * h + 9)
            for j in range(4):
                w = V("sconv_w", 8 * j + h)
                for o, n in ((0, T), (T, C)):
                    s = xbp[:, (XB0 if o == 0 else XBC) - 2 + j:(XB0 if o == 0 else XBC) - 2 + j + n]
                    if j >= 1:
                        line.sync(1)
                    if j == 0:
                        line.go(TS(u[:, o:o + n], s, w, V("sconv_b", h), ALU.mult, ALU.add))
                    else:
                        line.go(STT(out=u[:, o:o + n], in0=s, scalar=w, in1=u[:, o:o + n], op0=ALU.mult, op1=ALU.add))
            line.sync()
            dve.sem_inc(S("e_u"), 1)
            dve.wait_ge(S("e_uh"), h + 1)
            TT_(u_lo[:, :], u[:, :], u_hi[:, :].bitcast(F32), ALU.subtract).then_inc(S("e_ul"), 1)
            dve.wait_ge(S("e_evac"), 8 * h + 10)
            TT_(upad[:, PAD:PAD + T], slot(1), sg[:, :], ALU.mult).then_inc(S("e_va"), 1)
            dve.wait_ge(S("e_va"), h + 1)
            for j in range(TAPS):
                o = col(uc, h) if j % 2 == 0 else acc1[:, :]
                s, w = upad[:, j:j + T], V("conv_w", 8 * j + h)
                if j == 0:
                    line.go(TS(o, s, w, V("conv_b", h), ALU.mult, ALU.add))
                elif j == 1:
                    line.go(TS(o, s, w, None, ALU.mult))
                else:
                    line.sync(1)
                    line.go(STT(out=o, in0=s, scalar=w, in1=o, op0=ALU.mult, op1=ALU.add))
            line.sync()
            line.go(TT_(col(uc, h), col(uc, h), acc1[:, :], ALU.add))
            for d in range(2):
                dve.wait_ge(S("e_a2"), 2 * h + d + 1)
                STT(out=tt[d][:, :], in0=a2[:, :], scalar=1.0, in1=tt[d][:, :], op0=ALU.add, op1=ALU.mult)\
                    .then_inc(S("e_q"), 1)
                line.go(TT_(ii[d][:, :], ii[d][:, :], u[:, :], ALU.mult))
            line.sync()
            for d in range(2):
                dve.wait_ge(S("e_sqrt"), 2 * h + d + 1)
                line(TT_(tt[d][:, :], tt[d][:, :], ii[d][:, :], ALU.mult))
                for lo, hi, init in ((T, TC, 0.0), (0, T, ii[d][:, TC - 1:TC] if d == 0 else ii[d][:, T:T + 1])):
                    f = slice(lo, hi) if d == 0 else (slice(hi - 1, lo - 1, -1) if lo else slice(hi - 1, None, -1))
                    line(dve.tensor_tensor_scan(out=ii[d][:, f], data0=ra[d][:, f], data1=tt[d][:, f],
                                                initial=init, op0=ALU.mult, op1=ALU.add))
            line(TT_(tt[0][:, 0:T], ii[0][:, 0:T], ii[1][:, 0:T], ALU.add))
            dve.wait_ge(S("e_evac"), 8 * h + 15)
            line(TT_(tt[0][:, 0:T], tt[0][:, 0:T], gb[:, :], ALU.mult))
            line(dve.tensor_copy(yb_hi[:, :], tt[0][:, 0:T]))
            TT_(yb_lo[:, :], tt[0][:, 0:T], yb_hi[:, :].bitcast(F32), ALU.subtract).then_inc(S("e_lru"), 1)

        line.repeat(8, 8 + TAPS + 1 + 2 + 6 + 3, even_head)
        dve.wait_ge(S("e_lru"), 9)
        line.sync()
        end(dve)

        begin(dve, "even_out")
        dve.sem_inc(S("x_added"), 2)
        dve.wait_ge(S("ln_sum"), 1)
        line(TS(xs_[:, :], slot(3), 1.0 / D, None, ALU.mult))
        for k in range(KT):
            TT_(col(uc, k), col(uc, k), xs_[:, :], ALU.subtract).then_inc(S("ln_centered"), 1)
        dve.wait_ge(S("ln_rs"), 1)

        def scale_ln(k):
            TT_(col(uc, k), col(uc, k), xs_[:, :], ALU.mult).then_inc(S("ln_scaled"), 1)
        scale_ln(0)
        for k in range(KT):
            if k + 1 < KT:
                scale_ln(k + 1)
            dve.wait_ge(S("ln_silu"), k + 1)
            dve.wait_ge(S(f"ga_loaded{k % 2}"), 16 * (k // 2 + 1))
            TT_(col(uc, k), col(uc, k), tmp[k % 2][:, :], ALU.mult).then_inc(S("ya_gated"), 1)
            dve.wait_ge(S("ya_high"), k + 1)
            TT_(col(y_lo, k), col(uc, k), col(y_hi, k).bitcast(F32), ALU.subtract).then_inc(S("ya_ready"), 1)

        def residual(r, gate, name, last):
            if last:
                line(dve.memset(xs_[:, :], 0.0))

            def two(i):
                for q in range(2):
                    m = 2 * i + q
                    w = first[name] + 2 + (4 * i + 3 + q if name == "w_even_out" else 2 * i + q + 1)
                    dve.wait_ge(S("w_used"), w)
                    dve.wait_ge(S("x_in"), 128 * (r + 1))
                    if gate is None:
                        TT_(col(xr, m), slot(q), col(xr, m), ALU.add).then_inc(S("x_added"), 1)
                    else:
                        STT(out=col(xr, m), in0=slot(q), scalar=gate(m), in1=col(xr, m), op0=ALU.mult,
                            op1=ALU.add).then_inc(S("x_added"), 1)
                    dve.wait_ge(S("x_added"), 8 * r + m + 3)
                    dve.sem_inc(S("x_new"), 1)
                    if last:
                        line(TT_(tmp[0][:, :], col(xr, m), col(xr, m), ALU.mult))
                        line(TT_(xs_[:, :], xs_[:, :], tmp[0][:, :], ALU.add))
            line.repeat(4, 4 if last else 0, two)
            if last:
                dve.sem_inc(S("sq_ready"), 1)

        def normalize(stat, op, gain=None, layer=None):
            dve.wait_ge(S("rs"), stat + 1)
            for k in range(KT + 2):
                if k < KT:
                    t = tmp[k % 3]
                    if k >= 3:
                        dve.wait_ge(S("h_ready"), 8 * op + k - 2)
                    if layer is None:
                        STT(out=t[:, :], in0=col(xr, k), scalar=V(gain[0], gain[1] + k), in1=xs_[:, :],
                            op0=ALU.mult, op1=ALU.mult).then_inc(S("n_scaled"), 1)
                    else:
                        line(TT_(t[:, :], col(xr, k), xs_[:, :], ALU.mult))
                        TS(t[:, :], t[:, :], gsc[:, 16 * layer + k:16 * layer + k + 1], mod(layer, 0, 0, k),
                           ALU.mult, ALU.add).then_inc(S("n_scaled"), 1)
                if k >= 1 and k <= KT:
                    dve.wait_ge(S("n_high"), 8 * op + k)
                    TT_(col(h_lo, k - 1), tmp[(k - 1) % 3][:, :], col(h_hi, k - 1).bitcast(F32), ALU.subtract)\
                        .then_inc(S("h_ready"), 1)
            dve.wait_ge(S("h_ready"), 8 * op + 8)

        residual(0, lambda m: mod(0, 0, 2, m), "w_even_out", True)
        normalize(1, 1, layer=1)
        end(dve)

        def odd_groups(part):
            nm = "w_odd_in_" + "ab"[part]
            v3 = lambda t: t[:, :].rearrange("p (r c) -> p r c", c=80)
            for i in range(2):
                g = 2 * part + i
                w0 = first[nm] + 2 + 12 * i
                if i == 1:
                    dve.wait_ge(S("w_used"), w0)
                for j in range(4):
                    for b in range(2):
                        dve.wait_ge(S("o_u"), 8 * g + 2 * j + b + 1)
                        bufs = [pa, pb]
                        line(TT_(v3(pa)[:, :, 1:80], v3(up)[:, :, 0:79], v3(up)[:, :, 1:80], ALU.add))
                        cur, a, z = 0, 1, 80
                        for e in range(g):
                            s = 1 << e
                            a, z = a + s, z - s
                            line(TT_(v3(bufs[1 - cur])[:, :, a:z], v3(bufs[cur])[:, :, a - s:z - s],
                                     v3(bufs[cur])[:, :, a + s:z + s], ALU.add))
                            cur = 1 - cur
                        p3 = v3(bufs[cur])[:, :, 8:72]
                        rc = V("rcount", 64 * g, 64).unsqueeze(1).to_broadcast((P, 8, 64))
                        line(TT_(p3, p3, rc, ALU.mult))
                        o3 = v3(bufs[1 - cur])[:, :, 8:72]
                        line(TT_(o3, p3, v3(up)[:, :, 8:72], ALU.subtract))
                        dve.sem_inc(S("o_up"), 1)
                        dh = d_hi[:, j * T + b * HALF:j * T + (b + 1) * HALF]
                        dl = d_lo[:, j * T + b * HALF:j * T + (b + 1) * HALF]
                        r3 = lambda t: t.rearrange("p (r c) -> p r c", c=64)
                        line(dve.tensor_copy(r3(dh), o3))
                        line(TT_(r3(dl), o3, r3(dh).bitcast(F32), ALU.subtract))
                    dve.sem_inc(S("o_d"), 1)
                for j in range(4):
                    dve.wait_ge(S("w_used"), w0 + 6 + 2 * j)
                    dve.wait_ge(S("o_act"), 8 * g + 13 + j)
                    t = gs[j % 2][:, :]
                    m = 4 * i + j
                    STT(out=t, in0=slot((2 * j + 1) % 4), scalar=V("od_scale", 8 * part + m), in1=t,
                        op0=ALU.mult, op1=ALU.mult).then_inc(S("o_y"), 1)
                    dve.wait_ge(S("o_y"), 4 * g + j + 5)
                    line(dve.tensor_copy(col(y_hi, m), t))
                    line(TT_(col(y_lo, m), t, col(y_hi, m).bitcast(F32), ALU.subtract))
                    dve.sem_inc(S("o_gs"), 1)
            end(dve)

        begin(dve, "odd_a")
        dve.sem_inc(S("o_y"), 4)
        dve.sem_inc(S("o_gs"), 2)
        line(dve.memset(up[:, :], 0.0))
        dve.sem_inc(S("o_up"), 1)
        odd_groups(0)
        begin(dve, "oout_a")
        residual(1, lambda m: mod(1, 0, 2, m), "w_odd_out_a", False)
        end(dve)
        begin(dve, "odd_b")
        odd_groups(1)
        begin(dve, "oout_b")
        residual(2, lambda m: mod(1, 0, 2, m), "w_odd_out_b", True)
        dve.wait_ge(S("rs"), 3)
        end(dve)
        begin(dve, "final1")
        for k in range(KT):
            line(STT(out=col(xr, k), in0=col(xr, k), scalar=V("final_g", k), in1=xs_[:, :], op0=ALU.mult,
                     op1=ALU.mult))
            dve.sem_inc(S("f1_new"), 1)
            if k == 0:
                line(TT_(tmp[2][:, :], col(xr, k), col(xr, k), ALU.mult))
            else:
                line(TT_(tmp[0][:, :], col(xr, k), col(xr, k), ALU.mult))
                line(TT_(tmp[2][:, :], tmp[2][:, :], tmp[0][:, :], ALU.add))
        line(dve.tensor_copy(xs_[:, :], tmp[2][:, :]))
        dve.sem_inc(S("sq_ready"), 1)
        normalize(3, 2, gain=("norm_mixer", 0))
        end(dve)

        begin(dve, "gla")
        dve.sem_inc(S("g_go"), 1)
        line(dve.memset(cmask[:, :], 1.0))
        line(dve.memset(cmask[:, :].rearrange("p (n c) -> p n c", c=CH)[:, :, 0:1], 0.0))

        def gla_head(i):
            wu = lambda n: dve.wait_ge(S("w_used"), first["w_gla_in"] + 2 + n + 6 * i)
            line(dve.memset(att[:, :], 0.0))
            line(dve.memset(st[:, 0:DV], 0.0))
            dve.wait_ge(S("g_lg"), i + 1)
            TS(cum[:, :], slot(3), V("b_a", i), 0.0, ALU.add, ALU.min).then_inc(S("g_min"), 1)
            dve.wait_ge(S("g_te"), i + 1)
            line(TT_(te[:, :], cum[:, :], te[:, :], ALU.subtract))
            dve.tensor_tensor_scan(out=cum[:, :], data0=cmask[:, :], data1=te[:, :], initial=0.0,
                                   op0=ALU.mult, op1=ALU.add).then_inc(S("g_cum"), 1)
            dve.wait_ge(S("g_exp"), 4 * i + 1)
            wu(1)
            line.go(STT(out=qin[:, :], in0=slot(0), scalar=DK ** -0.5, in1=te[:, :], op0=ALU.mult, op1=ALU.mult))
            dve.wait_ge(S("g_exp"), 4 * i + 3)
            wu(2)
            line(TT_(kin[:, :], slot(1), kdec[:, :], ALU.mult))
            c3 = cum[:, :].rearrange("p (n c) -> p n c", c=CH)
            TT_(kdec[:, :].rearrange("p (n c) -> p n c", c=CH), c3[:, :, CH - 1:CH].to_broadcast((P, 16, CH)),
                c3, ALU.subtract).then_inc(S("g_cl"), 1)
            dve.wait_ge(S("g_exp"), 4 * i + 4)
            TT_(kdec[:, :], slot(1), kdec[:, :], ALU.mult).then_inc(S("g_kdec"), 1)
            dve.sem_inc(S("g_st"), 1)
            for n in range(15):
                if n % 4 == 0:
                    dve.wait_ge(S("g_kv"), 4 * i + n // 4 + 1)
                if n + 1 >= 8:
                    if (n + 1) % 2 == 0:
                        dve.wait_ge(S("g_o"), 8 * i + (n + 1 - 8) // 2 + 1)
                STT(out=st[:, ((n + 1) % 8) * DV:((n + 1) % 8 + 1) * DV], in0=st[:, (n % 8) * DV:(n % 8 + 1) * DV],
                    scalar=dec[:, n:n + 1], in1=kv_at(n),
                    op0=ALU.mult, op1=ALU.add).then_inc(S("g_st"), 1)
                dve.wait_ge(S("g_st"), 16 * i + n + 2)
            for v, sem in enumerate(("g_g0", "g_g1")):
                dve.wait_ge(S("g_rs"), i + 1)
                line(STT(out=kdec[:, :], in0=slot(v), scalar=V("o_norm", v), in1=cum[:, :], op0=ALU.mult, op1=ALU.mult))
                dve.wait_ge(S(sem), i + 1)
                line(TT_(kdec[:, :], kdec[:, :], (att, kdt)[v][:, :], ALU.mult))
                line(dve.tensor_copy(col(y_hi, 2 * i + v), kdec[:, :]))
                line(TT_(col(y_lo, 2 * i + v), kdec[:, :], col(y_hi, 2 * i + v).bitcast(F32), ALU.subtract))
            dve.sem_inc(S("g_go"), 1)

        line.repeat(4, 2 + 1 + 2 + 8, gla_head)
        end(dve)
        begin(dve, "gout")
        residual(3, None, "w_gla_out", True)
        normalize(4, 3, gain=("ple_norm", 0))
        end(dve)

        def ple(r, name):
            begin(dve, name)
            if r == 0:
                dve.sem_inc(S("p_added"), 2)
            dve.wait_ge(S("p_loaded"), 16 * (r + 1))
            line(dve.tensor_copy(p_hi[:, :], pf[:, :]))
            TT_(p_lo[:, :], pf[:, :], p_hi[:, :].bitcast(F32), ALU.subtract).then_inc(S("p_split"), 1)
            line(dve.memset(xs_[:, :], 0.0))

            def two(i):
                for q in range(2):
                    m = 2 * i + q
                    dve.wait_ge(S("p_sig"), 8 * r + m + 1)
                    line(TT_(tmp[2][:, :], slot(2 * q), tmp[q][:, :], ALU.mult))
                    dve.sem_inc(S("p_added"), 1)
                    line(TT_(col(xr, m), col(xr, m), tmp[2][:, :], ALU.add))
                    dve.sem_inc(S("p_new"), 1)
                    line(TT_(tmp[2][:, :], col(xr, m), col(xr, m), ALU.mult))
                    line(TT_(xs_[:, :], xs_[:, :], tmp[2][:, :], ALU.add))
            line.repeat(4, 8, two)
            dve.sem_inc(S("sq_ready"), 1)
            if r == 0:
                normalize(5, 4, gain=("norm_mixer", 8))
            else:
                dve.wait_ge(S("rs"), 8)
            end(dve)
        ple(0, "ple0")

        begin(dve, "fox")
        r16 = slice(0, 16)
        dve.wait_ge(S("w_used"), first["w_fox_in"] + 2)
        TS(fz[0][r16, :], slot(0)[r16, :], vec[0:16, VEC["b_f"][0]:VEC["b_f"][0] + 1], 0.0, ALU.add, ALU.min)\
            .then_inc(S("f_min"), 1)
        line(dve.memset(fz[3][r16, :], 1.0))
        dve.wait_ge(S("f_te"), 1)
        line(TT_(fz[0][r16, :], fz[1][r16, :], fz[0][r16, :], ALU.subtract))
        dve.tensor_tensor_scan(out=fz[2][r16, :], data0=fz[3][r16, :], data1=fz[0][r16, :], initial=0.0,
                               op0=ALU.mult, op1=ALU.add).then_inc(S("f_c"), 1)
        dve.wait_ge(S("f_negc"), 1)
        dve.sem_inc(S("f_go"), 1)

        def fox_pair(i):
            for j in range(2):
                dve.wait_ge(S("f_rs"), 2 * i + j + 1)
                STT(out=lg[j][:, :], in0=lg[j][:, :], scalar=gq[:, 0:1] if j == 0 else V("k_norm"), in1=frs[:, :],
                    op0=ALU.mult, op1=ALU.mult).then_inc(S("f_nrm"), 1)
            for n, (lo, src, hi) in enumerate(((ql, lg[0], qh), (kl, lg[1], kh), (vl, None, vh))):
                dve.wait_ge(S("f_high"), 3 * i + n + 1)
                line.go(TT_(lo[:, :], src[:, :] if src is not None else slot(0), hi[:, :].bitcast(F32), ALU.subtract))
            line.sync()
            dve.wait_ge(S("f_g"), i + 1)
            dve.sem_inc(S("f_ready"), 1)

            def top(s):
                t = s % 8
                n = (t + 1) * P
                dve.wait_ge(S("f_qk"), 16 * i + s + 1)
                dve.wait_ge(S("f_cin"), 32 * i + 16 * (s // 8) + 16)
                if s >= 2:
                    dve.wait_ge(S("f_t"), 16 * i + s - 1)
                dve.sem_inc(S("max_begun"), 1)
                dve.tensor_tensor_reduce(lg[s % 2][:, 0:n], slot(2 + s % 2)[:, 0:n], negc[:, 0:n], 1.0, -3e38,
                                         ALU.add, ALU.max, mx[s % 2][:, 0:1]).then_inc(S("f_max"), 1)
                dve.wait_ge(S("f_max"), 16 * i + s + 1)
                TS(nmx[s % 2][:, :], mx[s % 2][:, :], -1.0, None, ALU.mult).then_inc(S("f_nmx"), 1)

            top(0)
            for s in range(16):
                n = (s % 8 + 1) * P
                hh = s // 8
                if s < 15:
                    top(s + 1)
                dve.wait_ge(S("f_exp"), 16 * i + s + 1)
                line(dve.reciprocal(rps[s % 2][:, :], psm[s % 2][:, :]))
                TS(lg[s % 2][:, 0:n], lg[s % 2][:, 0:n], rps[s % 2][:, 0:1], None, ALU.mult).then_inc(S("f_prob"), 1)
                dve.wait_ge(S("f_ph"), 16 * i + s + 1)
                TT_(ptl[:, 0:n], slot(0)[:, 0:n], pth[:, 0:n].bitcast(F32), ALU.subtract).then_inc(S("f_pt"), 1)
                if s % 8 == 7:
                    r = slice(64 * hh, 64 * hh + 64)
                    dve.wait_ge(S("f_pv"), 16 * i + s + 1)
                    line(TT_(gf[r, :], slot(1)[r, :], gf[r, :], ALU.mult))
                    dve.sem_inc(S("f_y"), 1)
                    yh_, yl_ = y_hi[r, bass.ds(i * T, T)], y_lo[r, bass.ds(i * T, T)]
                    line(dve.tensor_copy(yh_, gf[r, :]))
                    line(TT_(yl_, gf[r, :], yh_.bitcast(F32), ALU.subtract))
            dve.sem_inc(S("f_go"), 1)

        line.repeat(8, 3 + 16 + 6, fox_pair)
        end(dve)
        begin(dve, "fout")
        residual(4, None, "w_fox_out", True)
        normalize(6, 5, gain=("ple_norm", 8))
        end(dve)
        ple(1, "ple1")
        begin(dve, "end")
        for k in range(KT):
            STT(out=col(xr, k), in0=col(xr, k), scalar=V("final_norm", k), in1=xs_[:, :], op0=ALU.mult,
                op1=ALU.mult).then_inc(S("out_ready"), 1)

    block_cm.__exit__(None, None, None)


def _tiles(w):
    k, m = w.shape
    return w.reshape(k // P, P, m // P, P).transpose(2, 1, 0, 3).reshape(m // P, P, k)


def _stream(*rounds):
    return np.ascontiguousarray(np.concatenate([np.concatenate(r, axis=1) for r in rounds], axis=0))


def _cols(v):
    return v.reshape(-1, P).T


def _rank_tiles(w):
    t = _tiles(np.concatenate([w, np.zeros((D, P - w.shape[1]), np.float32)], axis=1))[0]
    return [t[:, 0:512], t[:, 512:1024]]


def _streams(a):
    w = _tiles(a["ev_w_in"][0])
    va, vg, ga, xb, gb = (w[8 * k:8 * k + 8] for k in range(5))
    gates = [np.concatenate([a[n][0, d, h] for d in range(2) for n in ("ev_w_r", "ev_w_i")], axis=1) for h in range(8)]
    s = {"w_even_in": _stream(*[[t for h in (2 * i, 2 * i + 1) for t in (xb[h], va[h], vg[h], gates[h], gb[h], ga[h])]
                                for i in range(4)])}
    wa, wb = _tiles(a["ev_w_out"][0][0:D]), _tiles(a["ev_w_out"][0][D:2 * D])
    s["w_even_out"] = _stream(*[[wb[2 * i], wb[2 * i + 1], wa[2 * i], wa[2 * i + 1]] for i in range(4)])
    w = _tiles(a["od_w_in"][0])
    grp = [_tiles(a["od_w_grp"][0, g]) for g in range(4)]
    for part in range(2):
        s["w_odd_in_" + "ab"[part]] = _stream(*[
            [w[4 * g + j] for j in range(4)] + [t for j in range(4) for t in (w[16 + 4 * g + j], grp[g][j])]
            for g in (2 * part, 2 * part + 1)])
        wo = _tiles(a["od_w_out"][0][part * D:(part + 1) * D])
        s["w_odd_out_" + "ab"[part]] = _stream(*[[wo[2 * i], wo[2 * i + 1]] for i in range(4)])
    w = a["gla_w_in_2"][0]
    s["w_gla_rank"] = _stream(_rank_tiles(w[:, 3072:3088]))
    w = _tiles(w[:, 0:3072])
    s["w_gla_in"] = _stream(*[[w[i], w[4 + i], w[8 + 2 * i], w[9 + 2 * i], w[16 + 2 * i], w[17 + 2 * i]] for i in range(4)])
    w = a["fox_w_in_2"][0]
    s["w_fox_gate"] = _stream(_rank_tiles(w[:, 4096:4112]))
    w = _tiles(w[:, 0:4096])
    s["w_fox_in"] = _stream(*[[w[i], w[8 + i], w[16 + i], w[24 + i]] for i in range(8)])
    for n, src in (("w_gla_out", "gla_w_out_2"), ("w_fox_out", "fox_w_out_2")):
        w = _tiles(a[src][0])
        s[n] = _stream(*[[w[2 * i], w[2 * i + 1]] for i in range(4)])
    for r in range(2):
        wp, wg = _tiles(a["ple_proj_2"][r]), _tiles(a["ple_gate_2"][r])
        s[f"w_ple_{r}"] = _stream(*[[wp[m], wg[m]] for m in range(8)])
    w = np.concatenate([_tiles(a["mod_w"][0]), _tiles(a["mod_w"][1])])
    s["w_mod"] = _stream(*[[w[4 * c + q] for q in range(4)] for c in range(12)])
    return s


def _vectors(a):
    f = np.float32
    t = np.arange(ROW)
    v = {
        "c": np.stack([_cols(a["c"][0]), _cols(a["c_ctx"])], axis=2).reshape(P, 16),
        "mod_b": _cols(a["mod_b"]), "norm_g": _cols(a["norm_g"]), "conv_w": _cols(a["ev_conv_w"][0]),
        "conv_b": _cols(a["ev_conv_b"]), "ln_g": _cols(a["ev_ln_g"]), "ln_b": _cols(a["ev_ln_b"]),
        "sconv_w": _cols(a["ev_sconv_w"][0]), "sconv_b": _cols(a["ev_sconv_b"]), "b_r": _cols(a["ev_b_r"][0]),
        "b_i": _cols(a["ev_b_i"][0]), "lam": _cols(a["ev_lam"][0]), "od_scale": _cols(a["od_scale"]),
        "final_g": _cols(a["final_g"]), "norm_mixer": _cols(a["norm_mixer_2"]), "b_a": _cols(a["gla_b_a_2"]),
        "o_norm": _cols(a["gla_o_norm_2"]), "q_norm": np.tile(a["fox_q_norm_2"], (1, 2)).T,
        "k_norm": np.tile(a["fox_k_norm_2"], (1, 2)).T,
        "b_f": np.concatenate([a["fox_b_f_2"][0], np.zeros(P - 16, f)])[:, None],
        "ple_norm": _cols(a["ple_norm_2"]), "final_norm": _cols(a["final_norm_2"]),
        "rcount": np.tile(np.concatenate([1.0 / (np.minimum(t + h, ROW) - np.maximum(t - h, 0))
                                          for h in (1, 2, 4, 8)]).astype(f), (P, 1)),
        "ident": np.eye(P, dtype=f), "ones": np.ones((P, P), f),
        "heads": np.kron(np.eye(2, dtype=f), np.ones((FH, FH), f)),
    }
    for name, (_, n) in VEC.items():
        assert v[name].shape == (P, n), (name, v[name].shape, n)
    return np.ascontiguousarray(np.concatenate([v[name] for name in VEC], axis=1))


def kernel(**inputs):
    import concourse.bacc as bacc
    from concourse.bass_utils import run_bass_kernel_spmd

    a = {k: np.asarray(v) for k, v in inputs.items()}
    arrays = _streams(a)
    arrays["vec"] = _vectors(a)
    arrays["xT"] = np.ascontiguousarray(a["x"][0].T)
    arrays["ctxT"] = np.ascontiguousarray(a["ctx"][0].T)
    arrays["pT"] = np.ascontiguousarray(a["p_2"][:, 0].transpose(0, 2, 1).reshape(512, T))
    arrays["a2"] = np.ascontiguousarray(a["gla_w_a2_2"][0].reshape(16, 4, P).transpose(1, 0, 2).reshape(64, P))
    nc = bacc.Bacc("TRN2", target_bir_lowering=False, num_devices=1)
    dram = {n: nc.dram_tensor(n, v.shape, F32, kind="ExternalInput").ap() for n, v in arrays.items()}
    out = nc.dram_tensor("out", (D, T), F32, kind="ExternalOutput").ap()
    build(nc, dram, out)
    r = run_bass_kernel_spmd(nc, [arrays], core_ids=[0])
    return np.ascontiguousarray(r.results[0]["out"].T).reshape(1, T, D)
```

```python
import numpy as np
import concourse.bass as bass
from concourse import mybir

F32, F32R, BF16 = mybir.dt.float32, mybir.dt.float32r, mybir.dt.bfloat16
ALU, ACT, AX = mybir.AluOpType, mybir.ActivationFunctionType, mybir.AxisListType

P = 128
D = 1024
T = 1024
C = 256
KT = D // P
TC = T + C
HALF = 512
TAPS, PAD = 31, 15
ROW = 64
CH = 64
DK, DV = 128, 256
FH = 64
LRU_C = 8.0
KB = 1024

STREAMS = [
    ("w_even_in", 4, [1024, 1024, 1024, 512, 1024, 1024] * 2),
    ("w_even_out", 4, [1024] * 4),
    ("w_odd_in_a", 2, [1024] * 4 + [1024, 512] * 4),
    ("w_odd_out_a", 4, [1024] * 2),
    ("w_odd_in_b", 2, [1024] * 4 + [1024, 512] * 4),
    ("w_odd_out_b", 4, [1024] * 2),
    ("w_gla_rank", 1, [512] * 2),
    ("w_gla_in", 4, [1024] * 6),
    ("w_gla_out", 4, [1024] * 2),
    ("w_ple_0", 8, [256, 1024]),
    ("w_fox_gate", 1, [512] * 2),
    ("w_fox_in", 8, [1024] * 4),
    ("w_fox_out", 4, [1024] * 2),
    ("w_ple_1", 8, [256, 1024]),
]

VEC = {}
_at = 0
for _name, _n in [("c", 16), ("mod_b", 48), ("norm_g", 16), ("conv_w", 8 * TAPS), ("conv_b", 8),
                  ("ln_g", 8), ("ln_b", 8), ("sconv_w", 32), ("sconv_b", 8), ("b_r", 16), ("b_i", 16),
                  ("lam", 16), ("od_scale", 16), ("final_g", 8), ("norm_mixer", 16), ("b_a", 4),
                  ("o_norm", 2), ("q_norm", 1), ("k_norm", 1), ("b_f", 1), ("ple_norm", 16),
                  ("final_norm", 8), ("rcount", 4 * ROW), ("ident", P), ("ones", P), ("heads", P)]:
    VEC[_name] = (_at, _n)
    _at += _n
NVEC = _at


class Line:

    def __init__(self, eng, sem):
        self.eng, self.sem, self.base, self.k = eng, sem, 0, 0

    def __call__(self, ins):
        ins.then_inc(self.sem, 1)
        self.k += 1
        self.eng.wait_ge(self.sem, self.base + self.k)

    def go(self, ins):
        ins.then_inc(self.sem, 1)
        self.k += 1

    def sync(self, back=0):
        self.eng.wait_ge(self.sem, self.base + (self.k - back))

    def repeat(self, times, steps, body):
        start = self.base + self.k
        with self.eng.Fori(0, times) as i:
            self.base, self.k = start + i * steps, 0
            body(i)
            assert self.k == steps, (self.k, steps)
        self.base, self.k = start + times * steps, 0


def build(nc, dram, out):
    base = (nc.sbuf_base + 31) // 32 * 32
    R0, R1, MISC = base + 32 * KB - 160, base + 96 * KB - 160, base + 160 * KB - 160
    assert MISC + 48 * KB <= nc.sbuf_usable_end, (MISC, nc.sbuf_usable_end)

    def sb(name, cols, at, dt=F32):
        return nc.alloc_sbuf_tensor_at("t_" + name, [P, cols], dt, offset=at)

    sems = {}

    def S(name):
        if name not in sems:
            sems[name] = nc.alloc_semaphore(name)
        return sems[name]

    wst = [sb(f"wst{i}", 1024, base + i * 4 * KB) for i in range(2)]
    wh = [sb(f"wh{i}", 1024, base + (2 + i) * 4 * KB, F32R) for i in range(2)]
    wl = [sb(f"wl{i}", 1024, base + (4 + i) * 4 * KB, F32R) for i in range(2)]
    cst = base + 24 * KB
    vec = sb("vec", NVEC, cst)
    vend = cst + (4 * NVEC + 31) // 32 * 32
    a2s = sb("a2s", P, vend)
    cx_rs = sb("cx_rs", C, vend + 512)
    sm = vend + 512 + 1024
    modv = sb("modv", 96, sm)
    gsc = sb("gsc", 32, sm + 384)
    silc = sb("silc", 16, sm + 512)
    sp8 = sb("sp8", 16, sm + 576)
    nsp8 = sb("nsp8", 16, sm + 640)
    lt = [sb(f"lt{i}", 16, sm + 704 + 64 * i) for i in range(3)]
    dec = sb("dec", 16, sm + 896)
    nma = [sb(f"nma{i}", 1, sm + 960 + 32 * i) for i in range(2)]
    nmx = [sb(f"nmx{i}", 1, sm + 1024 + 32 * i) for i in range(2)]
    psm = [sb(f"psm{i}", 1, sm + 1088 + 32 * i) for i in range(2)]
    rps = [sb(f"rps{i}", 1, sm + 1152 + 32 * i) for i in range(2)]
    gq = sb("gq", 1, sm + 1216)
    eps6 = sb("eps6", 1, sm + 1248)
    eps5 = sb("eps5", 1, sm + 1280)
    one1 = sb("one1", 1, sm + 1312)
    tri = sb("tri", P, sm + 1344, BF16)
    idb = sb("idb", P, sm + 1600, BF16)
    assert sm + 1856 <= R0, (sm + 1856, R0)

    h_hi, h_lo = sb("h_hi", 8192, R0, F32R), sb("h_lo", 8192, R0 + 32 * KB, F32R)
    y_hi, y_lo = sb("y_hi", 8192, R1, F32R), sb("y_lo", 8192, R1 + 32 * KB, F32R)
    xr = sb("xr", 8192, MISC)
    xs_ = sb("rs", 1024, MISC + 32 * KB)
    tmp = [sb(f"tmp{i}", 1024, MISC + (36 + 4 * i) * KB) for i in range(3)]

    def V(name, j=0, n=1):
        return vec[:, bass.ds(VEC[name][0] + j, n)]

    ident, ones, heads = V("ident", 0, P), V("ones", 0, P), V("heads", 0, P)

    ps = nc.alloc_psum_tensor("ps", [P, 8, HALF], F32)

    def slot(s, cols=1024):
        return ps[:, 2 * s:2 * s + 2, :].rearrange("p a b -> p (a b)")[:, 0:cols]

    def kv_at(n):
        c = (n % 2) * 2 + n % 4 // 2
        return slot(2 + n // 4 % 2)[:, c * DV:(c + 1) * DV]

    def bank(b, lo=0, hi=HALF):
        return ps[:, b, lo:hi]

    def scratch(name, n, cols=1024):
        return nc.dram_tensor(name, [n * P, cols], F32, kind="Internal").ap()
    yb_hi_d, yb_lo_d, ga_d = scratch("yb_hi_d", 9), scratch("yb_lo_d", 9), scratch("ga_d", 8)
    x_d = scratch("x_d", 8)
    negc_d = nc.dram_tensor("negc_d", [16, 1024], F32, kind="Internal").ap()

    def tile(ap, m):
        return ap[bass.ds(m * P, P), :]

    def col(t, m, n=1024):
        return t[:, bass.ds(m * n, n)]

    first, n = {}, 0
    for name, times, widths in STREAMS:
        first[name] = n
        n += times * len(widths)
        assert len(widths) % 2 == 0
    TILES = n
    PHASES = ["start", "even_in", "even_out", "odd_a", "oout_a", "odd_b", "oout_b", "final1",
              "gla", "gout", "ple0", "fox", "fout", "ple1", "end"]

    def begin(eng, phase):
        k = PHASES.index(phase)
        if k:
            eng.wait_ge(S("phase_ended"), 3 * k)

    def end(eng):
        eng.sem_inc(S("phase_ended"), 1)

    hc_hi, hc_lo = sb("hc_hi", 2048, R1, F32R), sb("hc_lo", 2048, R1 + 8 * KB, F32R)
    L0 = R1 + 16 * KB
    u = sb("u", TC, L0)
    u_hi, u_lo = sb("u_hi", TC, L0 + 5120, F32R), sb("u_lo", TC, L0 + 2 * 5120, F32R)
    yb_hi, yb_lo = sb("yb_hi", T, L0 + 5120, F32R), sb("yb_lo", T, L0 + 2 * 5120, F32R)
    a2 = sb("a2", TC, L0 + 5120)
    gb = sb("gb", T, L0 + 5120)
    ra = [sb(f"ra{d}", TC, L0 + (3 + 2 * d) * 5120) for d in range(2)]
    ii = [sb(f"ii{d}", TC, L0 + (4 + 2 * d) * 5120) for d in range(2)]
    tt = [sb("tt0", TC, L0 + 7 * 5120), sb("tt1", TC, MISC + 32 * KB)]
    sg = sb("sg", T, L0 + 8 * 5120)
    acc1 = sb("acc1", T, L0 + 8 * 5120 + 4096)
    uc = sb("uc", 8192, MISC)
    XB0, XBC = 2, 2 + T + 1 + 2
    xbp = sb("xbp", XBC + C + 1, MISC + 32 * KB + 5120)
    upad = sb("upad", T + 2 * PAD, MISC + 32 * KB + 5120 + 5152)
    assert 4 * (XBC + C + 1) <= 5152 and 5120 + 5152 + 4 * (T + 2 * PAD) <= 16 * KB
    d_hi, d_lo = sb("d_hi", 4096, MISC, F32R), sb("d_lo", 4096, MISC + 16 * KB, F32R)
    gs = [sb(f"gs{i}", T, MISC + (32 + 4 * i) * KB) for i in range(2)]
    up = sb("up", 8 * 80, MISC + 40 * KB)
    pa, pb = sb("pa", 8 * 80, MISC + 40 * KB + 2560), sb("pb", 8 * 80, MISC + 40 * KB + 5120)
    qin, kin, kdec, cum, te = (sb(nm, T, MISC + 4 * i * KB) for i, nm in enumerate(["qin", "kin", "kdec", "cum", "te"]))
    vt = sb("vt", 2048, MISC + 20 * KB)
    kdt = sb("kdt", T, MISC + 28 * KB)
    att = sb("att", T, MISC + 32 * KB)
    st = sb("st", 2048, MISC + 36 * KB)
    cmask = sb("cmask", T, MISC + 44 * KB)
    alr = sb("alr", T, R1 + 60 * KB)
    osq = sb("osq", 2048, MISC)
    pair_buf = []
    for par in range(2):
        at = MISC + 24 * KB * par
        b = {nm: sb(f"{nm}{par}", T, at + 4 * KB * n, F32R) for n, nm in enumerate(["qh", "ql", "kh", "kl", "vh", "vl"])}
        b |= {nm + "_f": sb(f"{nm}_f{par}", T, at + 4 * KB * n) for n, nm in enumerate(["qh", "ql", "kh", "kl"])}
        pair_buf.append(b)
    negc = [sb(f"negc{i}", T, R1 + (32 + 4 * i) * KB) for i in range(2)]
    lg = [sb(f"lg{i}", T, R1 + (40 + 4 * i) * KB) for i in range(2)]
    pth = [sb(f"pth{i}", HALF, R1 + (48 + 2 * i) * KB, F32R) for i in range(4)]
    ptl = [sb(f"ptl{i}", HALF, R1 + (56 + 2 * i) * KB, F32R) for i in range(4)]
    yf = sb("yf", 8192, R1)
    fz = [sb(f"fz{i}", T, MISC + 4 * i * KB) for i in range(4)]
    STEPS = [divmod(s, 8) for s in range(16)]
    UNITS = [(s, lo, min(lo + 4, t + 1)) for s, (_, t) in enumerate(STEPS) for lo in range(0, t + 1, 4)]
    UNITS_OF = [[q for q, un in enumerate(UNITS) if un[0] == s] for s in range(16)]
    NU = len(UNITS)

    def step_of(p, par, s):
        return (p, par, s) if s < 16 else (p + 1, 1 - par, s - 16)
    assert NU % 3 == 0 and NU % 4 == 0
    pf = sb("pf", 2048, R1 + 16 * KB)
    p_hi, p_lo = sb("p_hi", 2048, R1, F32R), sb("p_lo", 2048, R1 + 8 * KB, F32R)

    block_cm = nc.Block()
    block = block_cm.__enter__()

    modw = sb("modw", 16384, R1)
    ctxr = sb("ctxr", 2048, MISC + 32 * KB)
    squares = sb("squares", 10 * T, R0)
    sq0 = sb("sq0", T, MISC + 40 * KB)
    n_tmp = sb("n_tmp", T, MISC + 44 * KB)
    NCHUNK = 12

    @block.sync
    def _(sp):
        sp.dma_start(vec[:, :], dram["vec"]).then_inc(S("vec_loaded"), 16)
        sp.dma_start(xr[:, :].rearrange("p (k t) -> p k t", k=KT),
                     dram["xT"].rearrange("(k p) t -> p k t", p=P)).then_inc(S("x_loaded"), 16)
        sp.dma_start(ctxr[:, :].rearrange("p (k t) -> p k t", k=KT),
                     dram["ctxT"].rearrange("(k p) t -> p k t", p=P)).then_inc(S("ctx_loaded"), 16)
        for c in range(NCHUNK):
            if c >= 4:
                sp.wait_ge(S("mod_used"), c - 3)
            sp.dma_start(modw[:, (c % 4) * 4096:(c % 4 + 1) * 4096],
                         dram["w_mod"][c * P:(c + 1) * P, :]).then_inc(S(f"mod_loaded{c % 4}"), 16)
        for s, (name, times, widths) in enumerate(STREAMS):
            total = sum(widths)
            with sp.Fori(0, times) as i:
                at = 0
                for j, w in enumerate(widths):
                    n = first[name] + j + i * len(widths)
                    sp.wait_ge(S("w_split"), n + 1)
                    sp.dma_start(wst[j % 2][:, 0:w],
                                 dram[name][bass.ds(i * P, P), at:at + w]).then_inc(S(f"w_loaded{j % 2}"), 16)
                    at += w
        sp.wait_ge(S("out_stored"), 16 * KT)

    @block.gpsimd
    def _(pool):
        pool.sem_inc(S("w_split"), 2)
        pool.memset(tri[:, :], 0.0).then_inc(S("tri"), 1)
        pool.memset(idb[:, :], 0.0).then_inc(S("tri"), 1)
        pool.wait_ge(S("tri"), 2)
        pool.affine_select(out=tri[:, :], in_=tri[:, :], compare_op=ALU.is_ge, fill=-1e30, base=0,
                           pattern=[[-1, P]], channel_multiplier=1).then_inc(S("tri"), 1)
        pool.affine_select(out=idb[:, :], in_=idb[:, :], compare_op=ALU.not_equal, fill=1.0, base=0,
                           pattern=[[-1, P]], channel_multiplier=1).then_inc(S("tri"), 1)
        for name, times, widths in STREAMS:
            gla = name == "w_gla_in"
            with pool.Fori(0, times) as i:
                for j, w in enumerate(widths):
                    n = first[name] + j + i * len(widths)
                    if gla and j == 4:
                        pool.wait_ge(S("g_att"), i + 1)
                        for q in range(2):
                            pool.sem_inc(S("pool_begun"), 1)
                            a = att[64 * q:64 * q + 64, :].rearrange("p (b c) -> p b c", b=8)[:, :, 64 * q:64 * q + 64]
                            pool.affine_select(out=a, in_=a, compare_op=ALU.is_ge, fill=0.0, base=0,
                                               pattern=[[0, 8], [1, 64]], channel_multiplier=-1)\
                                .then_inc(S("g_causal"), 1)
                            pool.wait_ge(S("g_causal"), 2 * i + q + 1)
                    pool.wait_ge(S(f"w_loaded{j % 2}"), (first[name] // 2 + j // 2 + 1) * 16 + i * (len(widths) * 8))
                    pool.wait_ge(S("w_used"), n + 1)
                    pool.sem_inc(S("pool_begun"), 1)
                    pool.tensor_copy(wh[j % 2][:, 0:w], wst[j % 2][:, 0:w]).then_inc(S("w_high"), 1)
                    pool.wait_ge(S("w_high"), n + 1)
                    pool.tensor_tensor(wl[j % 2][:, 0:w], wst[j % 2][:, 0:w], wh[j % 2][:, 0:w].bitcast(F32),
                                       ALU.subtract).then_inc(S("w_split"), 1)

    @block.tensor
    def _(pe):
        def three(out_, pairs, cols):
            n = len(pairs)
            for k, (ah, al, bh, bl) in enumerate(pairs):
                pe.matmul(out_, ah, bh[:, cols] if cols else bh, start=(k == 0), stop=False)
                pe.matmul(out_, ah, bl[:, cols] if cols else bl, start=False, stop=False)
                last = pe.matmul(out_, al, bh[:, cols] if cols else bh, start=False, stop=(k == n - 1))
            return last

        def wtile(s, kts=8, off=0):
            return [(wh[s][:, off + 128 * k:off + 128 * k + 128], wl[s][:, off + 128 * k:off + 128 * k + 128])
                    for k in range(kts)]

        def project(s, dst, hi, lo, kts=8, off=0, kt0=0, ready=None, chunks=None, start=True, stop=True,
                    ks=None):
            for k in ks or range(kts):
                w1, w2 = wtile(s, kts, off)[k]
                if ready:
                    ready(k)
                for c0, cn, o in chunks or [(0, HALF, dst[:, 0:HALF]), (HALF, HALF, dst[:, HALF:2 * HALF])]:
                    src = o[1:] if isinstance(o, tuple) else (hi, lo)
                    o = o[0] if isinstance(o, tuple) else o
                    stride = T if len(o.shape) and src[0] is not hc_hi else C
                    x1 = src[0][:, (kt0 + k) * stride + c0:(kt0 + k) * stride + c0 + cn]
                    x2 = src[1][:, (kt0 + k) * stride + c0:(kt0 + k) * stride + c0 + cn]
                    pe.matmul(o, w1, x1, start=start and k == 0, stop=False)
                    pe.matmul(o, w1, x2, start=False, stop=False)
                    last = pe.matmul(o, w2, x1, start=False, stop=stop and k == kts - 1)
            return last

        def take(name, i, j):
            per = len(next(w for nm, _, w in STREAMS if nm == name))
            pe.wait_ge(S("w_split"), first[name] + j + 3 + i * per)

        pe.wait_ge(S("vec_loaded"), 16)

        def stats(r, sums=xs_):
            pe.wait_ge(S("sq_ready"), r + 1)
            for b in range(2):
                last = pe.matmul(bank(6 + b), ones, sums[:, b * HALF:(b + 1) * HALF], start=True, stop=True)
            last.then_inc(S("stats"), 1)

        def hready(r):
            return lambda k: pe.wait_ge(S("h_ready"), 8 * r + k + 1)

        pe.sem_inc(S("w_used"), 2)
        stats(0, sq0)
        pe.wait_ge(S("cx_sq"), 1)
        pe.matmul(bank(5, 0, C), ones, cx_rs[:, :], start=True, stop=True).then_inc(S("cx_stats"), 1)
        pe.wait_ge(S("silc"), 1)
        for c in range(NCHUNK):
            pe.wait_ge(S(f"mod_loaded{c % 4}"), 16 * (c // 4 + 1))
            for q in range(4):
                m = 4 * c + q
                layer, m = divmod(m, 24)
                for k in range(KT):
                    at = (c % 4) * 4096 + q * 1024 + k * P
                    last = pe.matmul(bank(layer, 2 * m, 2 * m + 2), modw[:, at:at + P],
                                     silc[:, 2 * k:2 * k + 2], start=(k == 0), stop=(k == KT - 1))
            last.then_inc(S("mod_used"), 1)
        pe.wait_ge(S("mod_used"), NCHUNK)
        end(pe)

        def even_head(i, q):
            h = 2 * i + q
            j = 6 * q
            nm = "w_even_in"
            evac = lambda n: pe.wait_ge(S("e_evac"), 8 * h + n)
            used = lambda ins: ins.then_inc(S("w_used"), 1)
            full = lambda dst, c: [(0, HALF, dst[:, 0:HALF]), (HALF, HALF, dst[:, HALF:2 * HALF])] + \
                ([(0, C, (c, hc_hi, hc_lo))] if c is not None else [])
            evac(6)
            take(nm, i, j)
            used(project(j % 2, slot(0), h_hi, h_lo, chunks=full(slot(0), bank(6, 0, C)),
                         ready=lambda k: pe.wait_ge(S("h_ready"), k + 1)))
            evac(7)
            take(nm, i, j + 1)
            used(project((j + 1) % 2, slot(1), h_hi, h_lo))
            evac(8)
            take(nm, i, j + 2)
            used(project(j % 2, slot(2), h_hi, h_lo))
            take(nm, i, j + 3)
            pe.wait_ge(S("e_ul"), h + 1)
            for g, (sl, b, wait) in enumerate([(0, 7, lambda: evac(9)), (1, 6, lambda: pe.wait_ge(S("e_va"), h + 1)),
                                               (2, 7, lambda: evac(11)), (0, 6, lambda: evac(12))]):
                wait()
                w1 = wh[(j + 3) % 2][:, g * P:(g + 1) * P]
                w2 = wl[(j + 3) % 2][:, g * P:(g + 1) * P]
                for o, c0, cn in ((slot(sl)[:, 0:HALF], 0, HALF), (slot(sl)[:, HALF:T], HALF, HALF), (bank(b, 0, C), T, C)):
                    pe.matmul(o, w1, u_hi[:, c0:c0 + cn], start=True, stop=False)
                    pe.matmul(o, w1, u_lo[:, c0:c0 + cn], start=False, stop=False)
                    last = pe.matmul(o, w2, u_hi[:, c0:c0 + cn], start=False, stop=True)
                if g < 3:
                    last.then_inc(S("e_gate"), 1)
            used(last)
            take(nm, i, j + 4)
            evac(12)
            used(project(j % 2, slot(1), h_hi, h_lo))
            take(nm, i, j + 5)
            evac(13)
            used(project((j + 1) % 2, slot(2), h_hi, h_lo))

        begin(pe, "even_in")
        with pe.Fori(0, 4) as i:
            even_head(i, 0)
            even_head(i, 1)
        pe.wait_ge(S("w_used"), first["w_even_out"] + 2)
        end(pe)

        begin(pe, "even_out")
        for k in range(KT):
            for b in range(2):
                last = pe.matmul(bank(6 + b), ones, uc[:, k * T + b * HALF:k * T + (b + 1) * HALF],
                                 start=(k == 0), stop=(k == KT - 1))
        last.then_inc(S("ln_sum"), 1)

        def out_pair(nm, i, parts, ring, tiles):
            for q in range(2):
                pe.wait_ge(S(ring), 8 * out_pair.call[nm] + 2 * i + q + 1)
            j = 0
            for p_, (hi, lo, ready) in enumerate(parts):
                for q in range(2):
                    take(nm, i, j)
                    project(j % 2, slot(q), hi, lo, ready=ready if q == 0 else None, start=(p_ == 0),
                            stop=(p_ == len(parts) - 1)).then_inc(S("w_used"), 1)
                    j += 1

        out_pair.call = {"w_even_out": 0, "w_odd_out_a": 1, "w_odd_out_b": 2, "w_gla_out": 3, "w_fox_out": 4}
        for k in range(KT):
            pe.wait_ge(S("ln_sq"), k + 1)
            for b in range(2):
                last = pe.matmul(bank(6 + b), ones, tmp[k % 2][:, b * HALF:(b + 1) * HALF],
                                 start=(k == 0), stop=(k == KT - 1))
            last.then_inc(S("ln_var"), 1)
        with pe.Fori(0, 4) as i:
            out_pair("w_even_out", i, [(h_hi, h_lo, lambda k: pe.wait_ge(S("yb_loaded"), 32)),
                                       (y_hi, y_lo, lambda k: pe.wait_ge(S("ya_ready"), k + 1))], "x_added", 4)
        pe.wait_ge(S("w_used"), first["w_odd_in_a"] + 2)
        stats(1)
        end(pe)

        def odd_groups(part):
            nm = "w_odd_in_" + "ab"[part]

            def group(i):
                g = 2 * part + i
                act = lambda n: pe.wait_ge(S("o_act"), 8 * g + n)
                yev = lambda n: pe.wait_ge(S("o_y"), 4 * g + n)
                for j in range(4):
                    (act, yev)[j % 2](7 + j // 2 if j % 2 == 0 else 3 + j // 2)
                    take(nm, i, j)
                    project(j % 2, slot(j), h_hi, h_lo, ready=hready(1) if j == 0 and part == 0 else None)\
                        .then_inc(S("w_used"), 1)
                for j in range(4):
                    a, b = 2 * j % 4, (2 * j + 1) % 4
                    act((9, 11, 13, 14)[j])
                    take(nm, i, 4 + 2 * j)
                    project(0, slot(a), h_hi, h_lo).then_inc(S("w_used"), 1)
                    act(10) if j == 0 else act(12) if j == 1 else yev(3 + j)
                    take(nm, i, 5 + 2 * j)
                    if j == 0:
                        pe.wait_ge(S("o_d"), 4 * g + 4)
                    project(1, slot(b), d_hi, d_lo, kts=4).then_inc(S("w_used"), 1)
            with pe.Fori(0, 2) as i:
                group(i)
            pe.wait_ge(S("w_used"), first["w_odd_out_" + "ab"[part]] + 2)
            end(pe)

        def out_phase(nm, ready, stat, after, operand=(y_hi, y_lo)):
            with pe.Fori(0, 4) as i:
                out_pair(nm, i, [(*operand, ready)], "x_added", 2)
            pe.wait_ge(S("w_used"), first[after] + 2)
            if stat is not None:
                stats(stat)
            end(pe)

        begin(pe, "odd_a")
        odd_groups(0)
        begin(pe, "oout_a")
        out_phase("w_odd_out_a", None, None, "w_odd_in_b")
        begin(pe, "odd_b")
        odd_groups(1)
        begin(pe, "oout_b")
        out_phase("w_odd_out_b", None, 2, "w_gla_rank")
        begin(pe, "final1")
        stats(3)
        end(pe)

        begin(pe, "gla")
        for j in range(2):
            take("w_gla_rank", 0, j)
            project(j, slot(0), h_hi, h_lo, kts=4, kt0=4 * j, ready=lambda k, j=j: hready(2)(4 * j + k),
                    start=(j == 0), stop=(j == 1)).then_inc(S("w_used"), 1)

        def transposed(s, dst, blocks=range(8)):
            for blk in blocks:
                for k in range(KT):
                    w1, w2 = wtile(s)[k]
                    x1 = h_hi[:, k * T + blk * P:k * T + (blk + 1) * P]
                    x2 = h_lo[:, k * T + blk * P:k * T + (blk + 1) * P]
                    o = dst[:, blk * P:(blk + 1) * P]
                    pe.matmul(o, x1, w1, start=(k == 0), stop=False)
                    pe.matmul(o, x1, w2, start=False, stop=False)
                    last = pe.matmul(o, x2, w1, start=False, stop=(k == KT - 1))
            return last

        def gla_head(i):
            nm = "w_gla_in"
            pe.wait_ge(S("g_alr"), 1)
            pe.wait_ge(S("g_go"), i + 1)
            pe.wait_ge(S("a2_loaded"), 16 * i + 16)
            for b in range(2):
                last = pe.matmul(bank(6 + b), a2s[0:16, :],
                                 alr[0:16, b * HALF:(b + 1) * HALF], start=True, stop=True)
            last.then_inc(S("g_lg"), 1)
            for j in range(2):
                take(nm, i, j)
                project(j, slot(j), h_hi, h_lo).then_inc(S("w_used"), 1)
            take(nm, i, 2)
            transposed(0, slot(2)).then_inc(S("w_used"), 1)
            take(nm, i, 3)
            pe.wait_ge(S("g_ab"), i + 1)
            transposed(1, slot(3)).then_inc(S("w_used"), 1)
            pe.wait_ge(S("g_kdec"), i + 1)
            for b in range(8):
                last = pe.matmul(slot(0)[:, b * P:(b + 1) * P], kin[:, b * P:(b + 1) * P],
                                 qin[:, b * P:(b + 1) * P], start=True, stop=True)
            last.then_inc(S("g_pe"), 1)
            for b in range(8):
                last = pe.transpose(slot(1)[:, b * P:(b + 1) * P], kdec[:, b * P:(b + 1) * P], ident)
            last.then_inc(S("g_pe"), 1)
            pe.wait_ge(S("g_kdt"), i + 1)
            for r in range(4):
                if r >= 2:
                    pe.wait_ge(S("g_st"), 16 * i + 4 * (r - 1) + 1)
                for c in range(4):
                    n = 4 * r + c
                    lo = 64 * (n % 2)
                    last = pe.matmul(kv_at(n), kdt[lo:lo + 64, (n // 2) * P:(n // 2 + 1) * P],
                                     vt[lo:lo + 64, (n // 2) * DV:(n // 2 + 1) * DV], start=True, stop=True)
                last.then_inc(S("g_kv"), 1)
                if r == 0:
                    pe.wait_ge(S("g_causal"), 2 * i + 2)
                    pe.wait_ge(S("g_kdt"), i + 1)
                if r in (1, 3):
                    for b in range(4 * (r // 2), 4 * (r // 2) + 4):
                        pe.wait_ge(S("g_st"), 16 * i + 2 * b + 2)
                        for v in range(2):
                            o = slot(v)[:, b * P:(b + 1) * P]
                            pe.matmul(o, vt[:, b * DV + v * P:b * DV + (v + 1) * P], att[:, b * P:(b + 1) * P],
                                      start=True, stop=False)
                            for c in range(2):
                                n = 2 * b + c
                                if n == 0:
                                    continue
                                last = pe.matmul(slot(v)[:, b * P + c * 64:b * P + c * 64 + 64],
                                                 st[:, (n % 8) * DV + v * P:(n % 8) * DV + (v + 1) * P],
                                                 qin[:, b * P + c * 64:b * P + c * 64 + 64], start=False, stop=(c == 1))
                        last.then_inc(S("g_o"), 1)
            pe.wait_ge(S("g_st"), 16 * i + 16)
            take(nm, i, 4)
            project(0, slot(2), h_hi, h_lo).then_inc(S("w_used"), 1)
            pe.wait_ge(S("g_sq"), i + 1)
            for b in range(2):
                for v in range(2):
                    last = pe.matmul(bank(6 + b), ones, osq[:, v * T + b * HALF:v * T + (b + 1) * HALF],
                                     start=(v == 0), stop=(v == 1))
            last.then_inc(S("g_ss"), 1)
            take(nm, i, 5)
            pe.wait_ge(S("g_g0"), i + 1)
            project(1, slot(2), h_hi, h_lo).then_inc(S("w_used"), 1)

        with pe.Fori(0, 4) as i:
            gla_head(i)
        pe.wait_ge(S("w_used"), first["w_gla_out"] + 2)
        end(pe)
        begin(pe, "gout")
        out_phase("w_gla_out", None, 4, "w_ple_0")

        def ple(r):
            nm = f"w_ple_{r}"

            def two(i):
                for q in range(2):
                    m = 2 * i + q
                    pe.wait_ge(S("p_added"), 8 * r + m + 1)
                    pe.wait_ge(S("p_split"), r + 1)
                    with_round(nm, m, 0)
                    project(0, slot(2 * q), p_hi, p_lo, kts=2).then_inc(S("w_used"), 1)
                    with_round(nm, m, 1)
                    project(1, slot(2 * q + 1), h_hi, h_lo, ready=hready(3 + 2 * r)).then_inc(S("w_used"), 1)

            def with_round(nm, m, j):
                pe.wait_ge(S("w_split"), first[nm] + j + 3 + m * 2)
            with pe.Fori(0, 4) as i:
                two(i)
            pe.wait_ge(S("w_used"), (first["w_fox_gate"] if r == 0 else TILES) + 2)
            stats(5 + 2 * r)
            end(pe)

        begin(pe, "ple0")
        ple(0)

        begin(pe, "fox")
        pe.wait_ge(S("tri"), 4)
        for j in range(2):
            take("w_fox_gate", 0, j)
            project(j, slot(0), h_hi, h_lo, kts=4, kt0=4 * j, ready=lambda k, j=j: hready(4)(4 * j + k),
                    start=(j == 0), stop=(j == 1)).then_inc(S("w_used"), 1)
        pe.wait_ge(S("f_negc"), 1)

        def share(n, parts, at):
            return {at + k: range(k * n // parts, (k + 1) * n // parts) for k in range(parts)}

        Q_AT, K_AT, V_AT, G_AT = share(8, 6, 0), share(8, 5, 9), share(8, 5, 17), share(8, 6, 24)

        def project_pair(p, it, half, first_pair=False):
            nm, n = "w_fox_in", 2 * it + half

            def tile_part(j, at, free):
                if n == min(at):
                    free()
                    take(nm, p, j)
                for k in at[n]:
                    last = project(j % 2, slot(3), h_hi, h_lo, ks=(k,))
                if n == max(at):
                    last.then_inc(S("w_used"), 1)
            if n in Q_AT:
                tile_part(0, Q_AT, lambda: None if first_pair else pe.wait_ge(S("f_g"), p))
            if n in K_AT:
                tile_part(1, K_AT, lambda: pe.wait_ge(S("f_nrm"), 2 * p + 1))
            if n in G_AT:
                tile_part(3, G_AT, lambda: pe.wait_ge(S("f_vl"), p + 1))
            if n in (7, 15):
                j = (n - 7) // 8
                pe.wait_ge(S("f_sq"), 2 * p + j + 1)
                b = pair_buf_of(project_pair.par)[("qh_f", "kh_f")[j]]
                for c in range(2):
                    last = pe.matmul(bank(6 + c), heads, b[:, c * HALF:(c + 1) * HALF], start=True, stop=True)
                last.then_inc(S("f_ss"), 1)
            if n in V_AT:
                if n == min(V_AT):
                    pe.wait_ge(S("f_nrm"), 2 * p + 2)
                    take(nm, p, 2)
                for blk in V_AT[n]:
                    last = transposed(0, slot(3), (blk,))
                if n == max(V_AT):
                    last.then_inc(S("w_used"), 1)

        def pair_buf_of(par):
            return pair_buf[par]

        def scores(p, par, s):
            B, (hh, t) = pair_buf[par], STEPS[s]
            rows = slice(64 * hh, 64 * hh + 64)
            if s == 0:
                pe.wait_ge(S("f_low"), 2 * p + 2)
            for q in UNITS_OF[s]:
                _, lo, hi = UNITS[q]
                pe.wait_ge(S("f_max"), NU * p + q + 1)
                o = bank(q % 3, 0, (hi - lo) * P)
                a, b = slice(t * P, (t + 1) * P), slice(lo * P, hi * P)
                pe.matmul(o, B["qh"][rows, a], B["kh"][rows, b], start=True, stop=False)
                pe.matmul(o, B["qh"][rows, a], B["kl"][rows, b], start=False, stop=False)
                last = pe.matmul(o, B["ql"][rows, a], B["kh"][rows, b], start=False, stop=hi <= t)
                if hi == t + 1:
                    last = pe.matmul(bank(q % 3, (hi - lo - 1) * P, (hi - lo) * P), idb[:, :], tri[:, :],
                                     start=False, stop=True)
                last.then_inc(S("f_qk"), 1)

        def turn(p, s):
            pe.wait_ge(S("f_prob"), 16 * p + s + 1)
            for q in UNITS_OF[s]:
                _, lo, hi = UNITS[q]
                pe.wait_ge(S("f_pt"), NU * p + q + 1)
                for b in range(lo, hi):
                    last = pe.transpose(bank(3 + q % 2, (b - lo) * P, (b - lo + 1) * P),
                                        lg[s % 2][:, b * P:(b + 1) * P], ident)
                last.then_inc(S("f_t"), 1)

        def values(p, par, s):
            B, (hh, t) = pair_buf[par], STEPS[s]
            if s == 0:
                pe.wait_ge(S("f_vl"), p + 1)
            if s % 4 == 0:
                pe.wait_ge(S("f_y"), 4 * p + s // 4 + 1)
            for q in UNITS_OF[s]:
                _, lo, hi = UNITS[q]
                pe.wait_ge(S("f_pt"), NU * p + q + 3)
                o = bank(5, (t % 4) * P, (t % 4 + 1) * P)
                for b in range(lo, hi):
                    c, d = slice(b * P, (b + 1) * P), slice((b - lo) * P, (b - lo + 1) * P)
                    pe.matmul(o, B["vh"][:, c], pth[q % 4][:, d], start=(b == 0), stop=False)
                    pe.matmul(o, B["vl"][:, c], pth[q % 4][:, d], start=False, stop=False)
                    last = pe.matmul(o, B["vh"][:, c], ptl[q % 4][:, d], start=False, stop=(b == t))
                last.then_inc(S("f_pv"), 1)

        def attend(p, par, s, scored=True, project_next=True):
            c, cpar, cs = step_of(p, par, s)
            project_pair.par = 1 - cpar
            if project_next:
                project_pair(c + 1, cs, 0)
            turn(c, cs)
            if scored:
                scores(*step_of(p, par, s + 2))
            if project_next:
                project_pair(c + 1, cs, 1)
            if s:
                values(*step_of(p, par, s - 1))

        pe.sem_inc(S("f_t"), 3)
        pe.sem_inc(S("f_pv"), 4)
        project_pair.par = 0
        for it in range(16):
            for half in range(2):
                project_pair(0, it, half, first_pair=True)
        scores(0, 0, 0)
        scores(0, 0, 1)
        for s in range(2):
            attend(0, 0, s)

        def rest_and_first(p, par, last_next=True):
            for s in range(2, 18):
                attend(p, par, s, project_next=last_next or s < 16)
        with pe.Fori(0, 3) as i:
            rest_and_first(2 * i, 0)
            rest_and_first(2 * i + 1, 1)
        rest_and_first(6, 0, last_next=False)
        for s in range(2, 16):
            attend(7, 1, s, scored=s < 14, project_next=False)
        values(7, 1, 15)
        pe.wait_ge(S("f_pv"), 8 * NU + 4)
        end(pe)
        begin(pe, "fout")
        out_phase("w_fox_out", lambda k: pe.wait_ge(S("yf_ready"), k + 1), 6, "w_ple_1", (h_hi, h_lo))
        begin(pe, "ple1")
        ple(1)
        begin(pe, "end")

    @block.scalar
    def _(act):
        line = Line(act, S("act_line"))
        A = act.activation

        def rsqrt(dst, src, n, eps):
            line(A(dst, src, ACT.Ln, bias=eps[:, 0:1], scale=1.0 / n))
            return A(dst, dst, ACT.Exp, scale=-0.5)

        def high(r):
            act.wait_ge(S("stats"), r["stat"] + 1)
            rsqrt(xs_[:, :], slot(3), D, eps6).then_inc(S("rs"), 1)
            if r.get("op") is None:
                return
            for k in range(KT):
                t = tmp[k % r["bufs"]]
                act.wait_ge(S("n_scaled"), 8 * r["op"] + k + 1)
                A(col(h_hi, k), t[:, :], ACT.Copy).then_inc(S("n_high"), 1)

        act.wait_ge(S("vec_loaded"), 16)
        act.wait_ge(S("consts"), 1)
        A(silc[:, :], V("c", 0, 16), ACT.Silu).then_inc(S("silc"), 1)
        for k in range(KT):
            act.wait_ge(S("x_loaded"), 16)
            if k >= 2:
                act.wait_ge(S("x_sq_used"), k - 1)
            A(squares[:, (k % 2) * T:(k % 2 + 1) * T], col(xr, k), ACT.Square).then_inc(S("x_sq"), 1)
        act.wait_ge(S("ctx_loaded"), 16)
        for k in range(KT):
            A(squares[:, (2 + k) * T:(2 + k) * T + C], ctxr[:, k * C:(k + 1) * C], ACT.Square).then_inc(S("c_sq"), 1)
        line(A(lt[0][:, :], V("lam", 0, 16), ACT.Abs))
        A(lt[0][:, :], lt[0][:, :], ACT.Exp, scale=-1.0).then_inc(S("lam_exp"), 1)
        act.wait_ge(S("stats"), 1)
        rsqrt(sq0[:, :], slot(3), D, eps6).then_inc(S("rs"), 1)
        act.wait_ge(S("cx_stats"), 1)
        rsqrt(cx_rs[:, :], bank(5, 0, C), D, eps6).then_inc(S("cx_rs"), 1)
        for k in range(KT):
            act.wait_ge(S("n_scaled"), k + 1)
            A(col(h_hi, k), n_tmp[:, :], ACT.Copy).then_inc(S("n_high"), 1)
        act.wait_ge(S("c_scaled"), 1)
        A(hc_hi[:, :], ctxr[:, :], ACT.Copy).then_inc(S("c_high"), 1)
        act.wait_ge(S("c_high"), 1)
        end(act)

        begin(act, "even_in")
        act.sem_inc(S("e_evac"), 8)
        act.sem_inc(S("ga_stored"), 16)

        def even_head(h):
            w0 = first["w_even_in"] + 2
            wu = lambda n: act.wait_ge(S("w_used"), w0 + n + 6 * h)
            ev = lambda ins: ins.then_inc(S("e_evac"), 1)
            wu(1)
            act.wait_ge(S("e_u"), h + 1)
            A(xbp[:, XB0:XB0 + T], slot(0), ACT.Copy)
            ev(A(xbp[:, XBC:XBC + C], bank(6, 0, C), ACT.Copy))
            wu(3)
            act.wait_ge(S("ga_stored"), 16 * h + 16)
            ev(A(sg[:, :], slot(2), ACT.Sigmoid))
            store_yb(h)
            act.wait_ge(S("e_u"), h + 2)
            act.wait_ge(S("yb_stored"), 32 * h + 32)
            A(u_hi[:, :], u[:, :], ACT.Copy).then_inc(S("e_uh"), 1)
            act.wait_ge(S("e_lru"), h + 1)
            for g in range(4):
                d = g // 2
                if g < 3:
                    act.wait_ge(S("e_gate"), 3 * h + g + 1)
                else:
                    wu(4)
                buf, bias = (ra, ii)[g % 2][d], V(("b_r", "b_i")[g % 2], 8 * d + h)
                sl, b = ((0, 7), (1, 6), (2, 7), (0, 6))[g]
                A(buf[:, 0:T], slot(sl), ACT.Sigmoid, bias=bias)
                ev(A(buf[:, T:TC], bank(b, 0, C), ACT.Sigmoid, bias=bias))
            act.wait_ge(S("e_evac"), 8 * h + 14)
            for d in range(2):
                line.go(A(tt[d][:, :], ra[d][:, :], ACT.Tanh, scale=sp8[:, bass.ds(8 * d + h, 1)]))
            line.sync()
            for d in range(2):
                line(A(ra[d][:, :], ra[d][:, :], ACT.Exp, scale=nsp8[:, bass.ds(8 * d + h, 1)]))
                if d == 1:
                    act.wait_ge(S("e_q"), 2 * h + 1)
                A(a2[:, :], ra[d][:, :], ACT.Square).then_inc(S("e_a2"), 1)
            for d in range(2):
                act.wait_ge(S("e_q"), 2 * h + d + 1)
                A(tt[d][:, :], tt[d][:, :], ACT.Sqrt).then_inc(S("e_sqrt"), 1)
            wu(5)
            ev(A(gb[:, :], slot(1), ACT.Silu))
            wu(6)
            act.wait_ge(S("e_va"), h + 1)
            ev(A(sg[:, :], slot(2), ACT.Silu))
            act.wait_ge(S("e_evac"), 8 * h + 16)
            act.dma_start(tile(ga_d, h), sg[:, :]).then_inc(S("ga_stored"), 16)

        def store_yb(h):
            act.wait_ge(S("e_lru"), h + 1)
            act.dma_start(tile(yb_hi_d, h), yb_hi[:, :].bitcast(F32)).then_inc(S("yb_stored"), 16)
            act.dma_start(tile(yb_lo_d, h), yb_lo[:, :].bitcast(F32)).then_inc(S("yb_stored"), 16)

        line.repeat(8, 4, even_head)
        store_yb(8)
        act.wait_ge(S("yb_stored"), 32 * 9)
        act.wait_ge(S("ga_stored"), 16 * 9)
        end(act)

        begin(act, "even_out")
        act.dma_start(h_hi[:, :].bitcast(F32).rearrange("p (k t) -> p k t", k=KT),
                      yb_hi_d[P:9 * P, :].rearrange("(k p) t -> p k t", p=P)).then_inc(S("yb_loaded"), 16)
        act.dma_start(h_lo[:, :].bitcast(F32).rearrange("p (k t) -> p k t", k=KT),
                      yb_lo_d[P:9 * P, :].rearrange("(k p) t -> p k t", p=P)).then_inc(S("yb_loaded"), 16)
        for k in range(KT):
            act.wait_ge(S("ln_centered"), k + 1)
            if k >= 2:
                act.wait_ge(S("ln_var"), k - 1)
            A(tmp[k % 2][:, :], col(uc, k), ACT.Square).then_inc(S("ln_sq"), 1)
        act.wait_ge(S("ln_var"), 8)
        for k in range(2):
            act.dma_start(tmp[k][:, :], tile(ga_d, k)).then_inc(S(f"ga_loaded{k}"), 16)
        rsqrt(xs_[:, :], slot(3), D, eps5).then_inc(S("ln_rs"), 1)
        for k in range(KT):
            act.wait_ge(S("ln_scaled"), k + 1)
            A(col(uc, k), col(uc, k), ACT.Silu, bias=V("ln_b", k), scale=V("ln_g", k)).then_inc(S("ln_silu"), 1)
            act.wait_ge(S("ya_gated"), k + 1)
            A(col(y_hi, k), col(uc, k), ACT.Copy).then_inc(S("ya_high"), 1)
            if k + 2 < KT:
                act.dma_start(tmp[k % 2][:, :], tile(ga_d, k + 2)).then_inc(S(f"ga_loaded{k % 2}"), 16)
            act.wait_ge(S("ya_ready"), k + 1)
            act.dma_start(col(xr, k), tile(dram["xT"], k)).then_inc(S("x_in"), 16)
        def stored(m):
            act.wait_ge(S("x_new"), m + 1)
            act.dma_start(tile(x_d, m), col(xr, m)).then_inc(S("x_stored"), 16)
        with act.Fori(0, KT) as m:
            stored(m)
        high({"stat": 1, "op": 1, "bufs": 3})
        act.wait_ge(S("n_high"), 16)
        act.wait_ge(S("x_stored"), 16 * 8)
        end(act)

        def odd_groups(part):
            nm = "w_odd_in_" + "ab"[part]

            def group(i):
                g = 2 * part + i
                w0 = first[nm] + 2
                ev = lambda ins: ins.then_inc(S("o_act"), 1)
                for j in range(4):
                    act.wait_ge(S("w_used"), w0 + j + 1 + i * 12)
                    for b in range(2):
                        act.wait_ge(S("o_up"), 8 * g + 2 * j + b + 1)
                        ins = A(up[:, :].rearrange("p (r c) -> p r c", c=80)[:, :, 8:72],
                                bank(2 * j + b).rearrange("p (r c) -> p r c", c=64), ACT.Copy)
                        ins.then_inc(S("o_u"), 1)
                    act.wait_ge(S("o_u"), 8 * g + 2 * j + 2)
                    act.sem_inc(S("o_act"), 1)
                for j in range(4):
                    act.wait_ge(S("w_used"), w0 + 5 + 2 * j + i * 12)
                    act.wait_ge(S("o_gs"), 4 * g + j + 1)
                    ev(A(gs[j % 2][:, :], slot(2 * j % 4), ACT.Silu))
            with act.Fori(0, 2) as i:
                group(i)
            act.wait_ge(S("o_act"), 16 * part + 24)
            end(act)

        def out_load(src):
            for k in range(KT):
                act.dma_start(col(xr, k), tile(src, k)).then_inc(S("x_in"), 16)

        begin(act, "odd_a")
        act.sem_inc(S("o_act"), 8)
        odd_groups(0)

        def out_phase(r, name, spec=None, store=True, before=None):
            begin(act, name)
            if before:
                before()
            out_load(x_d)
            if store:
                n0 = 8 * out_phase.stores

                def stored(m):
                    act.wait_ge(S("x_new"), 8 * r + m + 1)
                    act.dma_start(tile(x_d, m), col(xr, m)).then_inc(S("x_stored"), 16)
                with act.Fori(0, KT) as m:
                    stored(m)
                out_phase.stores += 1
                act.wait_ge(S("x_stored"), 16 * 8 * out_phase.stores)
            if spec:
                high(spec)
            end(act)
        out_phase.stores = 1

        out_phase(1, "oout_a")
        begin(act, "odd_b")
        odd_groups(1)
        out_phase(2, "oout_b", {"stat": 2}, store=False)
        begin(act, "final1")
        with act.Fori(0, KT) as m:
            act.wait_ge(S("f1_new"), m + 1)
            act.dma_start(tile(x_d, m), col(xr, m)).then_inc(S("x_stored"), 16)
        out_phase.stores += 1
        high({"stat": 3, "op": 2, "bufs": 3})
        act.wait_ge(S("n_high"), 24)
        act.wait_ge(S("x_stored"), 16 * 8 * out_phase.stores)
        end(act)

        begin(act, "gla")
        act.wait_ge(S("w_used"), first["w_gla_in"] + 2)
        A(alr[0:16, :], slot(0)[0:16, :], ACT.Copy).then_inc(S("g_alr"), 1)

        def gla_head(i):
            wu = lambda n: act.wait_ge(S("w_used"), first["w_gla_in"] + 2 + n + 6 * i)
            act.dma_start(a2s[0:16, :], dram["a2"][bass.ds(i * 16, 16), :]).then_inc(S("a2_loaded"), 16)
            act.wait_ge(S("g_min"), i + 1)
            line(A(te[:, :], slot(3), ACT.Abs, bias=V("b_a", i)))
            act.sem_inc(S("g_ab"), 1)
            line(A(te[:, :], te[:, :], ACT.Exp, scale=-1.0))
            A(te[:, :], te[:, :], ACT.Ln, bias=one1[:, 0:1]).then_inc(S("g_te"), 1)
            act.wait_ge(S("g_cum"), i + 1)
            A(te[:, :], cum[:, :], ACT.Exp, scale=1.0 / 16).then_inc(S("g_exp"), 1)
            A(kdec[:, :], cum[:, :], ACT.Exp, scale=-1.0 / 16).then_inc(S("g_exp"), 1)
            A(dec[:, :], cum[:, CH - 1::CH],
              ACT.Exp, scale=1.0 / 16).then_inc(S("g_exp"), 1)
            act.wait_ge(S("g_cl"), i + 1)
            A(kdec[:, :], kdec[:, :], ACT.Exp, scale=1.0 / 16).then_inc(S("g_exp"), 1)
            for v in range(2):
                wu(3 + v)
                A(vt[:, :].rearrange("p (b d) -> p b d", d=DV)[:, :, v * P:(v + 1) * P],
                  slot(2 + v).rearrange("p (b d) -> p b d", d=P), ACT.Copy).then_inc(S("g_v"), 1)
            act.wait_ge(S("g_pe"), 2 * i + 1)
            for q in range(2):
                r = slice(64 * q, 64 * q + 64)
                line.go(A(att[r, :].rearrange("p (b c) -> p b c", b=8)[:, :, 64 * q:64 * q + 64],
                          slot(0)[r, :].rearrange("p (b c) -> p b c", b=8)[:, :, 64 * q:64 * q + 64], ACT.Copy))
            line.sync()
            act.sem_inc(S("g_att"), 1)
            act.wait_ge(S("g_pe"), 2 * i + 2)
            act.wait_ge(S("g_v"), 2 * i + 2)
            A(kdt[:, :], slot(1), ACT.Copy).then_inc(S("g_kdt"), 1)
            act.wait_ge(S("g_o"), 8 * i + 8)
            line(A(osq[:, 0:T], slot(0), ACT.Square))
            A(osq[:, T:2 * T], slot(1), ACT.Square).then_inc(S("g_sq"), 1)
            wu(5)
            act.wait_ge(S("g_kdt"), i + 1)
            A(att[:, :], slot(2), ACT.Silu).then_inc(S("g_g0"), 1)
            act.wait_ge(S("g_ss"), i + 1)
            rsqrt(cum[:, :], slot(3), DV, eps6).then_inc(S("g_rs"), 1)
            wu(6)
            A(kdt[:, :], slot(2), ACT.Silu).then_inc(S("g_g1"), 1)

        line.repeat(4, 6, gla_head)
        act.wait_ge(S("g_g1"), 4)
        end(act)

        def p_load(r, layer):
            act.dma_start(pf[:, :].rearrange("p (k t) -> p k t", k=2),
                          dram["pT"][layer * 2 * P:(layer + 1) * 2 * P, :].rearrange("(k p) t -> p k t", p=P))\
                .then_inc(S("p_loaded"), 16)

        out_phase(3, "gout", {"stat": 4, "op": 3, "bufs": 3}, store=False)

        def ple(r, name):
            begin(act, name)
            p_load(r, r)
            nm = f"w_ple_{r}"

            def two(i):
                for q in range(2):
                    m = 2 * i + q
                    act.wait_ge(S("w_used"), first[nm] + 4 + 2 * m)
                    act.wait_ge(S("p_added"), 8 * r + m + 1)
                    A(tmp[q][:, :], slot(2 * q + 1), ACT.Sigmoid).then_inc(S("p_sig"), 1)
            with act.Fori(0, 4) as i:
                two(i)
            if r == 0:
                with act.Fori(0, KT) as m:
                    act.wait_ge(S("p_new"), m + 1)
                    act.dma_start(tile(x_d, m), col(xr, m)).then_inc(S("x_stored"), 16)
                out_phase.stores += 1
                high({"stat": 5, "op": 4, "bufs": 3})
                act.wait_ge(S("n_high"), 40)
                act.wait_ge(S("x_stored"), 16 * 8 * out_phase.stores)
            else:
                high({"stat": 7})
            end(act)
        ple(0, "ple0")

        begin(act, "fox")
        act.wait_ge(S("f_min"), 1)
        r16 = slice(0, 16)
        line(A(fz[1][r16, :], slot(0)[r16, :], ACT.Abs, bias=vec[0:16, VEC["b_f"][0]:VEC["b_f"][0] + 1]))
        line(A(fz[1][r16, :], fz[1][r16, :], ACT.Exp, scale=-1.0))
        A(fz[1][r16, :], fz[1][r16, :], ACT.Ln, bias=one1[0:16, 0:1]).then_inc(S("f_te"), 1)
        act.wait_ge(S("f_c"), 1)
        act.dma_start(negc_d, fz[2][r16, :]).then_inc(S("f_negc_out"), 16)
        act.wait_ge(S("f_negc_out"), 16)
        act.sem_inc(S("f_negc"), 1)

        def load_c(p, hh):
            act.dma_start(negc[hh][:, :], negc_d[bass.ds(2 * p + hh, 1), :].to_broadcast((P, T)))\
                .then_inc(S(f"f_cin{hh}"), 16)

        def pair_work(p, par, it):
            B = pair_buf[par]
            wu = lambda n: act.wait_ge(S("w_used"), first["w_fox_in"] + 2 + n + 4 * p)
            for j, (raw, sq, high_) in enumerate((("ql_f", "qh_f", "qh"), ("kl_f", "kh_f", "kh"))):
                if it == 3 + 4 * j:
                    wu(1 + j)
                    line(A(B[raw][:, :], slot(3), ACT.Copy))
                    A(B[sq][:, :], B[raw][:, :], ACT.Square).then_inc(S("f_sq"), 1)
                if it == 4 + 4 * j:
                    act.wait_ge(S("f_ss"), 2 * p + j + 1)
                    rsqrt(slot(3), slot(3), FH, eps6).then_inc(S("f_rs"), 1)
                if it == 5 + 4 * j:
                    act.wait_ge(S("f_nrm"), 2 * p + j + 1)
                    A(B[high_][:, :], B[raw][:, :], ACT.Copy).then_inc(S("f_high"), 1)
            if it == 11:
                wu(3)
                A(B["vh"][:, :], slot(3), ACT.Copy).then_inc(S("f_high"), 1)
            if it == 15:
                wu(4)
                A(yf[:, bass.ds(p * T, T)], slot(3), ACT.Silu).then_inc(S("f_g"), 1)

        def expo(p, s):
            n = (STEPS[s][1] + 1) * P
            act.wait_ge(S("f_max"), NU * p + UNITS_OF[s][-1] + 4)
            A(lg[s % 2][:, 0:n], lg[s % 2][:, 0:n], ACT.Exp, bias=nmx[s % 2][:, 0:1], scale=-1.0,
              accum_out=psm[s % 2][:, 0:1]).then_inc(S("f_exp"), 1)

        def pt_high(p, s):
            for q in UNITS_OF[s]:
                n = (UNITS[q][2] - UNITS[q][1]) * P
                act.wait_ge(S("f_t"), NU * p + q + 4)
                act.wait_ge(S("f_pv"), NU * p + q + 1)
                A(pth[q % 4][:, 0:n], bank(3 + q % 2, 0, n), ACT.Copy).then_inc(S("f_ph"), 1)

        def attend(p, par, s, more=True, next_pair=True):
            c, cpar, cs = step_of(p, par, s)
            if more:
                n, _, ns = step_of(p, par, s + 1)
                expo(n, ns)
            if next_pair:
                pair_work(c + 1, 1 - cpar, cs)
            pt_high(c, cs)
            if next_pair and cs in (8, 15):
                act.wait_ge(S("f_max"), NU * c + NU // 2 * (1 + cs // 15) + 3)
                load_c(c + 1, cs // 15)

        for it in range(16):
            pair_work(0, 0, it)
        load_c(0, 0)
        load_c(0, 1)
        expo(0, 0)
        for s in range(2):
            attend(0, 0, s)

        def rest_and_first(p, par, last_next=True):
            for s in range(2, 18):
                attend(p, par, s, next_pair=last_next or s < 16)

        def two_pairs(i):
            rest_and_first(2 * i, 0)
            rest_and_first(2 * i + 1, 1)
        line.repeat(3, 8, two_pairs)
        rest_and_first(6, 0, last_next=False)
        for s in range(2, 16):
            attend(7, 1, s, more=s < 15, next_pair=False)
        act.wait_ge(S("f_ph"), 8 * NU)
        end(act)

        def y_high():
            for k in range(KT):
                A(col(h_hi, k), col(yf, k), ACT.Copy).then_inc(S("yf_high"), 1)
        out_phase(4, "fout", {"stat": 6, "op": 5, "bufs": 3}, store=False, before=y_high)
        ple(1, "ple1")
        begin(act, "end")
        for k in range(KT):
            act.wait_ge(S("out_ready"), k + 1)
            act.dma_start(tile(out, k), col(xr, k)).then_inc(S("out_stored"), 16)
        act.wait_ge(S("out_stored"), 16 * KT)

    @block.vector
    def _(dve):
        line = Line(dve, S("dve_line"))
        TT_, TS, STT = dve.tensor_tensor, dve.tensor_scalar, dve.scalar_tensor_tensor
        for t, v in ((eps6, 1e-6), (eps5, 1e-5), (one1, 1.0)):
            line.go(dve.memset(t[:, :], v))
        line.sync()
        dve.sem_inc(S("consts"), 1)
        dve.wait_ge(S("vec_loaded"), 16)
        line(TS(gq[:, :], V("q_norm"), FH ** -0.5, None, ALU.mult))

        for k in range(KT):
            dve.wait_ge(S("x_sq"), k + 1)
            s = squares[:, (k % 2) * T:(k % 2 + 1) * T]
            if k == 0:
                line.go(dve.tensor_copy(sq0[:, :], s))
            else:
                line.go(TT_(sq0[:, :], sq0[:, :], s, ALU.add))
            line.sync()
            dve.sem_inc(S("x_sq_used"), 1)
        dve.sem_inc(S("sq_ready"), 1)
        dve.wait_ge(S("c_sq"), 8)
        line(TT_(cx_rs[:, :], squares[:, 2 * T:2 * T + C], squares[:, 3 * T:3 * T + C], ALU.add))
        for k in range(2, KT):
            line(TT_(cx_rs[:, :], cx_rs[:, :], squares[:, (2 + k) * T:(2 + k) * T + C], ALU.add))
        dve.sem_inc(S("cx_sq"), 1)
        dve.wait_ge(S("lam_exp"), 1)
        line(TS(lt[1][:, :], lt[0][:, :], 2.0, None, ALU.add))
        line(dve.reciprocal(lt[1][:, :], lt[1][:, :]))
        line(TT_(lt[0][:, :], lt[0][:, :], lt[1][:, :], ALU.mult))
        line(TT_(lt[1][:, :], lt[0][:, :], lt[0][:, :], ALU.mult))
        line(TS(lt[2][:, :], lt[1][:, :], 1 / 17, 1 / 15, ALU.mult, ALU.add))
        for n in (13, 11, 9, 7, 5, 3, 1):
            line(TT_(lt[2][:, :], lt[2][:, :], lt[1][:, :], ALU.mult))
            line(TS(lt[2][:, :], lt[2][:, :], 1 / n, None, ALU.add))
        line(TT_(lt[2][:, :], lt[2][:, :], lt[0][:, :], ALU.mult))
        line(TS(lt[1][:, :], V("lam", 0, 16), -1.0, 0.0, ALU.mult, ALU.max))
        line(STT(out=lt[2][:, :], in0=lt[2][:, :], scalar=2.0, in1=lt[1][:, :], op0=ALU.mult, op1=ALU.add))
        line(TS(sp8[:, :], lt[2][:, :], LRU_C, None, ALU.mult))
        line(TS(nsp8[:, :], lt[2][:, :], -LRU_C, None, ALU.mult))
        mv = modv[:, :].rearrange("p (l m v) -> p l v m", l=2, v=2)

        def mod_layer(layer):
            dve.wait_ge(S("mod_used"), 6 * (layer + 1))
            for v in range(2):
                line(TT_(mv[:, layer, v, :], bank(layer, 0, 48).rearrange("p (m v) -> p v m", v=2)[:, v, :],
                         V("mod_b", 24 * layer, 24), ALU.add))
                line(STT(out=gsc[:, (2 * layer + v) * 8:(2 * layer + v + 1) * 8], in0=mv[:, layer, v, 8:16],
                         scalar=1.0, in1=V("norm_g", 8 * layer, 8), op0=ALU.add, op1=ALU.mult))
        mod_layer(0)

        def mod(layer, v, part, k):
            return modv[:, bass.ds(48 * layer + 2 * (8 * part + k) + v, 1)]

        dve.wait_ge(S("rs"), 1)
        for k in range(KT):
            if k >= 1:
                dve.wait_ge(S("n_high"), k)
                line(TT_(col(h_lo, k - 1), n_tmp[:, :], col(h_hi, k - 1).bitcast(F32), ALU.subtract))
            line(TT_(n_tmp[:, :], col(xr, k), sq0[:, :], ALU.mult))
            TS(n_tmp[:, :], n_tmp[:, :], gsc[:, k:k + 1], mod(0, 0, 0, k), ALU.mult, ALU.add)\
                .then_inc(S("n_scaled"), 1)
        dve.wait_ge(S("n_high"), 8)
        line(TT_(col(h_lo, 7), n_tmp[:, :], col(h_hi, 7).bitcast(F32), ALU.subtract))
        dve.sem_inc(S("h_ready"), 8)
        dve.wait_ge(S("cx_rs"), 1)
        for k in range(KT):
            c = ctxr[:, k * C:(k + 1) * C]
            line(TT_(c, c, cx_rs[:, :], ALU.mult))
            line(TS(c, c, gsc[:, 8 + k:9 + k], mod(0, 1, 0, k), ALU.mult, ALU.add))
        mod_layer(1)
        dve.sem_inc(S("c_scaled"), 1)
        dve.wait_ge(S("c_high"), 1)
        line(TT_(hc_lo[:, :], ctxr[:, :], hc_hi[:, :].bitcast(F32), ALU.subtract))
        end(dve)

        begin(dve, "even_in")
        line.go(dve.memset(xbp[:, :], 0.0))
        line.go(dve.memset(upad[:, :], 0.0))
        line.go(dve.memset(yb_hi[:, :].bitcast(F32), 0.0))
        line.go(dve.memset(yb_lo[:, :].bitcast(F32), 0.0))
        line.sync()
        dve.sem_inc(S("e_u"), 1)
        dve.sem_inc(S("e_lru"), 1)

        def even_head(h):
            dve.wait_ge(S("e_evac"), 8 * h + 9)
            for j in range(4):
                w = V("sconv_w", 8 * j + h)
                for o, n in ((0, T), (T, C)):
                    s = xbp[:, (XB0 if o == 0 else XBC) - 2 + j:(XB0 if o == 0 else XBC) - 2 + j + n]
                    if j >= 1:
                        line.sync(1)
                    if j == 0:
                        line.go(TS(u[:, o:o + n], s, w, V("sconv_b", h), ALU.mult, ALU.add))
                    else:
                        line.go(STT(out=u[:, o:o + n], in0=s, scalar=w, in1=u[:, o:o + n], op0=ALU.mult, op1=ALU.add))
            line.sync()
            dve.sem_inc(S("e_u"), 1)
            dve.wait_ge(S("e_uh"), h + 1)
            TT_(u_lo[:, :], u[:, :], u_hi[:, :].bitcast(F32), ALU.subtract).then_inc(S("e_ul"), 1)
            dve.wait_ge(S("e_evac"), 8 * h + 10)
            TT_(upad[:, PAD:PAD + T], slot(1), sg[:, :], ALU.mult).then_inc(S("e_va"), 1)
            dve.wait_ge(S("e_va"), h + 1)
            for j in range(TAPS):
                o = col(uc, h) if j % 2 == 0 else acc1[:, :]
                s, w = upad[:, j:j + T], V("conv_w", 8 * j + h)
                if j == 0:
                    line.go(TS(o, s, w, V("conv_b", h), ALU.mult, ALU.add))
                elif j == 1:
                    line.go(TS(o, s, w, None, ALU.mult))
                else:
                    line.sync(1)
                    line.go(STT(out=o, in0=s, scalar=w, in1=o, op0=ALU.mult, op1=ALU.add))
            line.sync()
            line.go(TT_(col(uc, h), col(uc, h), acc1[:, :], ALU.add))
            for d in range(2):
                dve.wait_ge(S("e_a2"), 2 * h + d + 1)
                STT(out=tt[d][:, :], in0=a2[:, :], scalar=1.0, in1=tt[d][:, :], op0=ALU.add, op1=ALU.mult)\
                    .then_inc(S("e_q"), 1)
                line.go(TT_(ii[d][:, :], ii[d][:, :], u[:, :], ALU.mult))
            line.sync()
            for d in range(2):
                dve.wait_ge(S("e_sqrt"), 2 * h + d + 1)
                line(TT_(tt[d][:, :], tt[d][:, :], ii[d][:, :], ALU.mult))
                for lo, hi, init in ((T, TC, 0.0), (0, T, ii[d][:, TC - 1:TC] if d == 0 else ii[d][:, T:T + 1])):
                    f = slice(lo, hi) if d == 0 else (slice(hi - 1, lo - 1, -1) if lo else slice(hi - 1, None, -1))
                    line(dve.tensor_tensor_scan(out=ii[d][:, f], data0=ra[d][:, f], data1=tt[d][:, f],
                                                initial=init, op0=ALU.mult, op1=ALU.add))
            line(TT_(tt[0][:, 0:T], ii[0][:, 0:T], ii[1][:, 0:T], ALU.add))
            dve.wait_ge(S("e_evac"), 8 * h + 15)
            line(TT_(tt[0][:, 0:T], tt[0][:, 0:T], gb[:, :], ALU.mult))
            line(dve.tensor_copy(yb_hi[:, :], tt[0][:, 0:T]))
            TT_(yb_lo[:, :], tt[0][:, 0:T], yb_hi[:, :].bitcast(F32), ALU.subtract).then_inc(S("e_lru"), 1)

        line.repeat(8, 8 + TAPS + 1 + 2 + 6 + 3, even_head)
        dve.wait_ge(S("e_lru"), 9)
        line.sync()
        end(dve)

        begin(dve, "even_out")
        dve.sem_inc(S("x_added"), 2)
        dve.wait_ge(S("ln_sum"), 1)
        line(TS(xs_[:, :], slot(3), 1.0 / D, None, ALU.mult))
        for k in range(KT):
            TT_(col(uc, k), col(uc, k), xs_[:, :], ALU.subtract).then_inc(S("ln_centered"), 1)
        dve.wait_ge(S("ln_rs"), 1)

        def scale_ln(k):
            TT_(col(uc, k), col(uc, k), xs_[:, :], ALU.mult).then_inc(S("ln_scaled"), 1)
        scale_ln(0)
        for k in range(KT):
            if k + 1 < KT:
                scale_ln(k + 1)
            dve.wait_ge(S("ln_silu"), k + 1)
            dve.wait_ge(S(f"ga_loaded{k % 2}"), 16 * (k // 2 + 1))
            TT_(col(uc, k), col(uc, k), tmp[k % 2][:, :], ALU.mult).then_inc(S("ya_gated"), 1)
            dve.wait_ge(S("ya_high"), k + 1)
            TT_(col(y_lo, k), col(uc, k), col(y_hi, k).bitcast(F32), ALU.subtract).then_inc(S("ya_ready"), 1)

        def residual(r, gate, name, last):
            if last:
                line(dve.memset(xs_[:, :], 0.0))

            def two(i):
                for q in range(2):
                    m = 2 * i + q
                    w = first[name] + 2 + (4 * i + 3 + q if name == "w_even_out" else 2 * i + q + 1)
                    dve.wait_ge(S("w_used"), w)
                    dve.wait_ge(S("x_in"), 128 * (r + 1))
                    if gate is None:
                        TT_(col(xr, m), slot(q), col(xr, m), ALU.add).then_inc(S("x_added"), 1)
                    else:
                        STT(out=col(xr, m), in0=slot(q), scalar=gate(m), in1=col(xr, m), op0=ALU.mult,
                            op1=ALU.add).then_inc(S("x_added"), 1)
                    dve.wait_ge(S("x_added"), 8 * r + m + 3)
                    dve.sem_inc(S("x_new"), 1)
                    if last:
                        line(TT_(tmp[0][:, :], col(xr, m), col(xr, m), ALU.mult))
                        line(TT_(xs_[:, :], xs_[:, :], tmp[0][:, :], ALU.add))
            line.repeat(4, 4 if last else 0, two)
            if last:
                dve.sem_inc(S("sq_ready"), 1)

        def normalize(stat, op, gain=None, layer=None):
            dve.wait_ge(S("rs"), stat + 1)
            for k in range(KT + 2):
                if k < KT:
                    t = tmp[k % 3]
                    if k >= 3:
                        dve.wait_ge(S("h_ready"), 8 * op + k - 2)
                    if layer is None:
                        STT(out=t[:, :], in0=col(xr, k), scalar=V(gain[0], gain[1] + k), in1=xs_[:, :],
                            op0=ALU.mult, op1=ALU.mult).then_inc(S("n_scaled"), 1)
                    else:
                        line(TT_(t[:, :], col(xr, k), xs_[:, :], ALU.mult))
                        TS(t[:, :], t[:, :], gsc[:, 16 * layer + k:16 * layer + k + 1], mod(layer, 0, 0, k),
                           ALU.mult, ALU.add).then_inc(S("n_scaled"), 1)
                if k >= 1 and k <= KT:
                    dve.wait_ge(S("n_high"), 8 * op + k)
                    TT_(col(h_lo, k - 1), tmp[(k - 1) % 3][:, :], col(h_hi, k - 1).bitcast(F32), ALU.subtract)\
                        .then_inc(S("h_ready"), 1)
            dve.wait_ge(S("h_ready"), 8 * op + 8)

        residual(0, lambda m: mod(0, 0, 2, m), "w_even_out", True)
        normalize(1, 1, layer=1)
        end(dve)

        def odd_groups(part):
            nm = "w_odd_in_" + "ab"[part]
            v3 = lambda t: t[:, :].rearrange("p (r c) -> p r c", c=80)
            for i in range(2):
                g = 2 * part + i
                w0 = first[nm] + 2 + 12 * i
                if i == 1:
                    dve.wait_ge(S("w_used"), w0)
                for j in range(4):
                    for b in range(2):
                        dve.wait_ge(S("o_u"), 8 * g + 2 * j + b + 1)
                        bufs = [pa, pb]
                        line(TT_(v3(pa)[:, :, 1:80], v3(up)[:, :, 0:79], v3(up)[:, :, 1:80], ALU.add))
                        cur, a, z = 0, 1, 80
                        for e in range(g):
                            s = 1 << e
                            a, z = a + s, z - s
                            line(TT_(v3(bufs[1 - cur])[:, :, a:z], v3(bufs[cur])[:, :, a - s:z - s],
                                     v3(bufs[cur])[:, :, a + s:z + s], ALU.add))
                            cur = 1 - cur
                        p3 = v3(bufs[cur])[:, :, 8:72]
                        rc = V("rcount", 64 * g, 64).unsqueeze(1).to_broadcast((P, 8, 64))
                        line(TT_(p3, p3, rc, ALU.mult))
                        o3 = v3(bufs[1 - cur])[:, :, 8:72]
                        line(TT_(o3, p3, v3(up)[:, :, 8:72], ALU.subtract))
                        dve.sem_inc(S("o_up"), 1)
                        dh = d_hi[:, j * T + b * HALF:j * T + (b + 1) * HALF]
                        dl = d_lo[:, j * T + b * HALF:j * T + (b + 1) * HALF]
                        r3 = lambda t: t.rearrange("p (r c) -> p r c", c=64)
                        line(dve.tensor_copy(r3(dh), o3))
                        line(TT_(r3(dl), o3, r3(dh).bitcast(F32), ALU.subtract))
                    dve.sem_inc(S("o_d"), 1)
                for j in range(4):
                    dve.wait_ge(S("w_used"), w0 + 6 + 2 * j)
                    dve.wait_ge(S("o_act"), 8 * g + 13 + j)
                    t = gs[j % 2][:, :]
                    m = 4 * i + j
                    STT(out=t, in0=slot((2 * j + 1) % 4), scalar=V("od_scale", 8 * part + m), in1=t,
                        op0=ALU.mult, op1=ALU.mult).then_inc(S("o_y"), 1)
                    dve.wait_ge(S("o_y"), 4 * g + j + 5)
                    line(dve.tensor_copy(col(y_hi, m), t))
                    line(TT_(col(y_lo, m), t, col(y_hi, m).bitcast(F32), ALU.subtract))
                    dve.sem_inc(S("o_gs"), 1)
            end(dve)

        begin(dve, "odd_a")
        dve.sem_inc(S("o_y"), 4)
        dve.sem_inc(S("o_gs"), 2)
        line(dve.memset(up[:, :], 0.0))
        dve.sem_inc(S("o_up"), 1)
        odd_groups(0)
        begin(dve, "oout_a")
        residual(1, lambda m: mod(1, 0, 2, m), "w_odd_out_a", False)
        end(dve)
        begin(dve, "odd_b")
        odd_groups(1)
        begin(dve, "oout_b")
        residual(2, lambda m: mod(1, 0, 2, m), "w_odd_out_b", True)
        dve.wait_ge(S("rs"), 3)
        end(dve)
        begin(dve, "final1")
        for k in range(KT):
            line(STT(out=col(xr, k), in0=col(xr, k), scalar=V("final_g", k), in1=xs_[:, :], op0=ALU.mult,
                     op1=ALU.mult))
            dve.sem_inc(S("f1_new"), 1)
            if k == 0:
                line(TT_(tmp[2][:, :], col(xr, k), col(xr, k), ALU.mult))
            else:
                line(TT_(tmp[0][:, :], col(xr, k), col(xr, k), ALU.mult))
                line(TT_(tmp[2][:, :], tmp[2][:, :], tmp[0][:, :], ALU.add))
        line(dve.tensor_copy(xs_[:, :], tmp[2][:, :]))
        dve.sem_inc(S("sq_ready"), 1)
        normalize(3, 2, gain=("norm_mixer", 0))
        end(dve)

        begin(dve, "gla")
        dve.sem_inc(S("g_go"), 1)
        line(dve.memset(cmask[:, :], 1.0))
        line(dve.memset(cmask[:, :].rearrange("p (n c) -> p n c", c=CH)[:, :, 0:1], 0.0))

        def gla_head(i):
            wu = lambda n: dve.wait_ge(S("w_used"), first["w_gla_in"] + 2 + n + 6 * i)
            line(dve.memset(att[:, :], 0.0))
            line(dve.memset(st[:, 0:DV], 0.0))
            dve.wait_ge(S("g_lg"), i + 1)
            TS(cum[:, :], slot(3), V("b_a", i), 0.0, ALU.add, ALU.min).then_inc(S("g_min"), 1)
            dve.wait_ge(S("g_te"), i + 1)
            line(TT_(te[:, :], cum[:, :], te[:, :], ALU.subtract))
            dve.tensor_tensor_scan(out=cum[:, :], data0=cmask[:, :], data1=te[:, :], initial=0.0,
                                   op0=ALU.mult, op1=ALU.add).then_inc(S("g_cum"), 1)
            dve.wait_ge(S("g_exp"), 4 * i + 1)
            wu(1)
            line.go(STT(out=qin[:, :], in0=slot(0), scalar=DK ** -0.5, in1=te[:, :], op0=ALU.mult, op1=ALU.mult))
            dve.wait_ge(S("g_exp"), 4 * i + 3)
            wu(2)
            line(TT_(kin[:, :], slot(1), kdec[:, :], ALU.mult))
            c3 = cum[:, :].rearrange("p (n c) -> p n c", c=CH)
            TT_(kdec[:, :].rearrange("p (n c) -> p n c", c=CH), c3[:, :, CH - 1:CH].to_broadcast((P, 16, CH)),
                c3, ALU.subtract).then_inc(S("g_cl"), 1)
            dve.wait_ge(S("g_exp"), 4 * i + 4)
            TT_(kdec[:, :], slot(1), kdec[:, :], ALU.mult).then_inc(S("g_kdec"), 1)
            dve.sem_inc(S("g_st"), 1)
            for n in range(15):
                if n % 4 == 0:
                    dve.wait_ge(S("g_kv"), 4 * i + n // 4 + 1)
                if n + 1 >= 8:
                    if (n + 1) % 2 == 0:
                        dve.wait_ge(S("g_o"), 8 * i + (n + 1 - 8) // 2 + 1)
                STT(out=st[:, ((n + 1) % 8) * DV:((n + 1) % 8 + 1) * DV], in0=st[:, (n % 8) * DV:(n % 8 + 1) * DV],
                    scalar=dec[:, n:n + 1], in1=kv_at(n),
                    op0=ALU.mult, op1=ALU.add).then_inc(S("g_st"), 1)
                dve.wait_ge(S("g_st"), 16 * i + n + 2)
            for v, sem in enumerate(("g_g0", "g_g1")):
                dve.wait_ge(S("g_rs"), i + 1)
                line(STT(out=kdec[:, :], in0=slot(v), scalar=V("o_norm", v), in1=cum[:, :], op0=ALU.mult, op1=ALU.mult))
                dve.wait_ge(S(sem), i + 1)
                line(TT_(kdec[:, :], kdec[:, :], (att, kdt)[v][:, :], ALU.mult))
                line(dve.tensor_copy(col(y_hi, 2 * i + v), kdec[:, :]))
                line(TT_(col(y_lo, 2 * i + v), kdec[:, :], col(y_hi, 2 * i + v).bitcast(F32), ALU.subtract))
            dve.sem_inc(S("g_go"), 1)

        line.repeat(4, 2 + 1 + 2 + 8, gla_head)
        end(dve)
        begin(dve, "gout")
        residual(3, None, "w_gla_out", True)
        normalize(4, 3, gain=("ple_norm", 0))
        end(dve)

        def ple(r, name):
            begin(dve, name)
            if r == 0:
                dve.sem_inc(S("p_added"), 2)
            dve.wait_ge(S("p_loaded"), 16 * (r + 1))
            line(dve.tensor_copy(p_hi[:, :], pf[:, :]))
            TT_(p_lo[:, :], pf[:, :], p_hi[:, :].bitcast(F32), ALU.subtract).then_inc(S("p_split"), 1)
            line(dve.memset(xs_[:, :], 0.0))

            def two(i):
                for q in range(2):
                    m = 2 * i + q
                    dve.wait_ge(S("p_sig"), 8 * r + m + 1)
                    line(TT_(tmp[2][:, :], slot(2 * q), tmp[q][:, :], ALU.mult))
                    dve.sem_inc(S("p_added"), 1)
                    line(TT_(col(xr, m), col(xr, m), tmp[2][:, :], ALU.add))
                    dve.sem_inc(S("p_new"), 1)
                    line(TT_(tmp[2][:, :], col(xr, m), col(xr, m), ALU.mult))
                    line(TT_(xs_[:, :], xs_[:, :], tmp[2][:, :], ALU.add))
            line.repeat(4, 8, two)
            dve.sem_inc(S("sq_ready"), 1)
            if r == 0:
                normalize(5, 4, gain=("norm_mixer", 8))
            else:
                dve.wait_ge(S("rs"), 8)
            end(dve)
        ple(0, "ple0")

        begin(dve, "fox")
        r16 = slice(0, 16)
        dve.wait_ge(S("w_used"), first["w_fox_in"] + 2)
        TS(fz[0][r16, :], slot(0)[r16, :], vec[0:16, VEC["b_f"][0]:VEC["b_f"][0] + 1], 0.0, ALU.add, ALU.min)\
            .then_inc(S("f_min"), 1)
        line(dve.memset(fz[3][r16, :], 1.0))
        dve.wait_ge(S("f_te"), 1)
        line(TT_(fz[0][r16, :], fz[1][r16, :], fz[0][r16, :], ALU.subtract))
        dve.tensor_tensor_scan(out=fz[2][r16, :], data0=fz[3][r16, :], data1=fz[0][r16, :], initial=0.0,
                               op0=ALU.mult, op1=ALU.add).then_inc(S("f_c"), 1)
        dve.wait_ge(S("f_negc"), 1)
        dve.sem_inc(S("f_max"), 3)
        dve.sem_inc(S("f_pt"), 2)
        dve.sem_inc(S("f_y"), 1)

        def pair_work(p, par, it):
            B = pair_buf[par]
            for j, (raw, hi, lo) in enumerate((("ql_f", "qh", "ql"), ("kl_f", "kh", "kl"))):
                if it == 4 + 4 * j:
                    dve.wait_ge(S("f_rs"), 2 * p + j + 1)
                    STT(out=B[raw][:, :], in0=B[raw][:, :], scalar=gq[:, 0:1] if j == 0 else V("k_norm"),
                        in1=slot(3), op0=ALU.mult, op1=ALU.mult).then_inc(S("f_nrm"), 1)
                if it == 5 + 4 * j:
                    dve.wait_ge(S("f_high"), 3 * p + j + 1)
                    TT_(B[lo][:, :], B[raw][:, :], B[hi][:, :].bitcast(F32), ALU.subtract).then_inc(S("f_low"), 1)
            if it == 11:
                dve.wait_ge(S("f_high"), 3 * p + 3)
                TT_(B["vl"][:, :], slot(3), B["vh"][:, :].bitcast(F32), ALU.subtract).then_inc(S("f_vl"), 1)

        def top(p, s):
            hh, t = STEPS[s]
            for q in UNITS_OF[s]:
                _, lo, hi = UNITS[q]
                dve.wait_ge(S("f_qk"), NU * p + q + 1)
                if s in (0, 8) and lo == 0:
                    dve.wait_ge(S(f"f_cin{hh}"), 16 * p + 16)
                if lo == 0:
                    dve.wait_ge(S("f_t"), NU * p + (UNITS_OF[s - 2][-1] + 4 if s >= 2 else s + 1 + s * 1))
                else:
                    dve.wait_ge(S("f_max"), NU * p + q + 3)
                dve.sem_inc(S("max_begun"), 1)
                dve.tensor_tensor_reduce(lg[s % 2][:, lo * P:hi * P], bank(q % 3, 0, (hi - lo) * P),
                                         negc[hh][:, lo * P:hi * P], -1.0, 3e38 if lo == 0 else nma[s % 2][:, 0:1],
                                         ALU.add, ALU.min, (nmx if hi == t + 1 else nma)[s % 2][:, 0:1])\
                    .then_inc(S("f_max"), 1)

        def shares(p, s):
            n = (STEPS[s][1] + 1) * P
            dve.wait_ge(S("f_exp"), 16 * p + s + 1)
            line(dve.reciprocal(rps[s % 2][:, :], psm[s % 2][:, :]))
            TS(lg[s % 2][:, 0:n], lg[s % 2][:, 0:n], rps[s % 2][:, 0:1], None, ALU.mult).then_inc(S("f_prob"), 1)

        def pt_low(p, s):
            for q in UNITS_OF[s]:
                m = (UNITS[q][2] - UNITS[q][1]) * P
                dve.wait_ge(S("f_ph"), NU * p + q + 1)
                TT_(ptl[q % 4][:, 0:m], bank(3 + q % 2, 0, m), pth[q % 4][:, 0:m].bitcast(F32), ALU.subtract)\
                    .then_inc(S("f_pt"), 1)

        def outputs(p, s):
            e = s // 4
            r = slice(64 * (e // 2), 64 * (e // 2) + 64)
            dve.wait_ge(S("f_pv"), NU * p + UNITS_OF[s][-1] + 5)
            if e == 0:
                dve.wait_ge(S("f_g"), p + 1)
            y = yf[r, bass.ds(p * T + (e % 2) * HALF, HALF)]
            TT_(y, bank(5)[r, :], y, ALU.mult).then_inc(S("f_y"), 1)

        def attend(p, par, s, more=True, next_pair=True):
            c, cpar, cs = step_of(p, par, s)
            if more:
                n, _, ns = step_of(p, par, s + 1)
                top(n, ns)
            if s % 4 == 1 and s > 1:
                n, _, ns = step_of(p, par, s - 2)
                outputs(n, ns)
            if s:
                n, _, ns = step_of(p, par, s - 1)
                pt_low(n, ns)
            shares(c, cs)
            if next_pair:
                pair_work(c + 1, 1 - cpar, cs)

        for it in range(16):
            pair_work(0, 0, it)
        top(0, 0)
        for s in range(2):
            attend(0, 0, s)

        def rest_and_first(p, par, last_next=True):
            for s in range(2, 18):
                attend(p, par, s, next_pair=last_next or s < 16)

        def two_pairs(i):
            rest_and_first(2 * i, 0)
            rest_and_first(2 * i + 1, 1)
        line.repeat(3, 32, two_pairs)
        rest_and_first(6, 0, last_next=False)
        for s in range(2, 16):
            attend(7, 1, s, more=s < 15, next_pair=False)
        pt_low(7, 15)
        outputs(7, 15)
        dve.wait_ge(S("f_y"), 33)
        end(dve)
        begin(dve, "fout")
        for k in range(KT):
            dve.wait_ge(S("yf_high"), k + 1)
            TT_(col(h_lo, k), col(yf, k), col(h_hi, k).bitcast(F32), ALU.subtract).then_inc(S("yf_ready"), 1)
        residual(4, None, "w_fox_out", True)
        normalize(6, 5, gain=("ple_norm", 8))
        end(dve)
        ple(1, "ple1")
        begin(dve, "end")
        for k in range(KT):
            STT(out=col(xr, k), in0=col(xr, k), scalar=V("final_norm", k), in1=xs_[:, :], op0=ALU.mult,
                op1=ALU.mult).then_inc(S("out_ready"), 1)

    block_cm.__exit__(None, None, None)


def _tiles(w):
    k, m = w.shape
    return w.reshape(k // P, P, m // P, P).transpose(2, 1, 0, 3).reshape(m // P, P, k)


def _stream(*rounds):
    return np.ascontiguousarray(np.concatenate([np.concatenate(r, axis=1) for r in rounds], axis=0))


def _cols(v):
    return v.reshape(-1, P).T


def _rank_tiles(w):
    t = _tiles(np.concatenate([w, np.zeros((D, P - w.shape[1]), np.float32)], axis=1))[0]
    return [t[:, 0:512], t[:, 512:1024]]


def _streams(a):
    w = _tiles(a["ev_w_in"][0])
    va, vg, ga, xb, gb = (w[8 * k:8 * k + 8] for k in range(5))
    gates = [np.concatenate([a[n][0, d, h] for d in range(2) for n in ("ev_w_r", "ev_w_i")], axis=1) for h in range(8)]
    s = {"w_even_in": _stream(*[[t for h in (2 * i, 2 * i + 1) for t in (xb[h], va[h], vg[h], gates[h], gb[h], ga[h])]
                                for i in range(4)])}
    wa, wb = _tiles(a["ev_w_out"][0][0:D]), _tiles(a["ev_w_out"][0][D:2 * D])
    s["w_even_out"] = _stream(*[[wb[2 * i], wb[2 * i + 1], wa[2 * i], wa[2 * i + 1]] for i in range(4)])
    w = _tiles(a["od_w_in"][0])
    grp = [_tiles(a["od_w_grp"][0, g]) for g in range(4)]
    for part in range(2):
        s["w_odd_in_" + "ab"[part]] = _stream(*[
            [w[4 * g + j] for j in range(4)] + [t for j in range(4) for t in (w[16 + 4 * g + j], grp[g][j])]
            for g in (2 * part, 2 * part + 1)])
        wo = _tiles(a["od_w_out"][0][part * D:(part + 1) * D])
        s["w_odd_out_" + "ab"[part]] = _stream(*[[wo[2 * i], wo[2 * i + 1]] for i in range(4)])
    w = a["gla_w_in_2"][0]
    s["w_gla_rank"] = _stream(_rank_tiles(w[:, 3072:3088]))
    w = _tiles(w[:, 0:3072])
    s["w_gla_in"] = _stream(*[[w[i], w[4 + i], w[8 + 2 * i], w[9 + 2 * i], w[16 + 2 * i], w[17 + 2 * i]] for i in range(4)])
    w = a["fox_w_in_2"][0]
    s["w_fox_gate"] = _stream(_rank_tiles(w[:, 4096:4112]))
    w = _tiles(w[:, 0:4096])
    s["w_fox_in"] = _stream(*[[w[i], w[8 + i], w[16 + i], w[24 + i]] for i in range(8)])
    for n, src in (("w_gla_out", "gla_w_out_2"), ("w_fox_out", "fox_w_out_2")):
        w = _tiles(a[src][0])
        s[n] = _stream(*[[w[2 * i], w[2 * i + 1]] for i in range(4)])
    for r in range(2):
        wp, wg = _tiles(a["ple_proj_2"][r]), _tiles(a["ple_gate_2"][r])
        s[f"w_ple_{r}"] = _stream(*[[wp[m], wg[m]] for m in range(8)])
    w = np.concatenate([_tiles(a["mod_w"][0]), _tiles(a["mod_w"][1])])
    s["w_mod"] = _stream(*[[w[4 * c + q] for q in range(4)] for c in range(12)])
    return s


def _vectors(a):
    f = np.float32
    t = np.arange(ROW)
    v = {
        "c": np.stack([_cols(a["c"][0]), _cols(a["c_ctx"])], axis=2).reshape(P, 16),
        "mod_b": _cols(a["mod_b"]), "norm_g": _cols(a["norm_g"]), "conv_w": _cols(a["ev_conv_w"][0]),
        "conv_b": _cols(a["ev_conv_b"]), "ln_g": _cols(a["ev_ln_g"]), "ln_b": _cols(a["ev_ln_b"]),
        "sconv_w": _cols(a["ev_sconv_w"][0]), "sconv_b": _cols(a["ev_sconv_b"]), "b_r": _cols(a["ev_b_r"][0]),
        "b_i": _cols(a["ev_b_i"][0]), "lam": _cols(a["ev_lam"][0]), "od_scale": _cols(a["od_scale"]),
        "final_g": _cols(a["final_g"]), "norm_mixer": _cols(a["norm_mixer_2"]), "b_a": _cols(a["gla_b_a_2"]),
        "o_norm": _cols(a["gla_o_norm_2"]), "q_norm": np.tile(a["fox_q_norm_2"], (1, 2)).T,
        "k_norm": np.tile(a["fox_k_norm_2"], (1, 2)).T,
        "b_f": np.concatenate([a["fox_b_f_2"][0], np.zeros(P - 16, f)])[:, None],
        "ple_norm": _cols(a["ple_norm_2"]), "final_norm": _cols(a["final_norm_2"]),
        "rcount": np.tile(np.concatenate([1.0 / (np.minimum(t + h, ROW) - np.maximum(t - h, 0))
                                          for h in (1, 2, 4, 8)]).astype(f), (P, 1)),
        "ident": np.eye(P, dtype=f), "ones": np.ones((P, P), f),
        "heads": np.kron(np.eye(2, dtype=f), np.ones((FH, FH), f)),
    }
    for name, (_, n) in VEC.items():
        assert v[name].shape == (P, n), (name, v[name].shape, n)
    return np.ascontiguousarray(np.concatenate([v[name] for name in VEC], axis=1))


def kernel(**inputs):
    import concourse.bacc as bacc
    from concourse.bass_utils import run_bass_kernel_spmd

    a = {k: np.asarray(v) for k, v in inputs.items()}
    arrays = _streams(a)
    arrays["vec"] = _vectors(a)
    arrays["xT"] = np.ascontiguousarray(a["x"][0].T)
    arrays["ctxT"] = np.ascontiguousarray(a["ctx"][0].T)
    arrays["pT"] = np.ascontiguousarray(a["p_2"][:, 0].transpose(0, 2, 1).reshape(512, T))
    arrays["a2"] = np.ascontiguousarray(a["gla_w_a2_2"][0].reshape(16, 4, P).transpose(1, 0, 2).reshape(64, P))
    nc = bacc.Bacc("TRN2", target_bir_lowering=False, num_devices=1)
    dram = {n: nc.dram_tensor(n, v.shape, F32, kind="ExternalInput").ap() for n, v in arrays.items()}
    out = nc.dram_tensor("out", (D, T), F32, kind="ExternalOutput").ap()
    build(nc, dram, out)
    r = run_bass_kernel_spmd(nc, [arrays], core_ids=[0])
    return np.ascontiguousarray(r.results[0]["out"].T).reshape(1, T, D)
```

```python
import numpy as np
import concourse.bass as bass
from concourse import mybir

F32, F32R, BF16 = mybir.dt.float32, mybir.dt.float32r, mybir.dt.bfloat16
ALU, ACT, AX = mybir.AluOpType, mybir.ActivationFunctionType, mybir.AxisListType

P = 128
D = 1024
T = 1024
C = 256
KT = D // P
TC = T + C
HALF = 512
TAPS, PAD = 31, 15
ROW = 64
CH = 64
DK, DV = 128, 256
FH = 64
LRU_C = 8.0
KB = 1024

STREAMS = [
    ("w_even_in", 4, [1024, 1024, 1024, 512, 1024, 1024] * 2),
    ("w_even_out", 4, [1024] * 4),
    ("w_odd_in_a", 2, [1024] * 4 + [1024, 512] * 4),
    ("w_odd_out_a", 4, [1024] * 2),
    ("w_odd_in_b", 2, [1024] * 4 + [1024, 512] * 4),
    ("w_odd_out_b", 4, [1024] * 2),
    ("w_gla_rank", 1, [512] * 2),
    ("w_gla_in", 4, [1024] * 6),
    ("w_gla_out", 4, [1024] * 2),
    ("w_ple_0", 8, [640, 640]),
    ("w_fox_gate", 1, [512] * 2),
    ("w_fox_in", 8, [1024] * 4),
    ("w_fox_out", 4, [1024] * 2),
    ("w_ple_1", 8, [640, 640]),
]

VEC = {}
_at = 0
for _name, _n in [("c", 16), ("mod_b", 48), ("norm_g", 16), ("conv_w", 8 * TAPS), ("conv_b", 8),
                  ("ln_g", 8), ("ln_b", 8), ("sconv_w", 32), ("sconv_b", 8), ("b_r", 16), ("b_i", 16),
                  ("lam", 16), ("od_scale", 16), ("final_g", 8), ("norm_mixer", 16), ("b_a", 4),
                  ("o_norm", 2), ("q_norm", 1), ("k_norm", 1), ("b_f", 1), ("ple_norm", 16),
                  ("final_norm", 8), ("rcount", 4 * ROW), ("ident", P), ("ones", P), ("heads", P)]:
    VEC[_name] = (_at, _n)
    _at += _n
NVEC = _at


class Line:

    def __init__(self, eng, sem):
        self.eng, self.sem, self.base, self.k = eng, sem, 0, 0

    def __call__(self, ins):
        ins.then_inc(self.sem, 1)
        self.k += 1
        self.eng.wait_ge(self.sem, self.base + self.k)

    def go(self, ins):
        ins.then_inc(self.sem, 1)
        self.k += 1

    def sync(self, back=0):
        self.eng.wait_ge(self.sem, self.base + (self.k - back))

    def repeat(self, times, steps, body):
        start = self.base + self.k
        with self.eng.Fori(0, times) as i:
            self.base, self.k = start + i * steps, 0
            body(i)
            assert self.k == steps, (self.k, steps)
        self.base, self.k = start + times * steps, 0


def build(nc, dram, out):
    base = (nc.sbuf_base + 31) // 32 * 32
    R0, R1, MISC = base + 32 * KB - 160, base + 96 * KB - 160, base + 160 * KB - 160
    assert MISC + 48 * KB <= nc.sbuf_usable_end, (MISC, nc.sbuf_usable_end)

    def sb(name, cols, at, dt=F32):
        return nc.alloc_sbuf_tensor_at("t_" + name, [P, cols], dt, offset=at)

    sems = {}

    def S(name):
        if name not in sems:
            sems[name] = nc.alloc_semaphore(name)
        return sems[name]

    wst = [sb(f"wst{i}", 1024, base + i * 4 * KB) for i in range(2)]
    wh = [sb(f"wh{i}", 1024, base + (2 + i) * 4 * KB, F32R) for i in range(2)]
    wl = [sb(f"wl{i}", 1024, base + (4 + i) * 4 * KB, F32R) for i in range(2)]
    cst = base + 24 * KB
    vec = sb("vec", NVEC, cst)
    vend = cst + (4 * NVEC + 31) // 32 * 32
    a2s = sb("a2s", P, vend)
    cx_rs = sb("cx_rs", C, vend + 512)
    fold = sb("fold", 2 * P, vend)
    sm = vend + 512 + 1024
    modv = sb("modv", 96, sm)
    gsc = sb("gsc", 32, sm + 384)
    silc = sb("silc", 16, sm + 512)
    sp8 = sb("sp8", 16, sm + 576)
    nsp8 = sb("nsp8", 16, sm + 640)
    lt = [sb(f"lt{i}", 16, sm + 704 + 64 * i) for i in range(3)]
    dec = sb("dec", 16, sm + 896)
    nma = [sb(f"nma{i}", 1, sm + 960 + 32 * i) for i in range(2)]
    nmx = [sb(f"nmx{i}", 1, sm + 1024 + 32 * i) for i in range(2)]
    psm = [sb(f"psm{i}", 1, sm + 1088 + 32 * i) for i in range(2)]
    rps = [sb(f"rps{i}", 1, sm + 1152 + 32 * i) for i in range(2)]
    gq = sb("gq", 1, sm + 1216)
    eps6 = sb("eps6", 1, sm + 1248)
    eps5 = sb("eps5", 1, sm + 1280)
    one1 = sb("one1", 1, sm + 1312)
    tri = sb("tri", P, sm + 1344, BF16)
    idb = sb("idb", P, sm + 1600, BF16)
    assert sm + 1856 <= R0, (sm + 1856, R0)

    h_hi, h_lo = sb("h_hi", 8192, R0, F32R), sb("h_lo", 8192, R0 + 32 * KB, F32R)
    y_hi, y_lo = sb("y_hi", 8192, R1, F32R), sb("y_lo", 8192, R1 + 32 * KB, F32R)
    xr = sb("xr", 8192, MISC)
    xs_ = sb("rs", 1024, MISC + 32 * KB)
    tmp = [sb(f"tmp{i}", 1024, MISC + (36 + 4 * i) * KB) for i in range(3)]

    def V(name, j=0, n=1):
        return vec[:, bass.ds(VEC[name][0] + j, n)]

    ident, ones, heads = V("ident", 0, P), V("ones", 0, P), V("heads", 0, P)

    ps = nc.alloc_psum_tensor("ps", [P, 8, HALF], F32)

    def slot(s, cols=1024):
        return ps[:, 2 * s:2 * s + 2, :].rearrange("p a b -> p (a b)")[:, 0:cols]

    def kv_at(n):
        c = (n % 2) * 2 + n % 4 // 2
        return slot(2 + n // 4 % 2)[:, c * DV:(c + 1) * DV]

    def bank(b, lo=0, hi=HALF):
        return ps[:, b, lo:hi]

    def scratch(name, n, cols=1024):
        return nc.dram_tensor(name, [n * P, cols], F32, kind="Internal").ap()
    yb_hi_d, yb_lo_d, ga_d = scratch("yb_hi_d", 9), scratch("yb_lo_d", 9), scratch("ga_d", 8)
    x_d = scratch("x_d", 8)
    negc_d = nc.dram_tensor("negc_d", [16, 1024], F32, kind="Internal").ap()

    def tile(ap, m):
        return ap[bass.ds(m * P, P), :]

    def col(t, m, n=1024):
        return t[:, bass.ds(m * n, n)]

    first, n = {}, 0
    for name, times, widths in STREAMS:
        first[name] = n
        n += times * len(widths)
        assert len(widths) % 2 == 0
    TILES = n
    PHASES = ["start", "even_in", "even_out", "odd_a", "oout_a", "odd_b", "oout_b", "final1",
              "gla", "gout", "ple0", "fox", "fout", "ple1", "end"]

    def begin(eng, phase):
        k = PHASES.index(phase)
        if k:
            eng.wait_ge(S("phase_ended"), 3 * k)

    def end(eng):
        eng.sem_inc(S("phase_ended"), 1)

    hc_hi, hc_lo = sb("hc_hi", 2048, R1, F32R), sb("hc_lo", 2048, R1 + 8 * KB, F32R)
    L0 = R1 + 16 * KB
    u = sb("u", TC, L0)
    u_hi, u_lo = sb("u_hi", TC, L0 + 5120, F32R), sb("u_lo", TC, L0 + 2 * 5120, F32R)
    yb_hi, yb_lo = sb("yb_hi", T, L0 + 5120, F32R), sb("yb_lo", T, L0 + 2 * 5120, F32R)
    a2 = sb("a2", TC, L0 + 5120)
    gb = sb("gb", T, L0 + 2 * 5120)
    ra = [sb(f"ra{d}", TC, L0 + (3 + 2 * d) * 5120) for d in range(2)]
    ii = [sb(f"ii{d}", TC, L0 + (4 + 2 * d) * 5120) for d in range(2)]
    tt = [sb("tt0", TC, L0 + 7 * 5120), sb("tt1", TC, MISC + 32 * KB)]
    sg = sb("sg", T, L0 + 8 * 5120)
    acc1 = sb("acc1", T, L0 + 8 * 5120 + 4096)
    uc = sb("uc", 8192, MISC)
    XB0, XBC = 2, 2 + T + 1 + 2
    xbp = sb("xbp", XBC + C + 1, MISC + 32 * KB + 5120)
    upad = sb("upad", T + 2 * PAD, MISC + 32 * KB + 5120 + 5152)
    assert 4 * (XBC + C + 1) <= 5152 and 5120 + 5152 + 4 * (T + 2 * PAD) <= 16 * KB
    d_hi, d_lo = sb("d_hi", 4096, MISC, F32R), sb("d_lo", 4096, MISC + 16 * KB, F32R)
    gs = [sb(f"gs{i}", T, MISC + (32 + 4 * i) * KB) for i in range(2)]
    up = sb("up", 8 * 80, MISC + 40 * KB)
    pa, pb = sb("pa", 8 * 80, MISC + 40 * KB + 2560), sb("pb", 8 * 80, MISC + 40 * KB + 5120)
    qin, kin, kdec, cum, te = (sb(nm, T, MISC + 4 * i * KB) for i, nm in enumerate(["qin", "kin", "kdec", "cum", "te"]))
    vt = sb("vt", 2048, MISC + 20 * KB)
    kdt = sb("kdt", T, MISC + 28 * KB)
    att = sb("att", T, MISC + 32 * KB)
    st = sb("st", 2048, MISC + 36 * KB)
    cmask = sb("cmask", T, MISC + 44 * KB)
    alr = sb("alr", T, R1 + 60 * KB)
    osq = sb("osq", 2048, MISC)
    pair_buf = []
    for par in range(2):
        at = MISC + 24 * KB * par
        b = {nm: sb(f"{nm}{par}", T, at + 4 * KB * n, F32R) for n, nm in enumerate(["qh", "ql", "kh", "kl"])}
        b |= {nm + "_f": sb(f"{nm}_f{par}", T, at + 4 * KB * n) for n, nm in enumerate(["qh", "ql", "kh", "kl", "v"])}
        b["v"] = sb(f"v{par}", 2 * T, at + 16 * KB, F32R)
        pair_buf.append(b)

    def v_part(b, part):
        return b["v"][:, :].rearrange("p (m q d) -> p m q d", q=2, d=64)[:, :, part, :]

    negc = [sb(f"negc{i}", T, R1 + (32 + 4 * i) * KB) for i in range(2)]
    lg = [sb(f"lg{i}", T, R1 + (40 + 4 * i) * KB) for i in range(2)]
    pth = [sb(f"pth{i}", HALF, R1 + (48 + 2 * i) * KB, F32R) for i in range(4)]
    ptl = [sb(f"ptl{i}", HALF, R1 + (56 + 2 * i) * KB, F32R) for i in range(4)]
    yf = sb("yf", 8192, R1)
    fz = [sb(f"fz{i}", T, R1 + (48 + 4 * i) * KB) for i in range(4)]
    STEPS = [(hh, t) for hh in range(2) for t in (7, 0, 6, 1, 5, 2, 4, 3)]
    PLACES = [(0, 1, 6, 7), (2, 3, 4, 5)]
    UNITS = [(s, lo, min(lo + 4, t + 1)) for s, (_, t) in enumerate(STEPS) for lo in range(0, t + 1, 4)]
    UNITS_OF = [[q for q, un in enumerate(UNITS) if un[0] == s] for s in range(16)]
    NU = len(UNITS)

    def step_of(p, par, s):
        return (p, par, s) if s < 16 else (p + 1, 1 - par, s - 16)
    assert NU % 3 == 0 and NU % 4 == 0
    pf = sb("pf", 2048, R1 + 16 * KB)
    p_hi, p_lo = sb("p_hi", 2048, R1, F32R), sb("p_lo", 2048, R1 + 8 * KB, F32R)

    block_cm = nc.Block()
    block = block_cm.__enter__()

    modw = sb("modw", 12288, R1)
    ctxr = sb("ctxr", 2048, MISC + 32 * KB)
    squares = sb("squares", 10 * T, R0)
    sq0 = sb("sq0", T, MISC + 40 * KB)
    n_tmp = [sb(f"n_tmp{i}", T, R1 + (52 + 4 * i) * KB) for i in range(3)]
    NCHUNK = 12
    mrow = [sb(f"mrow{i}", HALF, R1 + (48 + 2 * i) * KB) for i in range(2)]

    @block.sync
    def _(sp):
        sp.dma_start(vec[:, :], dram["vec"]).then_inc(S("vec_loaded"), 16)
        for c in range(NCHUNK):
            if c == 2:
                sp.dma_start(xr[:, :].rearrange("p (k t) -> p k t", k=KT),
                             dram["xT"].rearrange("(k p) t -> p k t", p=P)).then_inc(S("x_loaded"), 16)
                sp.dma_start(ctxr[:, :].rearrange("p (k t) -> p k t", k=KT),
                             dram["ctxT"].rearrange("(k p) t -> p k t", p=P)).then_inc(S("ctx_loaded"), 16)
            if c >= 3:
                sp.wait_ge(S("mod_used"), c - 2)
            sp.dma_start(modw[:, (c % 3) * 4096:(c % 3 + 1) * 4096],
                         dram["w_mod"][c * P:(c + 1) * P, :]).then_inc(S(f"mod_loaded{c % 3}"), 16)
        for s, (name, times, widths) in enumerate(STREAMS):
            with sp.Fori(0, times) as i:
                at = 0
                for j, w in enumerate(widths):
                    n = first[name] + j + i * len(widths)
                    sp.wait_ge(S("w_split"), n + 1)
                    sp.dma_start(wst[j % 2][:, 0:w],
                                 dram[name][bass.ds(i * P, P), at:at + w]).then_inc(S(f"w_loaded{j % 2}"), 16)
                    at += w
        sp.wait_ge(S("out_stored"), 16 * KT)

    @block.gpsimd
    def _(pool):
        pool.sem_inc(S("w_split"), 2)
        pool.memset(tri[:, :], 0.0).then_inc(S("tri"), 1)
        pool.memset(idb[:, :], 0.0).then_inc(S("tri"), 1)
        pool.wait_ge(S("tri"), 2)
        pool.affine_select(out=tri[:, :], in_=tri[:, :], compare_op=ALU.is_ge, fill=-1e30, base=0,
                           pattern=[[-1, P]], channel_multiplier=1).then_inc(S("tri"), 1)
        pool.affine_select(out=idb[:, :], in_=idb[:, :], compare_op=ALU.not_equal, fill=1.0, base=0,
                           pattern=[[-1, P]], channel_multiplier=1).then_inc(S("tri"), 1)
        for name, times, widths in STREAMS:
            gla = name == "w_gla_in"
            with pool.Fori(0, times) as i:
                for j, w in enumerate(widths):
                    n = first[name] + j + i * len(widths)
                    if gla and j == 4:
                        pool.wait_ge(S("g_att"), i + 1)
                        for q in range(2):
                            pool.sem_inc(S("pool_begun"), 1)
                            a = att[64 * q:64 * q + 64, :].rearrange("p (b c) -> p b c", b=8)[:, :, 64 * q:64 * q + 64]
                            pool.affine_select(out=a, in_=a, compare_op=ALU.is_ge, fill=0.0, base=0,
                                               pattern=[[0, 8], [1, 64]], channel_multiplier=-1)\
                                .then_inc(S("g_causal"), 1)
                            pool.wait_ge(S("g_causal"), 2 * i + q + 1)
                    pool.wait_ge(S(f"w_loaded{j % 2}"), (first[name] // 2 + j // 2 + 1) * 16 + i * (len(widths) * 8))
                    pool.wait_ge(S("w_used"), n + 1)
                    pool.sem_inc(S("pool_begun"), 1)
                    pool.tensor_copy(wh[j % 2][:, 0:w], wst[j % 2][:, 0:w]).then_inc(S("w_high"), 1)
                    pool.wait_ge(S("w_high"), n + 1)
                    pool.tensor_tensor(wl[j % 2][:, 0:w], wst[j % 2][:, 0:w], wh[j % 2][:, 0:w].bitcast(F32),
                                       ALU.subtract).then_inc(S("w_split"), 1)

    @block.tensor
    def _(pe):
        def three(out_, pairs, cols):
            n = len(pairs)
            for k, (ah, al, bh, bl) in enumerate(pairs):
                pe.matmul(out_, ah, bh[:, cols] if cols else bh, start=(k == 0), stop=False)
                pe.matmul(out_, ah, bl[:, cols] if cols else bl, start=False, stop=False)
                last = pe.matmul(out_, al, bh[:, cols] if cols else bh, start=False, stop=(k == n - 1))
            return last

        def wtile(s, kts=8, off=0):
            return [(wh[s][:, off + 128 * k:off + 128 * k + 128], wl[s][:, off + 128 * k:off + 128 * k + 128])
                    for k in range(kts)]

        def project(s, dst, hi, lo, kts=8, off=0, kt0=0, ready=None, chunks=None, start=True, stop=True,
                    ks=None):
            for k in ks or range(kts):
                w1, w2 = wtile(s, kts, off)[k]
                if ready:
                    ready(k)
                for c0, cn, o in chunks or [(0, HALF, dst[:, 0:HALF]), (HALF, HALF, dst[:, HALF:2 * HALF])]:
                    src = o[1:] if isinstance(o, tuple) else (hi, lo)
                    o = o[0] if isinstance(o, tuple) else o
                    stride = T if len(o.shape) and src[0] is not hc_hi else C
                    x1 = src[0][:, (kt0 + k) * stride + c0:(kt0 + k) * stride + c0 + cn]
                    x2 = src[1][:, (kt0 + k) * stride + c0:(kt0 + k) * stride + c0 + cn]
                    pe.matmul(o, w1, x1, start=start and k == 0, stop=False)
                    pe.matmul(o, w1, x2, start=False, stop=False)
                    last = pe.matmul(o, w2, x1, start=False, stop=stop and k == kts - 1)
            return last

        def take(name, i, j):
            per = len(next(w for nm, _, w in STREAMS if nm == name))
            pe.wait_ge(S("w_split"), first[name] + j + 3 + i * per)

        pe.wait_ge(S("vec_loaded"), 16)

        def stats(r, sums=xs_):
            pe.wait_ge(S("sq_ready"), r + 1)
            for b in range(2):
                last = pe.matmul(bank(6 + b), ones, sums[:, b * HALF:(b + 1) * HALF], start=True, stop=True)
            last.then_inc(S("stats"), 1)

        def hready(r):
            return lambda k: pe.wait_ge(S("h_ready"), 8 * r + k + 1)

        pe.sem_inc(S("w_used"), 2)
        pe.wait_ge(S("silc"), 1)
        for c in range(NCHUNK + 1):
            if c == 3:
                stats(0, sq0)
                pe.wait_ge(S("cx_sq"), 1)
                pe.matmul(bank(5, 0, C), ones, cx_rs[:, :], start=True, stop=True).then_inc(S("cx_stats"), 1)
            if c < NCHUNK:
                pe.wait_ge(S(f"mod_loaded{c % 3}"), 16 * (c // 3 + 1))
                if c >= 2:
                    pe.wait_ge(S("mod_row"), c - 1)
                for k in range(KT):
                    at = (c % 3) * 4096 + k * HALF
                    last = pe.matmul(bank(2 + c % 2)[0:2, :], silc[:, 2 * k:2 * k + 2], modw[:, at:at + HALF],
                                     start=(k == 0), stop=(k == KT - 1))
                last.then_inc(S("mod_used"), 1)
            if c >= 1:
                pe.wait_ge(S("mod_row"), c)
                layer, m = divmod(4 * (c - 1), 24)
                for q in range(4):
                    last = pe.transpose(bank(layer, 2 * (m + q), 2 * (m + q) + 2),
                                        mrow[(c - 1) % 2][0:2, q * P:(q + 1) * P], ident[0:2, 0:2])
                last.then_inc(S("mod_turned"), 1)
        pe.wait_ge(S("mod_turned"), NCHUNK)
        end(pe)

        def even_head(i, q):
            h = 2 * i + q
            j = 6 * q
            nm = "w_even_in"
            evac = lambda n: pe.wait_ge(S("e_evac"), 8 * h + n)
            used = lambda ins: ins.then_inc(S("w_used"), 1)
            full = lambda dst, c: [(0, HALF, dst[:, 0:HALF]), (HALF, HALF, dst[:, HALF:2 * HALF])] + \
                ([(0, C, (c, hc_hi, hc_lo))] if c is not None else [])
            evac(6)
            take(nm, i, j)
            used(project(j % 2, slot(0), h_hi, h_lo, chunks=full(slot(0), bank(6, 0, C)),
                         ready=lambda k: pe.wait_ge(S("h_ready"), k + 1)))
            evac(7)
            take(nm, i, j + 1)
            used(project((j + 1) % 2, slot(1), h_hi, h_lo))
            evac(8)
            take(nm, i, j + 2)
            used(project(j % 2, slot(2), h_hi, h_lo))
            take(nm, i, j + 3)
            pe.wait_ge(S("e_ul"), h + 1)
            for g, (sl, b, wait) in enumerate([(0, 7, lambda: evac(9)), (1, 6, lambda: pe.wait_ge(S("e_va"), h + 1)),
                                               (2, 7, lambda: evac(11)), (0, 6, lambda: evac(12))]):
                wait()
                w1 = wh[(j + 3) % 2][:, g * P:(g + 1) * P]
                w2 = wl[(j + 3) % 2][:, g * P:(g + 1) * P]
                for o, c0, cn in ((slot(sl)[:, 0:HALF], 0, HALF), (slot(sl)[:, HALF:T], HALF, HALF), (bank(b, 0, C), T, C)):
                    pe.matmul(o, w1, u_hi[:, c0:c0 + cn], start=True, stop=False)
                    pe.matmul(o, w1, u_lo[:, c0:c0 + cn], start=False, stop=False)
                    last = pe.matmul(o, w2, u_hi[:, c0:c0 + cn], start=False, stop=True)
                if g < 3:
                    last.then_inc(S("e_gate"), 1)
            used(last)
            take(nm, i, j + 4)
            evac(12)
            used(project(j % 2, slot(1), h_hi, h_lo))
            take(nm, i, j + 5)
            evac(13)
            used(project((j + 1) % 2, slot(2), h_hi, h_lo))

        begin(pe, "even_in")
        with pe.Fori(0, 4) as i:
            even_head(i, 0)
            even_head(i, 1)
        pe.wait_ge(S("e_evac"), 72)
        for k in range(KT):
            pe.wait_ge(S("e_uc"), k + 1)
            for b in range(2):
                last = pe.matmul(bank(6 + b), ones, uc[:, k * T + b * HALF:k * T + (b + 1) * HALF],
                                 start=(k == 0), stop=(k == KT - 1))
        last.then_inc(S("ln_sum"), 1)
        pe.wait_ge(S("w_used"), first["w_even_out"] + 2)
        end(pe)

        begin(pe, "even_out")

        def out_pair(nm, i, parts, ring, tiles):
            j = 0
            for p_, (hi, lo, ready) in enumerate(parts):
                for q in range(2):
                    if p_ == 0:
                        pe.wait_ge(S(ring), 8 * out_pair.call[nm] + 2 * i + q + 1)
                    take(nm, i, j)
                    project(j % 2, slot(q), hi, lo, ready=ready if q == 0 else None, start=(p_ == 0),
                            stop=(p_ == len(parts) - 1)).then_inc(S("w_used"), 1)
                    j += 1

        out_pair.call = {"w_even_out": 0, "w_odd_out_a": 1, "w_odd_out_b": 2, "w_gla_out": 3, "w_fox_out": 4}
        for k in range(KT):
            pe.wait_ge(S("ln_sq"), k + 1)
            for b in range(2):
                last = pe.matmul(bank(6 + b), ones, tmp[k % 2][:, b * HALF:(b + 1) * HALF],
                                 start=(k == 0), stop=(k == KT - 1))
            last.then_inc(S("ln_var"), 1)
        with pe.Fori(0, 4) as i:
            out_pair("w_even_out", i, [(h_hi, h_lo, lambda k: pe.wait_ge(S("yb_loaded"), 32 + k // 4 * 32)),
                                       (y_hi, y_lo, lambda k: pe.wait_ge(S("ya_ready"), k + 1))], "x_added", 4)
        pe.wait_ge(S("w_used"), first["w_odd_in_a"] + 2)
        stats(1)
        end(pe)

        def odd_groups(part):
            nm = "w_odd_in_" + "ab"[part]

            def group(i, chase=False):
                g = 2 * part + i
                act = lambda n: pe.wait_ge(S("o_act"), 8 * g + n)
                yev = lambda n: pe.wait_ge(S("o_y"), 4 * g + n)
                if chase:
                    act(7)
                    yev(3)
                    take(nm, i, 1)
                    for k in range(KT):
                        for j in range(2):
                            last = project(j, slot(j), h_hi, h_lo, ks=(k,), ready=hready(1))
                            if k == KT - 1:
                                last.then_inc(S("w_used"), 1)
                for j in range(2 if chase else 0, 4):
                    (act, yev)[j % 2](7 + j // 2 if j % 2 == 0 else 3 + j // 2)
                    take(nm, i, j)
                    project(j % 2, slot(j), h_hi, h_lo).then_inc(S("w_used"), 1)
                for j in range(4):
                    a, b = 2 * j % 4, (2 * j + 1) % 4
                    act((9, 11, 13, 14)[j])
                    take(nm, i, 4 + 2 * j)
                    project(0, slot(a), h_hi, h_lo).then_inc(S("w_used"), 1)
                    act(10) if j == 0 else act(12) if j == 1 else yev(3 + j)
                    take(nm, i, 5 + 2 * j)
                    if j == 0:
                        pe.wait_ge(S("o_d"), 4 * g + 4)
                    project(1, slot(b), d_hi, d_lo, kts=4).then_inc(S("w_used"), 1)
            if part == 0:
                group(0, chase=True)
                group(1)
            else:
                with pe.Fori(0, 2) as i:
                    group(i)
            pe.wait_ge(S("w_used"), first["w_odd_out_" + "ab"[part]] + 2)
            end(pe)

        def out_phase(nm, ready, stat, after, operand=(y_hi, y_lo)):
            with pe.Fori(0, 4) as i:
                out_pair(nm, i, [(*operand, ready)], "x_added", 2)
            pe.wait_ge(S("w_used"), first[after] + 2)
            if stat is not None:
                stats(stat)
            end(pe)

        pe.wait_ge(S("rs"), 2)
        odd_groups(0)
        begin(pe, "oout_a")
        out_phase("w_odd_out_a", None, None, "w_odd_in_b")
        begin(pe, "odd_b")
        odd_groups(1)
        begin(pe, "oout_b")
        out_phase("w_odd_out_b", None, 2, "w_gla_rank")
        begin(pe, "final1")
        stats(3)
        end(pe)

        pe.wait_ge(S("rs"), 4)
        for j in range(2):
            take("w_gla_rank", 0, j)
            project(j, slot(0), h_hi, h_lo, kts=4, kt0=4 * j, ready=lambda k, j=j: hready(2)(4 * j + k),
                    start=(j == 0), stop=(j == 1)).then_inc(S("w_used"), 1)

        def gla_values(i):
            def part(blk, ks):
                o = bank(4 + blk // 2, blk % 2 * DV, (blk % 2 + 1) * DV)
                for k in ks:
                    c = slice(k % 4 * DV, (k % 4 + 1) * DV)
                    w1, w2 = wh[k // 4][:, c], wl[k // 4][:, c]
                    x1 = h_hi[:, k * T + blk * P:k * T + (blk + 1) * P]
                    x2 = h_lo[:, k * T + blk * P:k * T + (blk + 1) * P]
                    pe.matmul(o, x1, w1, start=(k == 0), stop=False)
                    pe.matmul(o, x1, w2, start=False, stop=False)
                    last = pe.matmul(o, x2, w1, start=False, stop=(k == KT - 1))
                return last
            take("w_gla_in", i, 2)
            for blk in range(0, 8, 2):
                part(blk, range(4))
            take("w_gla_in", i, 3)
            for blk in range(0, 8, 2):
                part(blk, range(4, 8))
            for blk in range(1, 8, 2):
                last = part(blk, range(8))
            return last

        def gla_head(i):
            nm = "w_gla_in"
            pe.wait_ge(S("g_alr"), 1)
            pe.wait_ge(S("g_go"), i + 1)
            pe.wait_ge(S("a2_loaded"), 16 * i + 16)
            for b in range(2):
                last = pe.matmul(bank(6 + b), a2s[0:16, :],
                                 alr[0:16, b * HALF:(b + 1) * HALF], start=True, stop=True)
            last.then_inc(S("g_lg"), 1)
            for j in range(2):
                take(nm, i, j)
                project(j, slot(j), h_hi, h_lo).then_inc(S("w_used"), 1)
            pe.wait_ge(S("g_ab"), i + 1)
            gla_values(i).then_inc(S("w_used"), 2)
            pe.wait_ge(S("g_kdec"), i + 1)
            for b in range(8):
                last = pe.matmul(slot(0)[:, b * P:(b + 1) * P], kin[:, b * P:(b + 1) * P],
                                 qin[:, b * P:(b + 1) * P], start=True, stop=True)
            last.then_inc(S("g_pe"), 1)
            for b in range(8):
                last = pe.transpose(slot(1)[:, b * P:(b + 1) * P], kdec[:, b * P:(b + 1) * P], ident)
            last.then_inc(S("g_pe"), 1)
            pe.wait_ge(S("g_kdt"), i + 1)
            for r in range(4):
                if r >= 2:
                    pe.wait_ge(S("g_st"), 16 * i + 4 * (r - 1) + 1)
                for c in range(4):
                    n = 4 * r + c
                    lo = 64 * (n % 2)
                    last = pe.matmul(kv_at(n), kdt[lo:lo + 64, (n // 2) * P:(n // 2 + 1) * P],
                                     vt[lo:lo + 64, (n // 2) * DV:(n // 2 + 1) * DV], start=True, stop=True)
                last.then_inc(S("g_kv"), 1)
                if r == 0:
                    pe.wait_ge(S("g_causal"), 2 * i + 2)
                    pe.wait_ge(S("g_kdt"), i + 1)
                if r in (1, 3):
                    for b in range(4 * (r // 2), 4 * (r // 2) + 4):
                        pe.wait_ge(S("g_st"), 16 * i + 2 * b + 2)
                        for v in range(2):
                            o = slot(v)[:, b * P:(b + 1) * P]
                            pe.matmul(o, vt[:, b * DV + v * P:b * DV + (v + 1) * P], att[:, b * P:(b + 1) * P],
                                      start=True, stop=False)
                            for c in range(2):
                                n = 2 * b + c
                                if n == 0:
                                    continue
                                last = pe.matmul(slot(v)[:, b * P + c * 64:b * P + c * 64 + 64],
                                                 st[:, (n % 8) * DV + v * P:(n % 8) * DV + (v + 1) * P],
                                                 qin[:, b * P + c * 64:b * P + c * 64 + 64], start=False, stop=(c == 1))
                        last.then_inc(S("g_o"), 1)
            pe.wait_ge(S("g_st"), 16 * i + 16)
            take(nm, i, 4)
            project(0, slot(2), h_hi, h_lo).then_inc(S("w_used"), 1)
            pe.wait_ge(S("g_sq"), i + 1)
            for b in range(2):
                for v in range(2):
                    last = pe.matmul(bank(6 + b), ones, osq[:, v * T + b * HALF:v * T + (b + 1) * HALF],
                                     start=(v == 0), stop=(v == 1))
            last.then_inc(S("g_ss"), 1)
            take(nm, i, 5)
            pe.wait_ge(S("g_g0"), i + 1)
            project(1, slot(2), h_hi, h_lo).then_inc(S("w_used"), 1)

        with pe.Fori(0, 4) as i:
            gla_head(i)
        pe.wait_ge(S("w_used"), first["w_gla_out"] + 2)
        end(pe)
        begin(pe, "gout")
        out_phase("w_gla_out", None, 4, "w_ple_0")

        def ple(r):
            nm = f"w_ple_{r}"

            def two(i):
                for q in range(2):
                    m = 2 * i + q
                    pe.wait_ge(S("p_added"), 8 * r + m + 1)
                    pe.wait_ge(S("p_split"), r + 1)
                    with_round(nm, m, 0)
                    project(0, slot(2 * q), p_hi, p_lo, kts=2)
                    project(0, slot(2 * q + 1), h_hi, h_lo, kts=3, off=256, ready=hready(3 + 2 * r), stop=False)\
                        .then_inc(S("w_used"), 1)
                    with_round(nm, m, 1)
                    project(1, slot(2 * q + 1), h_hi, h_lo, kts=5, kt0=3,
                            ready=lambda k: hready(3 + 2 * r)(k + 3), start=False).then_inc(S("w_used"), 1)

            def with_round(nm, m, j):
                pe.wait_ge(S("w_split"), first[nm] + j + 3 + m * 2)
            with pe.Fori(0, 4) as i:
                two(i)
            pe.wait_ge(S("w_used"), (first["w_fox_gate"] if r == 0 else TILES) + 2)
            stats(5 + 2 * r)
            end(pe)

        pe.wait_ge(S("rs"), 5)
        ple(0)

        pe.wait_ge(S("rs"), 6)
        pe.wait_ge(S("tri"), 4)
        for j in range(2):
            take("w_fox_gate", 0, j)
            project(j, slot(0), h_hi, h_lo, kts=4, kt0=4 * j, ready=lambda k, j=j: hready(4)(4 * j + k),
                    start=(j == 0), stop=(j == 1)).then_inc(S("w_used"), 1)

        def share(n, parts, at):
            return {at + k: range(k * n // parts, (k + 1) * n // parts) for k in range(parts)}

        Q_AT, K_AT, V_AT, G_AT = share(8, 6, 0), share(8, 5, 9), share(8, 5, 17), share(8, 6, 26)

        def project_pair(p, par, it, half, first_pair=False):
            nm, n = "w_fox_in", 2 * it + half

            def tile_part(j, at, free):
                if n == min(at):
                    free()
                    take(nm, p, j)
                for k in at[n]:
                    last = project(j % 2, slot(3), h_hi, h_lo, ks=(k,))
                if n == max(at):
                    last.then_inc(S("w_used"), 1)
            if n in Q_AT:
                tile_part(0, Q_AT, lambda: None if first_pair else pe.wait_ge(S("f_g"), p))
            if n in K_AT:
                tile_part(1, K_AT, lambda: pe.wait_ge(S("f_nrm"), 2 * p + 1))
            if n in G_AT:
                tile_part(3, G_AT, lambda: pe.wait_ge(S("f_vl"), p + 1))
            if n in (7, 15):
                j = (n - 7) // 8
                pe.wait_ge(S("f_sq"), 2 * p + j + 1)
                b = pair_buf[par][("qh_f", "kh_f")[j]]
                for c in range(2):
                    last = pe.matmul(bank(6 + c), heads, b[:, c * HALF:(c + 1) * HALF], start=True, stop=True)
                last.then_inc(S("f_ss"), 1)
            if n in V_AT:
                tile_part(2, V_AT, lambda: pe.wait_ge(S("f_nrm"), 2 * p + 2))
            if n == 23:
                pe.wait_ge(S("f_vraw"), p + 1)
                raw = pair_buf[par]["v_f"]
                for b in range(8):
                    last = pe.transpose(slot(3)[:, b * P:(b + 1) * P], raw[:, b * P:(b + 1) * P], ident)
                last.then_inc(S("f_vt"), 1)

        def scores(p, par, s):
            B, (hh, t) = pair_buf[par], STEPS[s]
            rows = slice(64 * hh, 64 * hh + 64)
            if s == 0:
                pe.wait_ge(S("f_low"), 2 * p + 2)
            for q in UNITS_OF[s]:
                _, lo, hi = UNITS[q]
                pe.wait_ge(S("f_max"), NU * p + q + 1)
                o = bank(q % 3, 0, (hi - lo) * P)
                a, b = slice(t * P, (t + 1) * P), slice(lo * P, hi * P)
                pe.matmul(o, B["qh"][rows, a], B["kh"][rows, b], start=True, stop=False)
                pe.matmul(o, B["qh"][rows, a], B["kl"][rows, b], start=False, stop=False)
                last = pe.matmul(o, B["ql"][rows, a], B["kh"][rows, b], start=False, stop=hi <= t)
                if hi == t + 1:
                    last = pe.matmul(bank(q % 3, (hi - lo - 1) * P, (hi - lo) * P), idb[:, :], tri[:, :],
                                     start=False, stop=True)
                last.then_inc(S("f_qk"), 1)

        def turn(p, s):
            pe.wait_ge(S("f_prob"), 16 * p + s + 1)
            for q in UNITS_OF[s]:
                _, lo, hi = UNITS[q]
                pe.wait_ge(S("f_pt"), NU * p + q + 1)
                for b in range(lo, hi):
                    last = pe.transpose(bank(3 + q % 2, (b - lo) * P, (b - lo + 1) * P),
                                        lg[s % 2][:, b * P:(b + 1) * P], ident)
                last.then_inc(S("f_t"), 1)

        def values(p, par, s):
            B, (hh, t) = pair_buf[par], STEPS[s]
            if s == 0:
                pe.wait_ge(S("f_vl"), p + 1)
            if s % 4 == 0:
                pe.wait_ge(S("f_y"), 4 * p + s // 4 + 1)
            for q in UNITS_OF[s]:
                _, lo, hi = UNITS[q]
                pe.wait_ge(S("f_pt"), NU * p + q + 3)
                c = PLACES[s // 4 % 2].index(t)
                o = bank(5, c * P, (c + 1) * P)
                for b in range(lo, hi):
                    v = B["v"][:, (2 * b + hh) * P:(2 * b + hh + 1) * P]
                    d = slice((b - lo) * P, (b - lo + 1) * P)
                    pe.matmul(o, v, pth[q % 4][:, d], start=(b == 0), stop=False)
                    last = pe.matmul(o, v, ptl[q % 4][:, d], start=False, stop=(b == t))
                last.then_inc(S("f_pv"), 1)

        def attend(p, par, s, scored=True, project_next=True):
            c, cpar, cs = step_of(p, par, s)
            if project_next:
                project_pair(c + 1, 1 - cpar, cs, 0)
            turn(c, cs)
            if scored:
                scores(*step_of(p, par, s + 2))
            if project_next:
                project_pair(c + 1, 1 - cpar, cs, 1)
            if s:
                values(*step_of(p, par, s - 1))

        pe.sem_inc(S("f_t"), 3)
        pe.sem_inc(S("f_pv"), 4)
        for it in range(16):
            for half in range(2):
                project_pair(0, 0, it, half, first_pair=True)
        scores(0, 0, 0)
        scores(0, 0, 1)
        for s in range(2):
            attend(0, 0, s)

        def rest_and_first(p, par, last_next=True):
            for s in range(2, 18):
                attend(p, par, s, project_next=last_next or s < 16)
        with pe.Fori(0, 3) as i:
            rest_and_first(2 * i, 0)
            rest_and_first(2 * i + 1, 1)
        rest_and_first(6, 0, last_next=False)
        for s in range(2, 16):
            attend(7, 1, s, scored=s < 14, project_next=False)
        values(7, 1, 15)
        pe.wait_ge(S("f_pv"), 8 * NU + 4)
        end(pe)
        begin(pe, "fout")
        out_phase("w_fox_out", lambda k: pe.wait_ge(S("yf_ready"), k + 1), 6, "w_ple_1", (h_hi, h_lo))
        pe.wait_ge(S("rs"), 7)
        ple(1)
        begin(pe, "end")

    @block.scalar
    def _(act):
        line = Line(act, S("act_line"))
        A = act.activation

        def rsqrt(dst, src, n, eps):
            line(A(dst, src, ACT.Ln, bias=eps[:, 0:1], scale=1.0 / n))
            return A(dst, dst, ACT.Exp, scale=-0.5)

        def p_load(layer):
            act.dma_start(pf[:, :].rearrange("p (k t) -> p k t", k=2),
                          dram["pT"][layer * 2 * P:(layer + 1) * 2 * P, :].rearrange("(k p) t -> p k t", p=P))\
                .then_inc(S("p_loaded"), 16)

        def high(r):
            if "ple" in r:
                act.wait_ge(S("w_used"), first[f"w_ple_{r['ple']}"] + 2)
                p_load(r["ple"])
            act.wait_ge(S("stats"), r["stat"] + 1)
            rsqrt(xs_[:, :], slot(3), D, eps6).then_inc(S("rs"), 1)
            if r.get("op") is None:
                return
            for k in range(KT):
                t = tmp[k % r["bufs"]]
                act.wait_ge(S("n_scaled"), 8 * r["op"] + k + 1)
                if "layer" in r:
                    m = 48 * r["layer"] + 2 * k
                    A(col(h_hi, k), t[:, :], ACT.Identity, bias=modv[:, m:m + 1])\
                        .then_inc(S("n_high"), 1)
                else:
                    A(col(h_hi, k), t[:, :], ACT.Copy).then_inc(S("n_high"), 1)

        act.wait_ge(S("vec_loaded"), 16)
        act.wait_ge(S("consts"), 1)
        A(silc[:, :], V("c", 0, 16), ACT.Silu).then_inc(S("silc"), 1)
        def mod_row(c):
            act.wait_ge(S("mod_used"), c + 1)
            if c >= 2:
                act.wait_ge(S("mod_turned"), c - 1)
            A(mrow[c % 2][0:2, :], bank(2 + c % 2)[0:2, :], ACT.Copy).then_inc(S("mod_row"), 1)

        mod_row(0)
        mod_row(1)
        for k in range(KT):
            act.wait_ge(S("x_loaded"), 16)
            if k >= 2:
                act.wait_ge(S("x_sq_used"), k - 1)
            A(squares[:, (k % 2) * T:(k % 2 + 1) * T], col(xr, k), ACT.Square).then_inc(S("x_sq"), 1)
        act.wait_ge(S("ctx_loaded"), 16)
        for k in range(KT):
            A(squares[:, (2 + k) * T:(2 + k) * T + C], ctxr[:, k * C:(k + 1) * C], ACT.Square).then_inc(S("c_sq"), 1)
        line(A(lt[0][:, :], V("lam", 0, 16), ACT.Abs))
        A(lt[0][:, :], lt[0][:, :], ACT.Exp, scale=-1.0).then_inc(S("lam_exp"), 1)
        act.wait_ge(S("stats"), 1)
        rsqrt(sq0[:, :], slot(3), D, eps6).then_inc(S("rs"), 1)
        act.wait_ge(S("cx_stats"), 1)
        rsqrt(cx_rs[:, :], bank(5, 0, C), D, eps6).then_inc(S("cx_rs"), 1)

        for c in range(2, 6):
            mod_row(c)
        for k in range(KT):
            act.wait_ge(S("n_scaled"), k + 1)
            A(col(h_hi, k), n_tmp[k % 3][:, :], ACT.Identity, bias=modv[:, 2 * k:2 * k + 1]).then_inc(S("n_high"), 1)
            if k in (2, 5, 7):
                mod_row(6 + (2, 5, 7).index(k))
        for c in range(9, NCHUNK):
            mod_row(c)
        act.wait_ge(S("c_scaled"), 1)
        A(hc_hi[:, :], ctxr[:, :], ACT.Copy).then_inc(S("c_high"), 1)
        act.wait_ge(S("c_high"), 1)
        end(act)

        begin(act, "even_in")
        act.sem_inc(S("e_evac"), 8)
        act.sem_inc(S("ga_stored"), 16)

        def even_head(h):
            w0 = first["w_even_in"] + 2
            wu = lambda n: act.wait_ge(S("w_used"), w0 + n + 6 * h)
            ev = lambda ins: ins.then_inc(S("e_evac"), 1)
            wu(1)
            act.wait_ge(S("e_u"), h + 1)
            A(xbp[:, XB0:XB0 + T], slot(0), ACT.Copy)
            ev(A(xbp[:, XBC:XBC + C], bank(6, 0, C), ACT.Copy))
            store_yb(h)
            act.wait_ge(S("e_u"), h + 2)
            act.wait_ge(S("yb_stored"), 32 * h + 32)
            A(u_hi[:, :], u[:, :], ACT.Copy).then_inc(S("e_uh"), 1)
            wu(3)
            act.wait_ge(S("ga_stored"), 16 * h + 16)
            ev(A(sg[:, :], slot(2), ACT.Sigmoid))
            act.wait_ge(S("e_lru"), h + 1)
            for g in range(4):
                d = g // 2
                if g < 3:
                    act.wait_ge(S("e_gate"), 3 * h + g + 1)
                else:
                    wu(4)
                buf, bias = (ra, ii)[g % 2][d], V(("b_r", "b_i")[g % 2], 8 * d + h)
                sl, b = ((0, 7), (1, 6), (2, 7), (0, 6))[g]
                A(buf[:, 0:T], slot(sl), ACT.Sigmoid, bias=bias)
                ev(A(buf[:, T:TC], bank(b, 0, C), ACT.Sigmoid, bias=bias))
            act.wait_ge(S("e_evac"), 8 * h + 14)
            for d in range(2):
                line.go(A(tt[d][:, :], ra[d][:, :], ACT.Tanh, scale=sp8[:, bass.ds(8 * d + h, 1)]))
            line.sync()
            for d in range(2):
                line(A(ra[d][:, :], ra[d][:, :], ACT.Exp, scale=nsp8[:, bass.ds(8 * d + h, 1)]))
                if d == 1:
                    wu(5)
                    ev(A(gb[:, :], slot(1), ACT.Silu))
                    wu(6)
                    act.wait_ge(S("e_va"), h + 1)
                    ev(A(sg[:, :], slot(2), ACT.Silu))
                    act.wait_ge(S("e_q"), 2 * h + 1)
                A(a2[:, :], ra[d][:, :], ACT.Square).then_inc(S("e_a2"), 1)
            for d in range(2):
                act.wait_ge(S("e_q"), 2 * h + d + 1)
                A(tt[d][:, :], tt[d][:, :], ACT.Sqrt).then_inc(S("e_sqrt"), 1)
            act.wait_ge(S("e_evac"), 8 * h + 16)
            act.dma_start(tile(ga_d, h), sg[:, :]).then_inc(S("ga_stored"), 16)

        def store_yb(h):
            act.wait_ge(S("e_lru"), h + 1)
            act.dma_start(tile(yb_hi_d, h), yb_hi[:, :].bitcast(F32)).then_inc(S("yb_stored"), 16)
            act.dma_start(tile(yb_lo_d, h), yb_lo[:, :].bitcast(F32)).then_inc(S("yb_stored"), 16)

        line.repeat(8, 4, even_head)

        def load_yb(k0, k1):
            for dst, src in ((h_hi, yb_hi_d), (h_lo, yb_lo_d)):
                act.dma_start(dst[:, k0 * T:k1 * T].bitcast(F32).rearrange("p (k t) -> p k t", k=k1 - k0),
                              src[(k0 + 1) * P:(k1 + 1) * P, :].rearrange("(k p) t -> p k t", p=P))\
                    .then_inc(S("yb_loaded"), 16)
        act.wait_ge(S("w_used"), first["w_even_out"] + 2)
        act.wait_ge(S("yb_stored"), 32 * 8)
        load_yb(0, KT // 2)
        store_yb(8)
        end(act)

        begin(act, "even_out")
        act.wait_ge(S("yb_stored"), 32 * 9)
        load_yb(KT // 2, KT)
        act.wait_ge(S("ga_stored"), 16 * 9)
        for k in range(KT):
            act.wait_ge(S("ln_centered"), k + 1)
            if k >= 2:
                act.wait_ge(S("ln_var"), k - 1)
            A(tmp[k % 2][:, :], col(uc, k), ACT.Square).then_inc(S("ln_sq"), 1)
        act.wait_ge(S("ln_var"), 8)
        for k in range(2):
            act.dma_start(tmp[k][:, :], tile(ga_d, k)).then_inc(S(f"ga_loaded{k}"), 16)
        rsqrt(xs_[:, :], slot(3), D, eps5).then_inc(S("ln_rs"), 1)
        for k in range(KT + 2):
            if k < KT:
                act.wait_ge(S("ln_scaled"), k + 1)
                A(col(uc, k), col(uc, k), ACT.Silu, bias=V("ln_b", k), scale=V("ln_g", k)).then_inc(S("ln_silu"), 1)
            if 1 <= k <= KT:
                act.wait_ge(S("ya_gated"), k)
                A(col(y_hi, k - 1), col(uc, k - 1), ACT.Copy).then_inc(S("ya_high"), 1)
                if k + 1 < KT:
                    act.dma_start(tmp[(k - 1) % 2][:, :], tile(ga_d, k + 1)).then_inc(S(f"ga_loaded{(k - 1) % 2}"), 16)
            if k >= 2:
                act.wait_ge(S("ya_ready"), k - 1)
                act.dma_start(col(xr, k - 2), tile(dram["xT"], k - 2)).then_inc(S("x_in"), 16)
        def stored(m):
            act.wait_ge(S("x_new"), m + 1)
            act.dma_start(tile(x_d, m), col(xr, m)).then_inc(S("x_stored"), 16)
        with act.Fori(0, KT) as m:
            stored(m)
        act.sem_inc(S("o_act"), 8)
        high({"stat": 1, "op": 1, "bufs": 3, "layer": 1})
        act.wait_ge(S("n_high"), 16)
        act.wait_ge(S("x_stored"), 16 * 8)
        end(act)

        def odd_groups(part):
            nm = "w_odd_in_" + "ab"[part]

            def group(i):
                g = 2 * part + i
                w0 = first[nm] + 2
                ev = lambda ins: ins.then_inc(S("o_act"), 1)
                for j in range(4):
                    act.wait_ge(S("w_used"), w0 + j + 1 + i * 12)
                    for b in range(2):
                        act.wait_ge(S("o_up"), 8 * g + 2 * j + b + 1)
                        ins = A(up[:, :].rearrange("p (r c) -> p r c", c=80)[:, :, 8:72],
                                bank(2 * j + b).rearrange("p (r c) -> p r c", c=64), ACT.Copy)
                        ins.then_inc(S("o_u"), 1)
                    act.wait_ge(S("o_u"), 8 * g + 2 * j + 2)
                    act.sem_inc(S("o_act"), 1)
                for j in range(4):
                    act.wait_ge(S("w_used"), w0 + 5 + 2 * j + i * 12)
                    act.wait_ge(S("o_gs"), 4 * g + j + 1)
                    ev(A(gs[j % 2][:, :], slot(2 * j % 4), ACT.Silu))
            with act.Fori(0, 2) as i:
                group(i)
            act.wait_ge(S("o_act"), 16 * part + 24)
            end(act)

        def out_load(src):
            for k in range(KT):
                act.dma_start(col(xr, k), tile(src, k)).then_inc(S("x_in"), 16)

        begin(act, "odd_a")
        odd_groups(0)

        def out_phase(r, name, spec=None, store=True, before=None):
            begin(act, name)
            if before:
                before()
            out_load(x_d)
            if store:

                def stored(m):
                    act.wait_ge(S("x_new"), 8 * r + m + 1)
                    act.dma_start(tile(x_d, m), col(xr, m)).then_inc(S("x_stored"), 16)
                with act.Fori(0, KT) as m:
                    stored(m)
                out_phase.stores += 1
                act.wait_ge(S("x_stored"), 16 * 8 * out_phase.stores)
            if spec:
                high(spec)
            end(act)
        out_phase.stores = 1

        out_phase(1, "oout_a")
        begin(act, "odd_b")
        odd_groups(1)
        out_phase(2, "oout_b", {"stat": 2}, store=False)
        begin(act, "final1")
        for m in range(KT):
            act.wait_ge(S("f1_new"), m + 1)
            act.dma_start(tile(x_d, m), col(xr, m)).then_inc(S("x_stored"), 16)
            if m >= 2:
                act.wait_ge(S("f1_added"), m - 1)
            A(tmp[m % 2][:, :], col(xr, m), ACT.Square).then_inc(S("f1_sq"), 1)
        out_phase.stores += 1
        high({"stat": 3, "op": 2, "bufs": 3})
        act.wait_ge(S("n_high"), 24)
        act.wait_ge(S("x_stored"), 16 * 8 * out_phase.stores)
        end(act)

        begin(act, "gla")
        act.wait_ge(S("w_used"), first["w_gla_in"] + 2)
        A(alr[0:16, :], slot(0)[0:16, :], ACT.Copy).then_inc(S("g_alr"), 1)

        def gla_head(i):
            wu = lambda n: act.wait_ge(S("w_used"), first["w_gla_in"] + 2 + n + 6 * i)
            act.dma_start(a2s[0:16, :], dram["a2"][bass.ds(i * 16, 16), :]).then_inc(S("a2_loaded"), 16)
            act.wait_ge(S("g_min"), i + 1)
            line(A(te[:, :], slot(3), ACT.Abs, bias=V("b_a", i)))
            act.sem_inc(S("g_ab"), 1)
            line(A(te[:, :], te[:, :], ACT.Exp, scale=-1.0))
            A(te[:, :], te[:, :], ACT.Ln, bias=one1[:, 0:1]).then_inc(S("g_te"), 1)
            act.wait_ge(S("g_cum"), i + 1)
            A(te[:, :], cum[:, :], ACT.Exp, scale=1.0 / 16).then_inc(S("g_exp"), 1)
            A(kdec[:, :], cum[:, :], ACT.Exp, scale=-1.0 / 16).then_inc(S("g_exp"), 1)
            A(dec[:, :], cum[:, CH - 1::CH],
              ACT.Exp, scale=1.0 / 16).then_inc(S("g_exp"), 1)
            act.wait_ge(S("g_cl"), i + 1)
            A(kdec[:, :], kdec[:, :], ACT.Exp, scale=1.0 / 16).then_inc(S("g_exp"), 1)
            for v in range(2):
                wu(4)
                A(vt[:, v * T:(v + 1) * T], slot(2 + v), ACT.Copy).then_inc(S("g_v"), 1)
            act.wait_ge(S("g_pe"), 2 * i + 1)
            for q in range(2):
                r = slice(64 * q, 64 * q + 64)
                line.go(A(att[r, :].rearrange("p (b c) -> p b c", b=8)[:, :, 64 * q:64 * q + 64],
                          slot(0)[r, :].rearrange("p (b c) -> p b c", b=8)[:, :, 64 * q:64 * q + 64], ACT.Copy))
            line.sync()
            act.sem_inc(S("g_att"), 1)
            act.wait_ge(S("g_pe"), 2 * i + 2)
            act.wait_ge(S("g_v"), 2 * i + 2)
            A(kdt[:, :], slot(1), ACT.Copy).then_inc(S("g_kdt"), 1)
            act.wait_ge(S("g_o"), 8 * i + 8)
            line(A(osq[:, 0:T], slot(0), ACT.Square))
            A(osq[:, T:2 * T], slot(1), ACT.Square).then_inc(S("g_sq"), 1)
            wu(5)
            act.wait_ge(S("g_kdt"), i + 1)
            A(att[:, :], slot(2), ACT.Silu).then_inc(S("g_g0"), 1)
            act.wait_ge(S("g_ss"), i + 1)
            rsqrt(cum[:, :], slot(3), DV, eps6).then_inc(S("g_rs"), 1)
            wu(6)
            A(kdt[:, :], slot(2), ACT.Silu).then_inc(S("g_g1"), 1)

        line.repeat(4, 6, gla_head)
        act.wait_ge(S("g_g1"), 4)
        end(act)

        out_phase(3, "gout", {"stat": 4, "op": 3, "bufs": 3, "ple": 0}, store=False)

        def ple(r, name):
            begin(act, name)
            nm = f"w_ple_{r}"

            def two(i):
                for q in range(2):
                    m = 2 * i + q
                    act.wait_ge(S("w_used"), first[nm] + 4 + 2 * m)
                    act.wait_ge(S("p_added"), 8 * r + m + 1)
                    A(tmp[q][:, :], slot(2 * q + 1), ACT.Sigmoid).then_inc(S("p_sig"), 1)
            with act.Fori(0, 4) as i:
                two(i)
            if r == 0:
                with act.Fori(0, KT) as m:
                    act.wait_ge(S("p_new"), m + 1)
                    act.dma_start(tile(x_d, m), col(xr, m)).then_inc(S("x_stored"), 16)
                out_phase.stores += 1
                high({"stat": 5, "op": 4, "bufs": 3})
                act.wait_ge(S("n_high"), 40)
                act.wait_ge(S("x_stored"), 16 * 8 * out_phase.stores)
            else:
                high({"stat": 7})
            end(act)
        ple(0, "ple0")

        begin(act, "fox")
        act.wait_ge(S("f_min"), 1)
        r16 = slice(0, 16)
        line(A(fz[1][r16, :], slot(0)[r16, :], ACT.Abs, bias=vec[0:16, VEC["b_f"][0]:VEC["b_f"][0] + 1]))
        line(A(fz[1][r16, :], fz[1][r16, :], ACT.Exp, scale=-1.0))
        A(fz[1][r16, :], fz[1][r16, :], ACT.Ln, bias=one1[0:16, 0:1]).then_inc(S("f_te"), 1)
        act.wait_ge(S("f_c"), 1)
        act.dma_start(negc_d, fz[2][r16, :]).then_inc(S("f_negc_out"), 16)

        def load_c(p, hh):
            act.dma_start(negc[hh][:, :], negc_d[bass.ds(2 * p + hh, 1), :].to_broadcast((P, T)))\
                .then_inc(S(f"f_cin{hh}"), 16)

        def pair_work(p, par, it):
            B = pair_buf[par]
            wu = lambda n: act.wait_ge(S("w_used"), first["w_fox_in"] + 2 + n + 4 * p)
            for j, (raw, sq, high_) in enumerate((("ql_f", "qh_f", "qh"), ("kl_f", "kh_f", "kh"))):
                if it == 3 + 4 * j:
                    wu(1 + j)
                    line(A(B[raw][:, :], slot(3), ACT.Copy))
                    A(B[sq][:, :], B[raw][:, :], ACT.Square).then_inc(S("f_sq"), 1)
                if it == 4 + 4 * j:
                    act.wait_ge(S("f_ss"), 2 * p + j + 1)
                    rsqrt(slot(3), slot(3), FH, eps6).then_inc(S("f_rs"), 1)
                if it == 5 + 4 * j:
                    act.wait_ge(S("f_nrm"), 2 * p + j + 1)
                    A(B[high_][:, :], B[raw][:, :], ACT.Copy).then_inc(S("f_high"), 1)
            if it == 11:
                wu(3)
                A(B["v_f"][:, :], slot(3), ACT.Copy).then_inc(S("f_vraw"), 1)
            if it == 12:
                act.wait_ge(S("f_vt"), p + 1)
                A(v_part(B, 0), slot(3).rearrange("p (m d) -> p m d", d=64), ACT.Copy).then_inc(S("f_high"), 1)
            if it == 15:
                wu(4)
                A(yf[:, bass.ds(p * T, T)], slot(3), ACT.Silu).then_inc(S("f_g"), 1)

        def expo(p, s):
            n = (STEPS[s][1] + 1) * P
            act.wait_ge(S("f_max"), NU * p + UNITS_OF[s][-1] + 4)
            A(lg[s % 2][:, 0:n], lg[s % 2][:, 0:n], ACT.Exp, bias=nmx[s % 2][:, 0:1], scale=-1.0,
              accum_out=psm[s % 2][:, 0:1]).then_inc(S("f_exp"), 1)

        def pt_high(p, s):
            for q in UNITS_OF[s]:
                n = (UNITS[q][2] - UNITS[q][1]) * P
                act.wait_ge(S("f_t"), NU * p + q + 4)
                act.wait_ge(S("f_pv"), NU * p + q + 1)
                A(pth[q % 4][:, 0:n], bank(3 + q % 2, 0, n), ACT.Copy).then_inc(S("f_ph"), 1)

        def attend(p, par, s, more=True, next_pair=True):
            c, cpar, cs = step_of(p, par, s)
            if more:
                n, _, ns = step_of(p, par, s + 1)
                expo(n, ns)
            if next_pair:
                pair_work(c + 1, 1 - cpar, cs)
            pt_high(c, cs)
            if next_pair and cs in (8, 15):
                act.wait_ge(S("f_max"), NU * c + NU // 2 * (1 + cs // 15) + 3)
                load_c(c + 1, cs // 15)

        for it in range(16):
            pair_work(0, 0, it)
        act.wait_ge(S("f_negc_out"), 16)
        act.sem_inc(S("f_negc"), 1)
        load_c(0, 0)
        load_c(0, 1)
        expo(0, 0)
        for s in range(2):
            attend(0, 0, s)

        def rest_and_first(p, par, last_next=True):
            for s in range(2, 18):
                attend(p, par, s, next_pair=last_next or s < 16)

        def two_pairs(i):
            rest_and_first(2 * i, 0)
            rest_and_first(2 * i + 1, 1)
        line.repeat(3, 8, two_pairs)
        rest_and_first(6, 0, last_next=False)
        for s in range(2, 16):
            attend(7, 1, s, more=s < 15, next_pair=False)
        act.wait_ge(S("f_ph"), 8 * NU)
        end(act)

        def y_high():
            for k in range(KT):
                A(col(h_hi, k), col(yf, k), ACT.Copy).then_inc(S("yf_high"), 1)
        out_phase(4, "fout", {"stat": 6, "op": 5, "bufs": 3, "ple": 1}, store=False, before=y_high)
        ple(1, "ple1")
        begin(act, "end")
        for k in range(KT):
            act.wait_ge(S("out_ready"), k + 1)
            act.dma_start(tile(out, k), col(xr, k)).then_inc(S("out_stored"), 16)
        act.wait_ge(S("out_stored"), 16 * KT)

    @block.vector
    def _(dve):
        line = Line(dve, S("dve_line"))
        TT_, TS, STT = dve.tensor_tensor, dve.tensor_scalar, dve.scalar_tensor_tensor
        for t, v in ((eps6, 1e-6), (eps5, 1e-5), (one1, 1.0)):
            line.go(dve.memset(t[:, :], v))
        line.sync()
        dve.sem_inc(S("consts"), 1)
        dve.wait_ge(S("vec_loaded"), 16)
        line(TS(gq[:, :], V("q_norm"), FH ** -0.5, None, ALU.mult))

        for k in range(KT):
            dve.wait_ge(S("x_sq"), k + 1)
            s = squares[:, (k % 2) * T:(k % 2 + 1) * T]
            if k == 0:
                line.go(dve.tensor_copy(sq0[:, :], s))
            else:
                line.go(TT_(sq0[:, :], sq0[:, :], s, ALU.add))
            line.sync()
            dve.sem_inc(S("x_sq_used"), 1)
        dve.sem_inc(S("sq_ready"), 1)
        dve.wait_ge(S("c_sq"), 8)
        line(TT_(cx_rs[:, :], squares[:, 2 * T:2 * T + C], squares[:, 3 * T:3 * T + C], ALU.add))
        for k in range(2, KT):
            line(TT_(cx_rs[:, :], cx_rs[:, :], squares[:, (2 + k) * T:(2 + k) * T + C], ALU.add))
        dve.sem_inc(S("cx_sq"), 1)
        dve.wait_ge(S("lam_exp"), 1)
        line(TS(lt[1][:, :], lt[0][:, :], 2.0, None, ALU.add))
        line(dve.reciprocal(lt[1][:, :], lt[1][:, :]))
        line(TT_(lt[0][:, :], lt[0][:, :], lt[1][:, :], ALU.mult))
        line(TT_(lt[1][:, :], lt[0][:, :], lt[0][:, :], ALU.mult))
        line(TS(lt[2][:, :], lt[1][:, :], 1 / 17, 1 / 15, ALU.mult, ALU.add))
        for n in (13, 11, 9, 7, 5, 3, 1):
            line(TT_(lt[2][:, :], lt[2][:, :], lt[1][:, :], ALU.mult))
            line(TS(lt[2][:, :], lt[2][:, :], 1 / n, None, ALU.add))
        line(TT_(lt[2][:, :], lt[2][:, :], lt[0][:, :], ALU.mult))
        line(TS(lt[1][:, :], V("lam", 0, 16), -1.0, 0.0, ALU.mult, ALU.max))
        line(STT(out=lt[2][:, :], in0=lt[2][:, :], scalar=2.0, in1=lt[1][:, :], op0=ALU.mult, op1=ALU.add))
        line(TS(sp8[:, :], lt[2][:, :], LRU_C, None, ALU.mult))
        line(TS(nsp8[:, :], lt[2][:, :], -LRU_C, None, ALU.mult))
        mv = modv[:, :].rearrange("p (l m v) -> p l v m", l=2, v=2)

        def mod_layer(layer):
            dve.wait_ge(S("mod_turned"), 6 * (layer + 1))
            for v in range(2):
                line(TT_(mv[:, layer, v, :], bank(layer, 0, 48).rearrange("p (m v) -> p v m", v=2)[:, v, :],
                         V("mod_b", 24 * layer, 24), ALU.add))
                line(STT(out=gsc[:, (2 * layer + v) * 8:(2 * layer + v + 1) * 8], in0=mv[:, layer, v, 8:16],
                         scalar=1.0, in1=V("norm_g", 8 * layer, 8), op0=ALU.add, op1=ALU.mult))
        mod_layer(0)

        def mod(layer, v, part, k):
            return modv[:, bass.ds(48 * layer + 2 * (8 * part + k) + v, 1)]

        def normalize(stat, op, gain=None, layer=None, bufs=tmp, rs=xs_):
            dve.wait_ge(S("rs"), stat + 1)
            for k in range(KT + 2):
                if k < KT:
                    t = bufs[k % 3]
                    if k >= 3:
                        dve.wait_ge(S("h_ready"), 8 * op + k - 2)
                    g = V(gain[0], gain[1] + k) if layer is None else gsc[:, 16 * layer + k:16 * layer + k + 1]
                    STT(out=t[:, :], in0=col(xr, k), scalar=g, in1=rs[:, :], op0=ALU.mult, op1=ALU.mult)\
                        .then_inc(S("n_scaled"), 1)
                if k >= 1 and k <= KT:
                    dve.wait_ge(S("n_high"), 8 * op + k)
                    t, hi, lo = bufs[(k - 1) % 3][:, :], col(h_hi, k - 1).bitcast(F32), col(h_lo, k - 1)
                    if layer is None:
                        ins = TT_(lo, t, hi, ALU.subtract)
                    else:
                        ins = STT(out=lo, in0=t, scalar=mod(layer, 0, 0, k - 1), in1=hi, op0=ALU.add, op1=ALU.subtract)
                    ins.then_inc(S("h_ready"), 1)
            dve.wait_ge(S("h_ready"), 8 * op + 8)

        normalize(0, 0, layer=0, bufs=n_tmp, rs=sq0)
        dve.wait_ge(S("cx_rs"), 1)
        c3 = ctxr[:, :].rearrange("p (k c) -> p k c", c=C)
        line(TT_(c3, c3, cx_rs[:, :].rearrange("p (o c) -> p o c", o=1).to_broadcast((P, KT, C)), ALU.mult))
        for k in range(KT):
            c = ctxr[:, k * C:(k + 1) * C]
            line.go(TS(c, c, gsc[:, 8 + k:9 + k], mod(0, 1, 0, k), ALU.mult, ALU.add))
        line.sync()
        dve.sem_inc(S("c_scaled"), 1)
        mod_layer(1)
        dve.wait_ge(S("c_high"), 1)
        line(TT_(hc_lo[:, :], ctxr[:, :], hc_hi[:, :].bitcast(F32), ALU.subtract))
        end(dve)

        begin(dve, "even_in")
        line.go(dve.memset(xbp[:, :], 0.0))
        line.go(dve.memset(upad[:, :], 0.0))
        line.go(dve.memset(yb_hi[:, :].bitcast(F32), 0.0))
        line.go(dve.memset(yb_lo[:, :].bitcast(F32), 0.0))
        line.sync()
        dve.sem_inc(S("e_u"), 1)
        dve.sem_inc(S("e_lru"), 1)

        def even_head(h):
            dve.wait_ge(S("e_evac"), 8 * h + 9)
            for j in range(4):
                w = V("sconv_w", 8 * j + h)
                for o, n in ((0, T), (T, C)):
                    s = xbp[:, (XB0 if o == 0 else XBC) - 2 + j:(XB0 if o == 0 else XBC) - 2 + j + n]
                    if j >= 1:
                        line.sync(1)
                    if j == 0:
                        line.go(TS(u[:, o:o + n], s, w, V("sconv_b", h), ALU.mult, ALU.add))
                    else:
                        line.go(STT(out=u[:, o:o + n], in0=s, scalar=w, in1=u[:, o:o + n], op0=ALU.mult, op1=ALU.add))
            line.sync()
            dve.sem_inc(S("e_u"), 1)
            dve.wait_ge(S("e_uh"), h + 1)
            TT_(u_lo[:, :], u[:, :], u_hi[:, :].bitcast(F32), ALU.subtract).then_inc(S("e_ul"), 1)
            dve.wait_ge(S("e_evac"), 8 * h + 10)
            TT_(upad[:, PAD:PAD + T], slot(1), sg[:, :], ALU.mult).then_inc(S("e_va"), 1)
            dve.wait_ge(S("e_va"), h + 1)
            for j in range(TAPS):
                o = col(uc, h) if j % 2 == 0 else acc1[:, :]
                s, w = upad[:, j:j + T], V("conv_w", 8 * j + h)
                if j == 0:
                    line.go(TS(o, s, w, V("conv_b", h), ALU.mult, ALU.add))
                elif j == 1:
                    line.go(TS(o, s, w, None, ALU.mult))
                else:
                    line.sync(1)
                    line.go(STT(out=o, in0=s, scalar=w, in1=o, op0=ALU.mult, op1=ALU.add))
            line.sync()
            TT_(col(uc, h), col(uc, h), acc1[:, :], ALU.add).then_inc(S("e_uc"), 1)
            for d in range(2):
                dve.wait_ge(S("e_a2"), 2 * h + d + 1)
                STT(out=tt[d][:, :], in0=a2[:, :], scalar=1.0, in1=tt[d][:, :], op0=ALU.add, op1=ALU.mult)\
                    .then_inc(S("e_q"), 1)
                line.go(TT_(ii[d][:, :], ii[d][:, :], u[:, :], ALU.mult))
            line.sync()
            for d in range(2):
                dve.wait_ge(S("e_sqrt"), 2 * h + d + 1)
                line(TT_(tt[d][:, :], tt[d][:, :], ii[d][:, :], ALU.mult))
                for lo, hi, init in ((T, TC, 0.0), (0, T, ii[d][:, TC - 1:TC] if d == 0 else ii[d][:, T:T + 1])):
                    f = slice(lo, hi) if d == 0 else (slice(hi - 1, lo - 1, -1) if lo else slice(hi - 1, None, -1))
                    line(dve.tensor_tensor_scan(out=ii[d][:, f], data0=ra[d][:, f], data1=tt[d][:, f],
                                                initial=init, op0=ALU.mult, op1=ALU.add))
            line(TT_(tt[0][:, 0:T], ii[0][:, 0:T], ii[1][:, 0:T], ALU.add))
            dve.wait_ge(S("e_evac"), 8 * h + 15)
            line(TT_(tt[0][:, 0:T], tt[0][:, 0:T], gb[:, :], ALU.mult))
            line(dve.tensor_copy(yb_hi[:, :], tt[0][:, 0:T]))
            TT_(yb_lo[:, :], tt[0][:, 0:T], yb_hi[:, :].bitcast(F32), ALU.subtract).then_inc(S("e_lru"), 1)

        line.repeat(8, 8 + TAPS + 2 + 6 + 3, even_head)
        dve.wait_ge(S("e_lru"), 9)
        line.sync()
        end(dve)

        begin(dve, "even_out")
        dve.sem_inc(S("x_added"), 2)
        dve.wait_ge(S("ln_sum"), 1)
        line(TS(xs_[:, :], slot(3), 1.0 / D, None, ALU.mult))
        for k in range(KT):
            TT_(col(uc, k), col(uc, k), xs_[:, :], ALU.subtract).then_inc(S("ln_centered"), 1)
        dve.wait_ge(S("ln_rs"), 1)

        def scale_ln(k):
            TT_(col(uc, k), col(uc, k), xs_[:, :], ALU.mult).then_inc(S("ln_scaled"), 1)
        scale_ln(0)
        for k in range(KT + 1):
            if k + 1 < KT:
                scale_ln(k + 1)
            if k < KT:
                dve.wait_ge(S("ln_silu"), k + 1)
                dve.wait_ge(S(f"ga_loaded{k % 2}"), 16 * (k // 2 + 1))
                TT_(col(uc, k), col(uc, k), tmp[k % 2][:, :], ALU.mult).then_inc(S("ya_gated"), 1)
            if k >= 1:
                dve.wait_ge(S("ya_high"), k)
                TT_(col(y_lo, k - 1), col(uc, k - 1), col(y_hi, k - 1).bitcast(F32), ALU.subtract)\
                    .then_inc(S("ya_ready"), 1)

        def residual(r, gate, name, last):
            if last:
                line(dve.memset(xs_[:, :], 0.0))

            def two(i):
                for q in range(2):
                    m = 2 * i + q
                    w = first[name] + 2 + (4 * i + 3 + q if name == "w_even_out" else 2 * i + q + 1)
                    dve.wait_ge(S("w_used"), w)
                    dve.wait_ge(S("x_in"), 128 * (r + 1))
                    if gate is None:
                        TT_(col(xr, m), slot(q), col(xr, m), ALU.add).then_inc(S("x_added"), 1)
                    else:
                        STT(out=col(xr, m), in0=slot(q), scalar=gate(m), in1=col(xr, m), op0=ALU.mult,
                            op1=ALU.add).then_inc(S("x_added"), 1)
                    dve.wait_ge(S("x_added"), 8 * r + m + 3)
                    dve.sem_inc(S("x_new"), 1)
                    if last:
                        line(TT_(tmp[0][:, :], col(xr, m), col(xr, m), ALU.mult))
                        line(TT_(xs_[:, :], xs_[:, :], tmp[0][:, :], ALU.add))
            line.repeat(4, 4 if last else 0, two)
            if last:
                dve.sem_inc(S("sq_ready"), 1)

        def p_split(r):
            if r == 0:
                dve.sem_inc(S("p_added"), 2)
            dve.wait_ge(S("p_loaded"), 16 * (r + 1))
            line(dve.tensor_copy(p_hi[:, :], pf[:, :]))
            TT_(p_lo[:, :], pf[:, :], p_hi[:, :].bitcast(F32), ALU.subtract).then_inc(S("p_split"), 1)

        residual(0, lambda m: mod(0, 0, 2, m), "w_even_out", True)
        dve.sem_inc(S("o_y"), 4)
        normalize(1, 1, layer=1)
        end(dve)

        def odd_groups(part):
            nm = "w_odd_in_" + "ab"[part]
            v3 = lambda t: t[:, :].rearrange("p (r c) -> p r c", c=80)
            for i in range(2):
                g = 2 * part + i
                w0 = first[nm] + 2 + 12 * i
                if i == 1:
                    dve.wait_ge(S("w_used"), w0)
                for j in range(4):
                    for b in range(2):
                        dve.wait_ge(S("o_u"), 8 * g + 2 * j + b + 1)
                        bufs = [pa, pb]
                        line(TT_(v3(pa)[:, :, 1:80], v3(up)[:, :, 0:79], v3(up)[:, :, 1:80], ALU.add))
                        cur, a, z = 0, 1, 80
                        for e in range(g):
                            s = 1 << e
                            a, z = a + s, z - s
                            line(TT_(v3(bufs[1 - cur])[:, :, a:z], v3(bufs[cur])[:, :, a - s:z - s],
                                     v3(bufs[cur])[:, :, a + s:z + s], ALU.add))
                            cur = 1 - cur
                        p3 = v3(bufs[cur])[:, :, 8:72]
                        rc = V("rcount", 64 * g, 64).unsqueeze(1).to_broadcast((P, 8, 64))
                        line(TT_(p3, p3, rc, ALU.mult))
                        o3 = v3(bufs[1 - cur])[:, :, 8:72]
                        line(TT_(o3, p3, v3(up)[:, :, 8:72], ALU.subtract))
                        dve.sem_inc(S("o_up"), 1)
                        dh = d_hi[:, j * T + b * HALF:j * T + (b + 1) * HALF]
                        dl = d_lo[:, j * T + b * HALF:j * T + (b + 1) * HALF]
                        r3 = lambda t: t.rearrange("p (r c) -> p r c", c=64)
                        line(dve.tensor_copy(r3(dh), o3))
                        line(TT_(r3(dl), o3, r3(dh).bitcast(F32), ALU.subtract))
                    dve.sem_inc(S("o_d"), 1)
                for j in range(4):
                    dve.wait_ge(S("w_used"), w0 + 6 + 2 * j)
                    dve.wait_ge(S("o_act"), 8 * g + 13 + j)
                    t = gs[j % 2][:, :]
                    m = 4 * i + j
                    STT(out=t, in0=slot((2 * j + 1) % 4), scalar=V("od_scale", 8 * part + m), in1=t,
                        op0=ALU.mult, op1=ALU.mult).then_inc(S("o_y"), 1)
                    dve.wait_ge(S("o_y"), 4 * g + j + 5)
                    line(dve.tensor_copy(col(y_hi, m), t))
                    line(TT_(col(y_lo, m), t, col(y_hi, m).bitcast(F32), ALU.subtract))
                    dve.sem_inc(S("o_gs"), 1)
            end(dve)

        begin(dve, "odd_a")
        dve.sem_inc(S("o_gs"), 2)
        line(dve.memset(up[:, :], 0.0))
        dve.sem_inc(S("o_up"), 1)
        odd_groups(0)
        begin(dve, "oout_a")
        residual(1, lambda m: mod(1, 0, 2, m), "w_odd_out_a", False)
        end(dve)
        begin(dve, "odd_b")
        odd_groups(1)
        begin(dve, "oout_b")
        residual(2, lambda m: mod(1, 0, 2, m), "w_odd_out_b", True)
        dve.wait_ge(S("rs"), 3)
        end(dve)
        begin(dve, "final1")
        for k in range(KT + 1):
            if k < KT:
                line(STT(out=col(xr, k), in0=col(xr, k), scalar=V("final_g", k), in1=xs_[:, :], op0=ALU.mult,
                         op1=ALU.mult))
                dve.sem_inc(S("f1_new"), 1)
            if k >= 2:
                dve.wait_ge(S("f1_sq"), k)
                a = tmp[0] if k == 2 else tmp[2]
                TT_((xs_ if k == KT else tmp[2])[:, :], a[:, :], tmp[(k - 1) % 2][:, :], ALU.add)\
                    .then_inc(S("f1_added"), 1)
                dve.wait_ge(S("f1_added"), k - 1)
        dve.sem_inc(S("sq_ready"), 1)
        normalize(3, 2, gain=("norm_mixer", 0))
        end(dve)

        begin(dve, "gla")
        dve.sem_inc(S("g_go"), 1)
        line(dve.memset(cmask[:, :], 1.0))
        line(dve.memset(cmask[:, :].rearrange("p (n c) -> p n c", c=CH)[:, :, 0:1], 0.0))

        def gla_head(i):
            wu = lambda n: dve.wait_ge(S("w_used"), first["w_gla_in"] + 2 + n + 6 * i)
            line(dve.memset(att[:, :], 0.0))
            line(dve.memset(st[:, 0:DV], 0.0))
            dve.wait_ge(S("g_lg"), i + 1)
            TS(cum[:, :], slot(3), V("b_a", i), 0.0, ALU.add, ALU.min).then_inc(S("g_min"), 1)
            dve.wait_ge(S("g_te"), i + 1)
            line(TT_(te[:, :], cum[:, :], te[:, :], ALU.subtract))
            dve.tensor_tensor_scan(out=cum[:, :], data0=cmask[:, :], data1=te[:, :], initial=0.0,
                                   op0=ALU.mult, op1=ALU.add).then_inc(S("g_cum"), 1)
            dve.wait_ge(S("g_exp"), 4 * i + 1)
            wu(1)
            line.go(STT(out=qin[:, :], in0=slot(0), scalar=DK ** -0.5, in1=te[:, :], op0=ALU.mult, op1=ALU.mult))
            dve.wait_ge(S("g_exp"), 4 * i + 3)
            wu(2)
            line(TT_(kin[:, :], slot(1), kdec[:, :], ALU.mult))
            c3 = cum[:, :].rearrange("p (n c) -> p n c", c=CH)
            TT_(kdec[:, :].rearrange("p (n c) -> p n c", c=CH), c3[:, :, CH - 1:CH].to_broadcast((P, 16, CH)),
                c3, ALU.subtract).then_inc(S("g_cl"), 1)
            dve.wait_ge(S("g_exp"), 4 * i + 4)
            TT_(kdec[:, :], slot(1), kdec[:, :], ALU.mult).then_inc(S("g_kdec"), 1)
            dve.sem_inc(S("g_st"), 1)
            for n in range(15):
                if n % 4 == 0:
                    dve.wait_ge(S("g_kv"), 4 * i + n // 4 + 1)
                if n + 1 >= 8:
                    if (n + 1) % 2 == 0:
                        dve.wait_ge(S("g_o"), 8 * i + (n + 1 - 8) // 2 + 1)
                STT(out=st[:, ((n + 1) % 8) * DV:((n + 1) % 8 + 1) * DV], in0=st[:, (n % 8) * DV:(n % 8 + 1) * DV],
                    scalar=dec[:, n:n + 1], in1=kv_at(n),
                    op0=ALU.mult, op1=ALU.add).then_inc(S("g_st"), 1)
                dve.wait_ge(S("g_st"), 16 * i + n + 2)
            dve.wait_ge(S("g_rs"), i + 1)
            for v, y in enumerate((kdec, kin)):
                line.go(STT(out=y[:, :], in0=slot(v), scalar=V("o_norm", v), in1=cum[:, :], op0=ALU.mult, op1=ALU.mult))
            line.sync()
            dve.sem_inc(S("g_go"), 1)
            for v, (y, sem) in enumerate(((kdec, "g_g0"), (kin, "g_g1"))):
                dve.wait_ge(S(sem), i + 1)
                line(TT_(y[:, :], y[:, :], (att, kdt)[v][:, :], ALU.mult))
                line(dve.tensor_copy(col(y_hi, 2 * i + v), y[:, :]))
                line(TT_(col(y_lo, 2 * i + v), y[:, :], col(y_hi, 2 * i + v).bitcast(F32), ALU.subtract))

        line.repeat(4, 2 + 1 + 2 + 8, gla_head)
        end(dve)
        begin(dve, "gout")
        residual(3, None, "w_gla_out", True)
        p_split(0)
        normalize(4, 3, gain=("ple_norm", 0))
        end(dve)

        def ple(r, name):
            begin(dve, name)
            line(dve.memset(xs_[:, :], 0.0))

            def two(i):
                for q in range(2):
                    m = 2 * i + q
                    dve.wait_ge(S("p_sig"), 8 * r + m + 1)
                    line(TT_(tmp[2][:, :], slot(2 * q), tmp[q][:, :], ALU.mult))
                    dve.sem_inc(S("p_added"), 1)
                    line(TT_(col(xr, m), col(xr, m), tmp[2][:, :], ALU.add))
                    dve.sem_inc(S("p_new"), 1)
                    line(TT_(tmp[2][:, :], col(xr, m), col(xr, m), ALU.mult))
                    line(TT_(xs_[:, :], xs_[:, :], tmp[2][:, :], ALU.add))
            line.repeat(4, 8, two)
            dve.sem_inc(S("sq_ready"), 1)
            if r == 0:
                normalize(5, 4, gain=("norm_mixer", 8))
            else:
                dve.wait_ge(S("rs"), 8)
            end(dve)
        ple(0, "ple0")

        begin(dve, "fox")
        r16 = slice(0, 16)
        dve.wait_ge(S("w_used"), first["w_fox_in"] + 2)
        TS(fz[0][r16, :], slot(0)[r16, :], vec[0:16, VEC["b_f"][0]:VEC["b_f"][0] + 1], 0.0, ALU.add, ALU.min)\
            .then_inc(S("f_min"), 1)
        line(dve.memset(fz[3][r16, :], 1.0))
        dve.wait_ge(S("f_te"), 1)
        line(TT_(fz[0][r16, :], fz[1][r16, :], fz[0][r16, :], ALU.subtract))
        dve.tensor_tensor_scan(out=fz[2][r16, :], data0=fz[3][r16, :], data1=fz[0][r16, :], initial=0.0,
                               op0=ALU.mult, op1=ALU.add).then_inc(S("f_c"), 1)
        dve.sem_inc(S("f_max"), 3)
        dve.sem_inc(S("f_pt"), 2)
        dve.sem_inc(S("f_y"), 1)

        def pair_work(p, par, it):
            B = pair_buf[par]
            for j, (raw, hi, lo) in enumerate((("ql_f", "qh", "ql"), ("kl_f", "kh", "kl"))):
                if it == 4 + 4 * j:
                    dve.wait_ge(S("f_rs"), 2 * p + j + 1)
                    STT(out=B[raw][:, :], in0=B[raw][:, :], scalar=gq[:, 0:1] if j == 0 else V("k_norm"),
                        in1=slot(3), op0=ALU.mult, op1=ALU.mult).then_inc(S("f_nrm"), 1)
                if it == 5 + 4 * j:
                    dve.wait_ge(S("f_high"), 3 * p + j + 1)
                    TT_(B[lo][:, :], B[raw][:, :], B[hi][:, :].bitcast(F32), ALU.subtract).then_inc(S("f_low"), 1)
            if it == 12:
                dve.wait_ge(S("f_high"), 3 * p + 3)
                TT_(v_part(B, 1), slot(3).rearrange("p (m d) -> p m d", d=64), v_part(B, 0).bitcast(F32),
                    ALU.subtract).then_inc(S("f_vl"), 1)

        def top(p, s):
            hh, t = STEPS[s]
            for q in UNITS_OF[s]:
                _, lo, hi = UNITS[q]
                dve.wait_ge(S("f_qk"), NU * p + q + 1)
                if s in (0, 8) and lo == 0:
                    dve.wait_ge(S(f"f_cin{hh}"), 16 * p + 16)
                if lo == 0:
                    dve.wait_ge(S("f_t"), NU * p + (UNITS_OF[s - 2][-1] + 4 - (NU if s < 2 else 0)))
                else:
                    dve.wait_ge(S("f_max"), NU * p + q + 3)
                dve.sem_inc(S("max_begun"), 1)
                dve.tensor_tensor_reduce(lg[s % 2][:, lo * P:hi * P], bank(q % 3, 0, (hi - lo) * P),
                                         negc[hh][:, lo * P:hi * P], -1.0, 3e38 if lo == 0 else nma[s % 2][:, 0:1],
                                         ALU.add, ALU.min, (nmx if hi == t + 1 else nma)[s % 2][:, 0:1])\
                    .then_inc(S("f_max"), 1)

        def shares(p, s):
            n = (STEPS[s][1] + 1) * P
            dve.wait_ge(S("f_exp"), 16 * p + s + 1)
            line(dve.reciprocal(rps[s % 2][:, :], psm[s % 2][:, :]))
            TS(lg[s % 2][:, 0:n], lg[s % 2][:, 0:n], rps[s % 2][:, 0:1], None, ALU.mult).then_inc(S("f_prob"), 1)

        def pt_low(p, s):
            for q in UNITS_OF[s]:
                m = (UNITS[q][2] - UNITS[q][1]) * P
                dve.wait_ge(S("f_ph"), NU * p + q + 1)
                TT_(ptl[q % 4][:, 0:m], bank(3 + q % 2, 0, m), pth[q % 4][:, 0:m].bitcast(F32), ALU.subtract)\
                    .then_inc(S("f_pt"), 1)

        def outputs(p, s):
            e = s // 4
            r = slice(64 * (e // 2), 64 * (e // 2) + 64)
            dve.wait_ge(S("f_pv"), NU * p + UNITS_OF[s][-1] + 5)
            if e == 0:
                dve.wait_ge(S("f_g"), p + 1)
            for q in range(2):
                c = slice(q * 2 * P, (q + 1) * 2 * P)
                y = yf[r, bass.ds(p * T + PLACES[e % 2][2 * q] * P, 2 * P)]
                line.go(TT_(fold[r, :], bank(5)[64:128, c], y, ALU.mult))
                line(TT_(y, bank(5)[0:64, c], y, ALU.mult))
                line(TT_(y, y, fold[r, :], ALU.add))
            dve.sem_inc(S("f_y"), 1)

        def attend(p, par, s, more=True, next_pair=True):
            c, cpar, cs = step_of(p, par, s)
            if more:
                n, _, ns = step_of(p, par, s + 1)
                top(n, ns)
            if s:
                n, _, ns = step_of(p, par, s - 1)
                pt_low(n, ns)
            shares(c, cs)
            if s % 4 == 1 and s > 1:
                n, _, ns = step_of(p, par, s - 2)
                outputs(n, ns)
            if next_pair:
                pair_work(c + 1, 1 - cpar, cs)

        for it in range(16):
            pair_work(0, 0, it)
        dve.wait_ge(S("f_negc"), 1)
        top(0, 0)
        for s in range(2):
            attend(0, 0, s)

        def rest_and_first(p, par, last_next=True):
            for s in range(2, 18):
                attend(p, par, s, next_pair=last_next or s < 16)

        def two_pairs(i):
            rest_and_first(2 * i, 0)
            rest_and_first(2 * i + 1, 1)
        line.repeat(3, 80, two_pairs)
        rest_and_first(6, 0, last_next=False)
        for s in range(2, 16):
            attend(7, 1, s, more=s < 15, next_pair=False)
        pt_low(7, 15)
        outputs(7, 15)
        dve.wait_ge(S("f_y"), 33)
        end(dve)
        begin(dve, "fout")
        for k in range(KT):
            dve.wait_ge(S("yf_high"), k + 1)
            TT_(col(h_lo, k), col(yf, k), col(h_hi, k).bitcast(F32), ALU.subtract).then_inc(S("yf_ready"), 1)
        residual(4, None, "w_fox_out", True)
        p_split(1)
        normalize(6, 5, gain=("ple_norm", 8))
        end(dve)
        ple(1, "ple1")
        begin(dve, "end")
        for k in range(KT):
            STT(out=col(xr, k), in0=col(xr, k), scalar=V("final_norm", k), in1=xs_[:, :], op0=ALU.mult,
                op1=ALU.mult).then_inc(S("out_ready"), 1)

    block_cm.__exit__(None, None, None)


def _tiles(w):
    k, m = w.shape
    return w.reshape(k // P, P, m // P, P).transpose(2, 1, 0, 3).reshape(m // P, P, k)


def _stream(*rounds):
    return np.ascontiguousarray(np.concatenate([np.concatenate(r, axis=1) for r in rounds], axis=0))


def _cols(v):
    return v.reshape(-1, P).T


def _rank_tiles(w):
    t = _tiles(np.concatenate([w, np.zeros((D, P - w.shape[1]), np.float32)], axis=1))[0]
    return [t[:, 0:512], t[:, 512:1024]]


def _by_row_tiles(w1, w2):
    w = np.stack([w1.reshape(P, 8, P), w2.reshape(P, 8, P)], axis=2).reshape(P, 2, 1024)
    return [w[:, 0], w[:, 1]]


def _streams(a):
    w = _tiles(a["ev_w_in"][0])
    va, vg, ga, xb, gb = (w[8 * k:8 * k + 8] for k in range(5))
    gates = [np.concatenate([a[n][0, d, h] for d in range(2) for n in ("ev_w_r", "ev_w_i")], axis=1) for h in range(8)]
    s = {"w_even_in": _stream(*[[t for h in (2 * i, 2 * i + 1) for t in (xb[h], va[h], vg[h], gates[h], gb[h], ga[h])]
                                for i in range(4)])}
    wa, wb = _tiles(a["ev_w_out"][0][0:D]), _tiles(a["ev_w_out"][0][D:2 * D])
    s["w_even_out"] = _stream(*[[wb[2 * i], wb[2 * i + 1], wa[2 * i], wa[2 * i + 1]] for i in range(4)])
    w = _tiles(a["od_w_in"][0])
    grp = [_tiles(a["od_w_grp"][0, g]) for g in range(4)]
    for part in range(2):
        s["w_odd_in_" + "ab"[part]] = _stream(*[
            [w[4 * g + j] for j in range(4)] + [t for j in range(4) for t in (w[16 + 4 * g + j], grp[g][j])]
            for g in (2 * part, 2 * part + 1)])
        wo = _tiles(a["od_w_out"][0][part * D:(part + 1) * D])
        s["w_odd_out_" + "ab"[part]] = _stream(*[[wo[2 * i], wo[2 * i + 1]] for i in range(4)])
    w = a["gla_w_in_2"][0]
    s["w_gla_rank"] = _stream(_rank_tiles(w[:, 3072:3088]))
    w = _tiles(w[:, 0:3072])
    s["w_gla_in"] = _stream(*[[w[i], w[4 + i], *_by_row_tiles(w[8 + 2 * i], w[9 + 2 * i]), w[16 + 2 * i], w[17 + 2 * i]]
                               for i in range(4)])
    w = a["fox_w_in_2"][0]
    s["w_fox_gate"] = _stream(_rank_tiles(w[:, 4096:4112]))
    w = _tiles(w[:, 0:4096])
    s["w_fox_in"] = _stream(*[[w[i], w[8 + i], w[16 + i], w[24 + i]] for i in range(8)])
    for n, src in (("w_gla_out", "gla_w_out_2"), ("w_fox_out", "fox_w_out_2")):
        w = _tiles(a[src][0])
        s[n] = _stream(*[[w[2 * i], w[2 * i + 1]] for i in range(4)])
    for r in range(2):
        wp, wg = _tiles(a["ple_proj_2"][r]), _tiles(a["ple_gate_2"][r])
        s[f"w_ple_{r}"] = _stream(*[[wp[m], wg[m][:, 0:384], wg[m][:, 384:]] for m in range(8)])
    w = a["mod_w"].reshape(2, KT, P, 6, HALF)
    s["w_mod"] = np.ascontiguousarray(w.transpose(0, 3, 2, 1, 4)).reshape(12 * P, KT * HALF)
    return s


def _vectors(a):
    f = np.float32
    t = np.arange(ROW)
    v = {
        "c": np.stack([_cols(a["c"][0]), _cols(a["c_ctx"])], axis=2).reshape(P, 16),
        "mod_b": _cols(a["mod_b"]), "norm_g": _cols(a["norm_g"]), "conv_w": _cols(a["ev_conv_w"][0]),
        "conv_b": _cols(a["ev_conv_b"]), "ln_g": _cols(a["ev_ln_g"]), "ln_b": _cols(a["ev_ln_b"]),
        "sconv_w": _cols(a["ev_sconv_w"][0]), "sconv_b": _cols(a["ev_sconv_b"]), "b_r": _cols(a["ev_b_r"][0]),
        "b_i": _cols(a["ev_b_i"][0]), "lam": _cols(a["ev_lam"][0]), "od_scale": _cols(a["od_scale"]),
        "final_g": _cols(a["final_g"]), "norm_mixer": _cols(a["norm_mixer_2"]), "b_a": _cols(a["gla_b_a_2"]),
        "o_norm": _cols(a["gla_o_norm_2"]), "q_norm": np.tile(a["fox_q_norm_2"], (1, 2)).T,
        "k_norm": np.tile(a["fox_k_norm_2"], (1, 2)).T,
        "b_f": np.concatenate([a["fox_b_f_2"][0], np.zeros(P - 16, f)])[:, None],
        "ple_norm": _cols(a["ple_norm_2"]), "final_norm": _cols(a["final_norm_2"]),
        "rcount": np.tile(np.concatenate([1.0 / (np.minimum(t + h, ROW) - np.maximum(t - h, 0))
                                          for h in (1, 2, 4, 8)]).astype(f), (P, 1)),
        "ident": np.eye(P, dtype=f), "ones": np.ones((P, P), f),
        "heads": np.kron(np.eye(2, dtype=f), np.ones((FH, FH), f)),
    }
    for name, (_, n) in VEC.items():
        assert v[name].shape == (P, n), (name, v[name].shape, n)
    return np.ascontiguousarray(np.concatenate([v[name] for name in VEC], axis=1))


def kernel(**inputs):
    import concourse.bacc as bacc
    from concourse.bass_utils import run_bass_kernel_spmd

    a = {k: np.asarray(v) for k, v in inputs.items()}
    arrays = _streams(a)
    arrays["vec"] = _vectors(a)
    arrays["xT"] = np.ascontiguousarray(a["x"][0].T)
    arrays["ctxT"] = np.ascontiguousarray(a["ctx"][0].T)
    arrays["pT"] = np.ascontiguousarray(a["p_2"][:, 0].transpose(0, 2, 1).reshape(512, T))
    arrays["a2"] = np.ascontiguousarray(a["gla_w_a2_2"][0].reshape(16, 4, P).transpose(1, 0, 2).reshape(64, P))
    nc = bacc.Bacc("TRN2", target_bir_lowering=False, num_devices=1)
    dram = {n: nc.dram_tensor(n, v.shape, F32, kind="ExternalInput").ap() for n, v in arrays.items()}
    out = nc.dram_tensor("out", (D, T), F32, kind="ExternalOutput").ap()
    build(nc, dram, out)
    r = run_bass_kernel_spmd(nc, [arrays], core_ids=[0])
    return np.ascontiguousarray(r.results[0]["out"].T).reshape(1, T, D)
```
